# Optimizing a Trainium2 kernel written in Bass

```python
import jax
import jax.numpy as jnp
from jax import lax
import numpy as np
import math
import jax, jax.numpy as jnp

D_MODEL = 1024
BATCH = 1
SEQ = 512
DEPTH = 2

GRID_W = 64
CTX_LEN = 256
EPS = 1e-6

CONV_DIM = 512
CONV_WIDTH = 31
MLSTM_HEADS = 4
MLSTM_QK = 64
MLSTM_V = 128
MLSTM_CHUNK = 64
AB_SIZES = (CONV_DIM, CONV_DIM, MLSTM_HEADS * MLSTM_QK, MLSTM_HEADS * MLSTM_QK,
            MLSTM_HEADS * MLSTM_V, MLSTM_HEADS * MLSTM_V, 4 * MLSTM_HEADS)
AB_IN = sum(AB_SIZES)
AB_OUT = CONV_DIM + MLSTM_HEADS * MLSTM_V

MLA_HEADS = 16
MLA_Q_LORA = 512
MLA_KV_LORA = 256
MLA_NOPE = 64
MLA_ROPE = 32
MLA_V = 64
MLA_QK = MLA_NOPE + MLA_ROPE
MLA_IN = MLA_Q_LORA + MLA_KV_LORA + MLA_ROPE
ROPE_BASE = 10000.0
ATTN_BLOCK = 128

FFN_DIM = 2816
FFN_CONV_WIDTH = 3


def _split_cols(a, sizes):
    return jnp.split(a, np.cumsum(sizes)[:-1].tolist(), axis=-1)

def _rms(x):
    xf = x.astype(jnp.float32)
    return (xf * lax.rsqrt(jnp.mean(xf * xf, axis=-1, keepdims=True) + EPS)).astype(x.dtype)

def _layer_norm(x, g, b):
    xf = x.astype(jnp.float32)
    mu = jnp.mean(xf, axis=-1, keepdims=True)
    var = jnp.mean(jnp.square(xf - mu), axis=-1, keepdims=True)
    return ((xf - mu) * lax.rsqrt(var + EPS)).astype(x.dtype) * g + b

def _modulate(x, shift, scale):
    return _rms(x) * (1 + scale) + shift

def _dwconv(x, w, b):
    k, ch = w.shape
    pad = (k - 1) // 2
    y = lax.conv_general_dilated(x, w[:, None, :].astype(x.dtype), (1,), [(pad, k - 1 - pad)],
                                 dimension_numbers=('NWC', 'WIO', 'NWC'), feature_group_count=ch)
    return y + b

def _zero_state(batch):
    return (jnp.zeros((batch, MLSTM_HEADS, MLSTM_V, MLSTM_QK), jnp.float32),
            jnp.zeros((batch, MLSTM_HEADS, MLSTM_QK), jnp.float32),
            jnp.zeros((batch, MLSTM_HEADS), jnp.float32))

def _mlstm_chunkwise(q, k, v, log_i, log_f, state):
    bsz, nh, t, _ = q.shape
    nc = t // MLSTM_CHUNK

    def chunks(a):
        return jnp.moveaxis(a.reshape(bsz, nh, nc, MLSTM_CHUNK, *a.shape[3:]), 2, 0)

    lower = jnp.tril(jnp.ones((MLSTM_CHUNK, MLSTM_CHUNK), bool))

    def step(carry, inp):
        c_mat, n_vec, m = carry
        qj, kj, vj, li, lf = inp
        b = jnp.cumsum(lf, axis=-1)
        log_d = jnp.where(lower, b[..., :, None] - b[..., None, :] + li[..., None, :], -jnp.inf)
        log_inter = b + m[..., None]
        m_row = jnp.maximum(log_inter, jnp.max(log_d, axis=-1))
        s = jnp.einsum('bhid,bhjd->bhij', qj, kj) * jnp.exp(log_d - m_row[..., None])
        inter = jnp.exp(log_inter - m_row)
        num = jnp.einsum('bhij,bhjv->bhiv', s, vj) + inter[..., None] * jnp.einsum('bhvd,bhid->bhiv', c_mat, qj)
        den = jnp.sum(s, axis=-1) + inter * jnp.einsum('bhd,bhid->bhi', n_vec, qj)
        h = num / jnp.maximum(jnp.abs(den), jnp.exp(-m_row))[..., None]
        b_last = b[..., -1]
        log_w = b_last[..., None] - b + li
        m_new = jnp.maximum(b_last + m, jnp.max(log_w, axis=-1))
        w = jnp.exp(log_w - m_new[..., None])
        decay = jnp.exp(b_last + m - m_new)
        c_new = decay[..., None, None] * c_mat + jnp.einsum('bhj,bhjv,bhjd->bhvd', w, vj, kj)
        n_new = decay[..., None] * n_vec + jnp.einsum('bhj,bhjd->bhd', w, kj)
        return (c_new, n_new, m_new), h

    state, h = lax.scan(step, state, (chunks(q), chunks(k), chunks(v), chunks(log_i), chunks(log_f)))
    return jnp.moveaxis(h, 0, 2).reshape(bsz, nh, t, -1), state

def _flip(t):
    return jnp.flip(t, axis=2)

def _ab_project(h, w_in, gate_bias):
    a, g, q, k, v, o, gates = _split_cols(h @ w_in, AB_SIZES)

    def heads(t, d):
        return t.reshape(*t.shape[:2], -1, d).transpose(0, 2, 1, 3).astype(jnp.float32)

    q = heads(q, MLSTM_QK)
    k = heads(k, MLSTM_QK) * (MLSTM_QK ** -0.5)
    v = heads(v, MLSTM_V)
    gates = (gates + gate_bias).astype(jnp.float32).transpose(0, 2, 1)
    ig_f, fg_f, ig_b, fg_b = jnp.split(gates, 4, axis=1)
    fwd = (ig_f, jax.nn.log_sigmoid(fg_f))
    bwd = (ig_b, jax.nn.log_sigmoid(fg_b))
    return a, g, q, k, v, o, fwd, bwd

def _conformer_mlstm_mixer(h_lat, h_ctx, w_in, gate_bias, conv_w, conv_b, ln_g, ln_b,
                           head_gain, w_out, with_ctx_out):
    lat = _ab_project(h_lat, w_in, gate_bias)
    ctx = _ab_project(h_ctx, w_in, gate_bias)
    zero = _zero_state(h_lat.shape[0])

    def scans(p, init_f, init_b):
        _, _, q, k, v, _, fwd, bwd = p
        h_f, st_f = _mlstm_chunkwise(q, k, v, fwd[0], fwd[1], init_f)
        h_b, st_b = _mlstm_chunkwise(_flip(q), _flip(k), _flip(v), _flip(bwd[0]), _flip(bwd[1]), init_b)
        return h_f + _flip(h_b), st_f, st_b

    h_ctx_seq, st_f, st_b = scans(ctx, zero, zero)
    h_lat_seq, _, _ = scans(lat, st_f, st_b)

    def merge(p, h_seq):
        a, g, _, _, _, o, _, _ = p
        u = _dwconv(a * jax.nn.sigmoid(g), conv_w, conv_b)
        u = jax.nn.silu(_layer_norm(u, ln_g, ln_b))
        hm = _rms(h_seq).transpose(0, 2, 1, 3)
        hm = hm.reshape(*hm.shape[:2], -1).astype(o.dtype) * head_gain * jax.nn.sigmoid(o)
        return jnp.concatenate([u, hm], axis=-1) @ w_out

    y_lat = merge(lat, h_lat_seq)
    y_ctx = merge(ctx, h_ctx_seq) if with_ctx_out else None
    return y_lat, y_ctx

def _axial_rope_tables(rows):
    row = jnp.repeat(jnp.arange(rows, dtype=jnp.float32), GRID_W)
    col = jnp.tile(jnp.arange(GRID_W, dtype=jnp.float32), rows)
    half = MLA_ROPE // 2
    inv_freq = ROPE_BASE ** (-jnp.arange(0, half, 2, dtype=jnp.float32) / half)
    ang = jnp.concatenate([row[:, None] * inv_freq, col[:, None] * inv_freq], axis=-1)
    return jnp.cos(ang), jnp.sin(ang)

def _rope_tail(t, cos, sin):
    nope, r = t[..., :MLA_NOPE], t[..., MLA_NOPE:]
    r = r.reshape(*r.shape[:-1], -1, 2)
    c = cos[None, :, None, :].astype(t.dtype)
    s = sin[None, :, None, :].astype(t.dtype)
    r1, r2 = r[..., 0], r[..., 1]
    rot = jnp.stack([r1 * c - r2 * s, r1 * s + r2 * c], axis=-1).reshape(*nope.shape[:-1], MLA_ROPE)
    return jnp.concatenate([nope, rot], axis=-1)

def _block_attention(q, k, v):
    bsz, tq, nh, dk = q.shape
    nb = tq // ATTN_BLOCK
    qb = jnp.moveaxis(q.reshape(bsz, nb, ATTN_BLOCK, nh, dk), 1, 0)
    scale = dk ** -0.5

    def one_block(qi):
        s = jnp.einsum('bqhd,bkhd->bhqk', qi, k).astype(jnp.float32) * scale
        p = jax.nn.softmax(s, axis=-1).astype(v.dtype)
        return jnp.einsum('bhqk,bkhd->bqhd', p, v)

    out = lax.map(one_block, qb)
    return jnp.moveaxis(out, 0, 1).reshape(bsz, tq, nh * v.shape[-1])

def _mla_mixer(h_lat, h_ctx, cos, sin, w_in, q_norm, kv_norm, w_uq, w_ukv, q_gain, k_gain,
               w_out, with_ctx_out):
    def queries(cq, rotate):
        q = (_rms(cq) * q_norm) @ w_uq
        q = _rms(q.reshape(*q.shape[:2], MLA_HEADS, MLA_QK)) * q_gain
        return _rope_tail(q, cos, sin) if rotate else q

    def keys_values(ckv, k_rope, rotate):
        ukv = ((_rms(ckv) * kv_norm) @ w_ukv).reshape(*ckv.shape[:2], MLA_HEADS, MLA_NOPE + MLA_V)
        k_nope, v = ukv[..., :MLA_NOPE], ukv[..., MLA_NOPE:]
        k_rope = jnp.broadcast_to(k_rope[:, :, None, :], (*k_nope.shape[:3], MLA_ROPE))
        k = _rms(jnp.concatenate([k_nope, k_rope], axis=-1)) * k_gain
        return (_rope_tail(k, cos, sin) if rotate else k), v

    cq_l, ckv_l, kr_l = _split_cols(h_lat @ w_in, (MLA_Q_LORA, MLA_KV_LORA, MLA_ROPE))
    ckv_c, kr_c = _split_cols(h_ctx @ w_in[:, MLA_Q_LORA:], (MLA_KV_LORA, MLA_ROPE))
    k_l, v_l = keys_values(ckv_l, kr_l, True)
    k_c, v_c = keys_values(ckv_c, kr_c, False)
    k_all = jnp.concatenate([k_c, k_l], axis=1)
    v_all = jnp.concatenate([v_c, v_l], axis=1)
    y_lat = _block_attention(queries(cq_l, True), k_all, v_all) @ w_out
    y_ctx = None
    if with_ctx_out:
        q_c = queries(h_ctx @ w_in[:, :MLA_Q_LORA], False)
        y_ctx = _block_attention(q_c, k_c, v_c) @ w_out
    return y_lat, y_ctx

def _conv_ffn(h, w_in, conv_w, conv_b, w_out):
    g, val = jnp.split(h @ w_in, 2, axis=-1)
    return (jax.nn.gelu(_dwconv(g, conv_w, conv_b), approximate=True) * val) @ w_out

def first_inputs(seed: int = 0) -> dict:
    key = jax.random.key(seed)
    ks = iter(jax.random.split(key, 32))
    n_even = (DEPTH + 1) // 2
    n_odd = DEPTH // 2
    f32 = jnp.float32

    def nrm(shape, scale):
        return jax.random.normal(next(ks), shape, f32) * scale

    def gain(shape):
        return 1.0 + nrm(shape, 0.1)

    inp = {}
    inp['x'] = nrm((BATCH, SEQ, D_MODEL), 1.0)
    inp['c'] = nrm((BATCH, D_MODEL), 1.0)
    inp['ctx'] = nrm((BATCH, CTX_LEN, D_MODEL), 1.0)
    inp['c_ctx'] = nrm((D_MODEL,), 1.0)
    inp['ada_w'] = nrm((DEPTH, D_MODEL, 6 * D_MODEL), 0.5 * D_MODEL ** -0.5)
    inp['ada_b'] = nrm((DEPTH, 6 * D_MODEL), 0.02)
    inp['ab_w_in'] = nrm((n_even, D_MODEL, AB_IN), D_MODEL ** -0.5)
    ig = nrm((n_even, 2, 1, MLSTM_HEADS), 0.1)
    fg = jnp.linspace(3.0, 6.0, MLSTM_HEADS, dtype=f32) + nrm((n_even, 2, 1, MLSTM_HEADS), 0.1)
    inp['ab_gate_bias'] = jnp.concatenate([ig, fg], axis=2).reshape(n_even, 4 * MLSTM_HEADS)
    inp['ab_conv_w'] = nrm((n_even, CONV_WIDTH, CONV_DIM), CONV_WIDTH ** -0.5)
    inp['ab_conv_b'] = nrm((n_even, CONV_DIM), 0.02)
    inp['ab_ln_g'] = gain((n_even, CONV_DIM))
    inp['ab_ln_b'] = nrm((n_even, CONV_DIM), 0.02)
    inp['ab_head_gain'] = gain((n_even, MLSTM_HEADS * MLSTM_V))
    inp['ab_w_out'] = nrm((n_even, AB_OUT, D_MODEL), AB_OUT ** -0.5)
    inp['mla_w_in'] = nrm((n_odd, D_MODEL, MLA_IN), D_MODEL ** -0.5)
    inp['mla_q_norm'] = gain((n_odd, MLA_Q_LORA))
    inp['mla_kv_norm'] = gain((n_odd, MLA_KV_LORA))
    inp['mla_w_uq'] = nrm((n_odd, MLA_Q_LORA, MLA_HEADS * MLA_QK), MLA_Q_LORA ** -0.5)
    inp['mla_w_ukv'] = nrm((n_odd, MLA_KV_LORA, MLA_HEADS * (MLA_NOPE + MLA_V)), MLA_KV_LORA ** -0.5)
    inp['mla_q_gain'] = gain((n_odd, MLA_QK))
    inp['mla_k_gain'] = gain((n_odd, MLA_QK))
    inp['mla_w_out'] = nrm((n_odd, MLA_HEADS * MLA_V, D_MODEL), (MLA_HEADS * MLA_V) ** -0.5)
    inp['ffn_w_in'] = nrm((DEPTH, D_MODEL, 2 * FFN_DIM), D_MODEL ** -0.5)
    inp['ffn_conv_w'] = nrm((DEPTH, FFN_CONV_WIDTH, FFN_DIM), FFN_CONV_WIDTH ** -0.5)
    inp['ffn_conv_b'] = nrm((DEPTH, FFN_DIM), 0.02)
    inp['ffn_w_out'] = nrm((DEPTH, FFN_DIM, D_MODEL), FFN_DIM ** -0.5)
    return inp

def first_block(x, c, ctx, c_ctx, ada_w, ada_b, ab_w_in, ab_gate_bias, ab_conv_w, ab_conv_b,
              ab_ln_g, ab_ln_b, ab_head_gain, ab_w_out, mla_w_in, mla_q_norm, mla_kv_norm,
              mla_w_uq, mla_w_ukv, mla_q_gain, mla_k_gain, mla_w_out, ffn_w_in, ffn_conv_w,
              ffn_conv_b, ffn_w_out):
    rows = x.shape[1] // GRID_W
    cos, sin = _axial_rope_tables(rows)
    xl, xc = x, ctx
    for layer in range(DEPTH):
        last = layer == DEPTH - 1
        j = layer // 2
        mod_l = jnp.split((jax.nn.silu(c) @ ada_w[layer] + ada_b[layer])[:, None, :], 6, axis=-1)
        mod_c = jnp.split(jax.nn.silu(c_ctx) @ ada_w[layer] + ada_b[layer], 6, axis=-1)
        h_lat = _modulate(xl, mod_l[0], mod_l[1])
        h_ctx = _modulate(xc, mod_c[0], mod_c[1])
        if layer % 2 == 0:
            y_lat, y_ctx = _conformer_mlstm_mixer(
                h_lat, h_ctx, ab_w_in[j], ab_gate_bias[j], ab_conv_w[j], ab_conv_b[j],
                ab_ln_g[j], ab_ln_b[j], ab_head_gain[j], ab_w_out[j], not last)
        else:
            y_lat, y_ctx = _mla_mixer(
                h_lat, h_ctx, cos, sin, mla_w_in[j], mla_q_norm[j], mla_kv_norm[j], mla_w_uq[j],
                mla_w_ukv[j], mla_q_gain[j], mla_k_gain[j], mla_w_out[j], not last)
        xl = xl + mod_l[2] * y_lat
        xl = xl + mod_l[5] * _conv_ffn(_modulate(xl, mod_l[3], mod_l[4]), ffn_w_in[layer],
                                       ffn_conv_w[layer], ffn_conv_b[layer], ffn_w_out[layer])
        if not last:
            xc = xc + mod_c[2] * y_ctx
            xc = xc + mod_c[5] * _conv_ffn(_modulate(xc, mod_c[3], mod_c[4]), ffn_w_in[layer],
                                           ffn_conv_w[layer], ffn_conv_b[layer], ffn_w_out[layer])
    return xl


DA_HEADS = 4
DA_HEAD_DIM = 64
DA_V_DIM = 2 * DA_HEAD_DIM
DA_QK = 2 * DA_HEADS * DA_HEAD_DIM
DA_WIDTH = DA_HEADS * DA_V_DIM
DIL_GROUPS = ((128, 1), (512, 4), (2048, 16))
DB_HEADS = 8
DB_HEAD_DIM = 64
DB_WIDTH = DB_HEADS * DB_HEAD_DIM
N_BRANCH = 2
FFN_HIDDEN = -(-8 * D_MODEL // (3 * 256)) * 256
ROPE_THETA = 10000.0
Q_BLOCK = 128
NORM_EPS = 1e-6
SUBLN_EPS = 1e-5
NEG_INF = -1e30
IN_SIZES = [DA_QK, DA_QK, DA_WIDTH] + [DB_WIDTH] * (3 * len(DIL_GROUPS)) + [N_BRANCH * D_MODEL]
IN_COLS = sum(IN_SIZES)


def rms_norm(x, g, eps):
    xf = x.astype(jnp.float32)
    y = xf * lax.rsqrt(jnp.mean(xf * xf, axis=-1, keepdims=True) + eps)
    return (y * g.astype(jnp.float32)).astype(x.dtype)

def rope_tables(seq, dim):
    inv = 1.0 / (ROPE_THETA ** (jnp.arange(0, dim, 2, dtype=jnp.float32) / dim))
    ang = jnp.arange(seq, dtype=jnp.float32)[:, None] * inv[None, :]
    return jnp.cos(ang), jnp.sin(ang)

def apply_rope(t, cos, sin):
    half = t.shape[-1] // 2
    tf = t.astype(jnp.float32)
    t1, t2 = tf[..., :half], tf[..., half:]
    c, s = cos[None, :, None, :], sin[None, :, None, :]
    return jnp.concatenate([t1 * c - t2 * s, t2 * c + t1 * s], axis=-1).astype(t.dtype)

def differential_attention(q, k, v, lam_full, subln_g, lambda_init):
    B, S, H2, Dh = q.shape
    H = H2 // 2
    scale = Dh ** -0.5
    qb = q.reshape(B, S // Q_BLOCK, Q_BLOCK, H, 2, Dh).transpose(1, 0, 2, 3, 4, 5)
    kk = k.reshape(B, S, H, 2, Dh)

    def block(qblk):
        s = jnp.einsum('bqhcd,bkhcd->bhcqk', qblk, kk, preferred_element_type=jnp.float32) * scale
        p = jax.nn.softmax(s, axis=-1)
        a = p[:, :, 0] - lam_full * p[:, :, 1]
        return jnp.einsum('bhqk,bkhe->bqhe', a.astype(v.dtype), v)

    o = lax.map(block, qb)
    o = o.transpose(1, 0, 2, 3, 4).reshape(B, S, H, 2 * Dh)
    o = rms_norm(o, subln_g, SUBLN_EPS) * (1.0 - lambda_init)
    return o.reshape(B, S, H * 2 * Dh)

def dilated_window_attention(q, k, v, dilation, n_side):
    B, S, H, Dh = q.shape
    blk = n_side
    L = -(-S // (dilation * blk)) * blk
    pad = L * dilation - S
    nb = L // blk

    def split(t):
        t = jnp.pad(t, ((0, 0), (0, pad), (0, 0), (0, 0)))
        t = t.reshape(B, L, dilation, H, Dh).transpose(0, 2, 1, 3, 4)
        return t.reshape(B, dilation, nb, blk, H, Dh)

    def neighbours(t):
        tp = jnp.pad(t, ((0, 0), (0, 0), (1, 1), (0, 0), (0, 0), (0, 0)))
        return jnp.concatenate([tp[:, :, :-2], tp[:, :, 1:-1], tp[:, :, 2:]], axis=3)

    qb = split(q)
    kn = neighbours(split(k))
    vn = neighbours(split(v))
    r = jnp.arange(dilation)[:, None, None, None]
    n = jnp.arange(nb)[None, :, None, None]
    i = jnp.arange(blk)[None, None, :, None]
    j = jnp.arange(3 * blk)[None, None, None, :]
    tq = n * blk + i
    tk = n * blk + j - blk
    mask = (jnp.abs(tk - tq) <= n_side) & (tk >= 0) & (tk * dilation + r < S)
    s = jnp.einsum('brnqhd,brnkhd->brnhqk', qb, kn, preferred_element_type=jnp.float32) * (Dh ** -0.5)
    s = jnp.where(mask[None, :, :, None, :, :], s, NEG_INF)
    m = jnp.max(s, axis=-1, keepdims=True)
    e = jnp.exp(s - m)
    den = jnp.sum(e, axis=-1)
    o = jnp.einsum('brnhqk,brnkhd->brnqhd', e.astype(vn.dtype), vn, preferred_element_type=jnp.float32)
    o = o / jnp.swapaxes(den, -1, -2)[..., None]
    lse = jnp.swapaxes(m[..., 0] + jnp.log(den), -1, -2)

    def merge(t):
        rest = t.shape[4:]
        t = t.reshape((B, dilation, L) + rest)
        t = jnp.moveaxis(t, 1, 2).reshape((B, L * dilation) + rest)
        return t[:, :S]

    return merge(o), merge(lse)

def hybrid_mixer(h, w_in, w_a, w_b, w_out, lam, subln_g, cos, sin, lambda_init):
    B, S, _ = h.shape
    z = h @ w_in
    idx = np.cumsum(IN_SIZES)[:-1].tolist()
    parts = jnp.split(z, idx, axis=-1)
    qa = apply_rope(parts[0].reshape(B, S, 2 * DA_HEADS, DA_HEAD_DIM), cos, sin)
    ka = apply_rope(parts[1].reshape(B, S, 2 * DA_HEADS, DA_HEAD_DIM), cos, sin)
    va = parts[2].reshape(B, S, DA_HEADS, DA_V_DIM)
    lamf = lam.astype(jnp.float32)
    lam_full = (jnp.exp(jnp.sum(lamf[0] * lamf[1])) - jnp.exp(jnp.sum(lamf[2] * lamf[3]))
                + lambda_init)
    oa = differential_attention(qa, ka, va, lam_full, subln_g, lambda_init)
    outs, lses = [], []
    for g, (window, dilation) in enumerate(DIL_GROUPS):
        base = 3 + 3 * g
        qg = apply_rope(parts[base].reshape(B, S, DB_HEADS, DB_HEAD_DIM), cos, sin)
        kg = apply_rope(parts[base + 1].reshape(B, S, DB_HEADS, DB_HEAD_DIM), cos, sin)
        vg = parts[base + 2].reshape(B, S, DB_HEADS, DB_HEAD_DIM)
        og, lg = dilated_window_attention(qg, kg, vg, dilation, (window // 2) // dilation)
        outs.append(og)
        lses.append(lg)
    wts = jax.nn.softmax(jnp.stack(lses), axis=0)
    ob = jnp.einsum('gbsh,gbshd->bshd', wts, jnp.stack(outs)).astype(h.dtype).reshape(B, S, DB_WIDTH)
    gates = jax.nn.sigmoid(parts[-1].astype(jnp.float32)).reshape(B, S, N_BRANCH, D_MODEL)
    merged = gates[:, :, 0] * (oa @ w_a).astype(jnp.float32) + gates[:, :, 1] * (ob @ w_b).astype(jnp.float32)
    return merged.astype(h.dtype) @ w_out

def swiglu(h, w_gate_up, w_down):
    gu = h @ w_gate_up
    g, u = jnp.split(gu, 2, axis=-1)
    return (jax.nn.silu(g) * u) @ w_down

def second_inputs(seed: int = 0) -> dict:
    key = jax.random.key(seed)
    ks = jax.random.split(key, 14)
    f32 = jnp.float32

    def nrm(k, shape, scale):
        return jax.random.normal(k, shape, f32) * scale

    def gain(k, shape):
        return 1.0 + 0.05 * jax.random.normal(k, shape, f32)

    return {
        "x": jax.random.normal(ks[0], (BATCH, SEQ, D_MODEL), f32),
        "w_in": nrm(ks[1], (DEPTH, D_MODEL, IN_COLS), D_MODEL ** -0.5),
        "w_a": nrm(ks[2], (DEPTH, DA_WIDTH, D_MODEL), DA_WIDTH ** -0.5),
        "w_b": nrm(ks[3], (DEPTH, DB_WIDTH, D_MODEL), DB_WIDTH ** -0.5),
        "w_out": nrm(ks[4], (DEPTH, D_MODEL, D_MODEL), D_MODEL ** -0.5),
        "lam": nrm(ks[5], (DEPTH, 4, DA_HEAD_DIM), 0.1),
        "subln_g": gain(ks[6], (DEPTH, DA_V_DIM)),
        "norm_mix_pre": gain(ks[7], (DEPTH, D_MODEL)),
        "norm_mix_post": gain(ks[8], (DEPTH, D_MODEL)),
        "w_gate_up": nrm(ks[9], (DEPTH, D_MODEL, 2 * FFN_HIDDEN), D_MODEL ** -0.5),
        "w_down": nrm(ks[10], (DEPTH, FFN_HIDDEN, D_MODEL), FFN_HIDDEN ** -0.5),
        "norm_ffn_pre": gain(ks[11], (DEPTH, D_MODEL)),
        "norm_ffn_post": gain(ks[12], (DEPTH, D_MODEL)),
    }

def second_block(x, w_in, w_a, w_b, w_out, lam, subln_g, norm_mix_pre, norm_mix_post,
              w_gate_up, w_down, norm_ffn_pre, norm_ffn_post):
    S = x.shape[1]
    cos, sin = rope_tables(S, DA_HEAD_DIM)
    for l in range(DEPTH):
        lambda_init = 0.8 - 0.6 * math.exp(-0.3 * l)
        h = rms_norm(x, norm_mix_pre[l], NORM_EPS)
        m = hybrid_mixer(h, w_in[l], w_a[l], w_b[l], w_out[l], lam[l], subln_g[l], cos, sin, lambda_init)
        x = x + rms_norm(m, norm_mix_post[l], NORM_EPS)
        h = rms_norm(x, norm_ffn_pre[l], NORM_EPS)
        f = swiglu(h, w_gate_up[l], w_down[l])
        x = x + rms_norm(f, norm_ffn_post[l], NORM_EPS)
    return x


def setup_inputs(seed=0):
    out = dict(first_inputs(seed))
    for name, value in second_inputs(seed + 1).items():
        if name != "x":
            out[name + "_2"] = value
    return out


def reference(
    x, c, ctx, c_ctx, ada_w, ada_b, ab_w_in, ab_gate_bias, ab_conv_w, ab_conv_b, ab_ln_g,
    ab_ln_b, ab_head_gain, ab_w_out, mla_w_in, mla_q_norm, mla_kv_norm, mla_w_uq, mla_w_ukv,
    mla_q_gain, mla_k_gain, mla_w_out, ffn_w_in, ffn_conv_w, ffn_conv_b, ffn_w_out, w_in_2,
    w_a_2, w_b_2, w_out_2, lam_2, subln_g_2, norm_mix_pre_2, norm_mix_post_2, w_gate_up_2,
    w_down_2, norm_ffn_pre_2, norm_ffn_post_2,
):
    x = first_block(
        x, c, ctx, c_ctx, ada_w, ada_b, ab_w_in, ab_gate_bias, ab_conv_w, ab_conv_b, ab_ln_g,
        ab_ln_b, ab_head_gain, ab_w_out, mla_w_in, mla_q_norm, mla_kv_norm, mla_w_uq, mla_w_ukv,
        mla_q_gain, mla_k_gain, mla_w_out, ffn_w_in, ffn_conv_w, ffn_conv_b, ffn_w_out,
    )
    return second_block(
        x, w_in_2, w_a_2, w_b_2, w_out_2, lam_2, subln_g_2, norm_mix_pre_2, norm_mix_post_2,
        w_gate_up_2, w_down_2, norm_ffn_pre_2, norm_ffn_post_2,
    )


_drawn_inputs = setup_inputs


def setup_inputs(seed=0):
    import zlib

    import numpy as np

    out = dict(_drawn_inputs(seed))
    spreads = {}
    factors = {'ab_ln_b': 4.162,
     'mla_q_norm': 8.0,
     'mla_q_gain': 8.0,
     'mla_k_gain': 8.0,
     'ffn_conv_b': 4.343}
    for name, (base, spread) in spreads.items():
        noise = np.random.default_rng([zlib.crc32(name.encode()), seed]).standard_normal(out[name].shape)
        drawn = base * np.exp(spread * noise) if base else spread * noise
        out[name] = jnp.asarray(drawn.astype(out[name].dtype))
    for name, factor in factors.items():
        out[name] = (out[name] * factor).astype(out[name].dtype)
    return out
```

```python
from contextlib import ExitStack

import concourse.bass as bass
import numpy as np
from concourse import mybir

F32 = mybir.dt.float32
F32R = mybir.dt.float32r
ACT = mybir.ActivationFunctionType
ALU = mybir.AluOpType
AX_X = mybir.AxisListType.X

P = 128
D = 1024
KD = D // P
T, C = 512, 256
TC = T + C
SLOTS = 3
EPS = 1e-6
SUBLN_EPS = 1e-5
NEG = -1e30
HEADS_M, QK_M, V_M = 4, 64, 128
TAPS = 31
CT = 4
HEADS_A, NOPE, ROPE = 16, 64, 32
QK_A = NOPE + ROPE
F_TILES = 22
PIECES = ((0, 8), (8, 8), (16, 6))
LAYERS = 2
HEADS_D = 4
GROUPS = (1, 4, 16)
SIDE = 64
KEYS_DIL = T + 2 * P
TB = T // P



class Lin:

    def __init__(self, reg, a, b):
        self.reg, self.a, self.b = reg, a, b

    def __add__(self, n):
        return Lin(self.reg, self.a, self.b + n)

    def __sub__(self, n):
        return Lin(self.reg, self.a, self.b - n)

    def __mul__(self, n):
        return Lin(self.reg, self.a * n, self.b * n)

    def __mod__(self, n):
        assert self.a % n == 0
        return self.b % n

    def __floordiv__(self, n):
        assert self.a % n == 0
        return Lin(self.reg, self.a // n, self.b // n)


def v(i):
    if isinstance(i, Lin):
        return i.reg * i.a + i.b if i.a else i.b
    return i


_at = 0


def _take(n):
    global _at
    g, _at = _at, _at + n
    return g


FFN_CHUNKS = sum(2 * n + KD for _, n in PIECES)
G_GLU = [_take(2 * CT), _take(2 * CT)]
G_QKVO = [_take(12), _take(12)]
G_ABOUT = [_take(KD), _take(KD)]
G_FFN = [_take(FFN_CHUNKS), _take(FFN_CHUNKS)]
G_MLA = [_take(7), _take(3)]
G_HEADS = _take(HEADS_A * 6 // KD)
G_MLAOUT = _take(KD)
G_FFN.append(_take(FFN_CHUNKS))
G_DIFF, G_DIL, G_MERGE, G_OUT = [], [], [], []
for _l in range(LAYERS):
    G_DIFF.append(_take(3 * HEADS_D))
    G_DIL.append(_take(9 * 4))
    G_MERGE.append(_take(3 * KD))
    G_OUT.append(_take(KD))
    G_FFN.append(_take(FFN_CHUNKS))
G_ALL = _at
ADA_M = 6 * KD
ADA_W = 2

_cols = {}
_nc = 0
for _name, _n in (("ada_b", LAYERS * ADA_M), ("conv_w", CT * TAPS), ("conv_b", CT), ("ln_g", CT), ("ln_b", CT),
                  ("head_gain", HEADS_M), ("q_norm", 4), ("kv_norm", 2), ("q_gain", 1), ("k_gain", 1),
                  ("ffn_w", LAYERS * 3 * F_TILES), ("ffn_b", LAYERS * F_TILES), ("gate_bias", 16),
                  ("mix_pre", LAYERS * KD), ("mix_post", LAYERS * KD), ("ffn_pre", LAYERS * KD),
                  ("ffn_post", LAYERS * KD), ("subln", LAYERS)):
    _cols[_name] = _nc
    _nc += _n
N_PCOL = _nc
CM = {n: i * P for i, n in enumerate(("ident", "ones", "upto", "from", "mask_f", "mask_b", "rot2", "rotm"))}
N_CM = len(CM) * P

NORMS = ["mix_lat", "mix_ctx", "ln_lat", "ln_ctx", "ffn_lat", "ffn_ctx", "mla_lat", "mla_ctx", "cq", "ckv_ctx", "ckv_lat", "mla_ffn"]
NORMS += [f"{w}{l}" for l in range(LAYERS) for w in ("mixpre", "mixpost", "ffnpre", "ffnpost")]
_k = {"ln_lat": CT, "ln_ctx": CT, "cq": 4, "ckv_ctx": 2, "ckv_lat": 2}
N_KT = [_k.get(n, KD) for n in NORMS]
N_BASE = [sum(N_KT[:i]) for i in range(len(NORMS))]
N_OUT = [sum(k for k, n in zip(N_KT[:i], NORMS) if "post" not in n) for i in range(len(NORMS))]

ARENA = 13300


def program(nc, stream, ada, xT, cT, cond, wgate, lam, pcol, cmat, trope, brope, bmask, out):
    with ExitStack() as ctx:
        def sb(name, shape, dt=F32):
            return ctx.enter_context(nc.sbuf_tensor(name, shape, dt))

        def sem(name):
            return ctx.enter_context(nc.semaphore(name))

        x = sb("x", [P, KD, T])
        xc = sb("xc", [P, KD, C])
        h_hi, h_lo = sb("h_hi", [P, KD * T], F32R), sb("h_lo", [P, KD * T], F32R)
        b_hi, b_lo = sb("b_hi", [P, KD * T], F32R), sb("b_lo", [P, KD * T], F32R)
        w_raw = sb("w_raw", [P, SLOTS, KD * P])
        w_hi, w_lo = sb("w_hi", [P, SLOTS, KD * P], F32R), sb("w_lo", [P, SLOTS, KD * P], F32R)
        pc = sb("pc", [P, N_PCOL])
        cm = sb("cm", [P, N_CM])
        mod = sb("mod", [P, LAYERS * ADA_M, 2])
        attA, attP, attT = sb("attA", [P, 2, TC]), sb("attP", [P, 2, TC]), sb("attT", [P, 2, TC])
        hsum = sb("hsum", [P, 6, P])
        small = sb("small", [P, 512])
        wg_raw = sb("wg_raw", [P, P])[:, :]
        wg_hi, wg_lo = sb("wg_hi", [P, 128], F32R), sb("wg_lo", [P, 128], F32R)
        cond_sb = sb("cond_sb", [P, 2 * KD])
        lam_junk = sb("lam_junk", [P, 64])
        arena = sb("arena", [P, ARENA])
        bank = [ctx.enter_context(nc.psum_tensor(f"bank{i}", [P, 512], F32)) for i in range(3)]
        pS = ctx.enter_context(nc.psum_tensor("pS", [P, 1024], F32))
        pT = ctx.enter_context(nc.psum_tensor("pT", [P, 1024], F32))
        pO = ctx.enter_context(nc.psum_tensor("pO", [P, 512], F32))

        def view(off, *shape):
            n = int(np.prod(shape))
            assert off + n <= ARENA, (off, shape)
            v = arena[:, off:off + n]
            if len(shape) == 2:
                v = v.rearrange("p (a b) -> p a b", b=shape[1])
            elif len(shape) == 3:
                v = v.rearrange("p (a b c) -> p a b c", b=shape[1], c=shape[2])
            return v

        def flat(t):
            return t[:, :, :].rearrange("p a b -> p (a b)")

        sq = flat(attT)[:, 0:1024].rearrange("p (a b) -> p a b", b=512)
        rt, rstd = flat(attA)[:, 0:512], flat(attA)[:, 512:1024]
        nt = flat(attP)[:, 0:1536].rearrange("p (a b) -> p a b", b=512)

        lam_in = flat(attT)[:, 1024:1024 + LAYERS * 256]

        def col(name, i=0, parts=slice(0, P)):
            return pc[parts, _cols[name] + i:_cols[name] + i + 1]

        def dcol(name, i):
            return pc[:, bass.ds(v(i + _cols[name]), 1)]

        def modd(layer, part, kt, stream_):
            return mod[:, bass.ds(v(kt + (layer * ADA_M + part * KD)), 1), stream_:stream_ + 1].rearrange("p a b -> p (a b)")

        def modc(layer, part, kt, stream_):
            return mod[:, layer * ADA_M + part * KD + kt, stream_:stream_ + 1]

        def dyn(j, n, base=0):
            return bass.ds(v(j * n + base), n)

        ident, ones = cm[:, CM["ident"]:CM["ident"] + P], cm[:, CM["ones"]:CM["ones"] + P]

        def const(name, rows=P, cols=P):
            return cm[0:rows, CM[name]:CM[name] + cols]

        consts_in = sem("consts_in")
        rope_in = sem("rope_in")
        raw_full = [sem(f"raw_full{s}") for s in range(SLOTS)]
        hi_ready = sem("hi_ready")
        lo_ready = sem("lo_ready")
        chunk_done = sem("chunk_done")
        evac = [sem(f"evac{b}") for b in range(SLOTS)]
        ada_in = [sem(f"ada_in{s}") for s in range(4)]
        ada_done = sem("ada_done")
        silu_done = sem("silu_done")
        mod_ready = sem("mod_ready")
        gate_w_hi, gate_w_lo = sem("gate_w_hi"), sem("gate_w_lo")
        sq_ready, sq_used, rt_ready, rstd_ready = sem("sq_ready"), sem("sq_used"), sem("rt_ready"), sem("rstd_ready")
        nt_ready, nhi_ready, nlo_ready = sem("nt_ready"), sem("nhi_ready"), sem("nlo_ready")
        mean_sum, centred = sem("mean_sum"), sem("centred")
        conv_ready, gelu_ready, act_hi, act_lo = sem("conv_ready"), sem("gelu_ready"), sem("act_hi"), sem("act_lo")
        dve_step, act_step, dve_link = sem("dve_step"), sem("act_step"), sem("dve_link")
        gates_sum, gates_in, gates_log, logf_ready = sem("gates_sum"), sem("gates_in"), sem("gates_log"), sem("logf_ready")
        prefix_sum, u_ready = sem("prefix_sum"), sem("u_ready")
        ubc_ready, u_copied, ud_ready, cmax_ready, guard_ready = (sem("ubc_ready"), sem("u_copied"), sem("ud_ready"),
                                                                  sem("cmax_ready"), sem("guard_ready"))
        ms_ready, me_ready, mp_ready, mt_ready, mtc_ready, mpv_ready, mh_ready = (
            sem("ms_ready"), sem("me_ready"), sem("mp_ready"), sem("mt_ready"), sem("mtc_ready"), sem("mpv_ready"), sem("mh_ready"))
        hs_sq, hs_scaled, hs_turned, hs_val, hs_hi, hs_lo = (sem("hs_sq"), sem("hs_scaled"), sem("hs_turned"), sem("hs_val"),
                                                             sem("hs_hi"), sem("hs_lo"))
        padded = sem("padded")
        s_ready, nm_ready, e_ready, pt_ready, ptc_act, ptc_dve, pv_ready, o_ready = (
            sem("s_ready"), sem("nm_ready"), sem("e_ready"), sem("pt_ready"), sem("ptc_act"), sem("ptc_dve"),
            sem("pv_ready"), sem("o_ready"))
        hq_copied, hq_sq, hq_sums, hq_rt, hq_norm, hq_rot, hq_ready = (
            sem("hq_copied"), sem("hq_sq"), sem("hq_sums"), sem("hq_rt"), sem("hq_norm"), sem("hq_rot"), sem("hq_ready"))
        rot_ready, rope_done = sem("rot_ready"), sem("rope_done")
        o_turned, o_val, o_hi, o_lo, o_sq, o_scaled = (sem("o_turned"), sem("o_val"), sem("o_hi"), sem("o_lo"), sem("o_sq"),
                                                       sem("o_scaled"))
        v_copied = sem("v_copied")
        lam_sums, lam_exp, lam_ready = sem("lam_sums"), sem("lam_exp"), sem("lam_ready")
        merged = sem("merged")
        m_hi, m_lo = sem("m_hi"), sem("m_lo")
        perm_a, perm_b = sem("perm_a"), sem("perm_b")
        x_ready = sem("x_ready")
        stored = sem("stored")

        def items(eng, n, unroll, body, start=0):
            loops = n // unroll if n // unroll >= 2 else 0
            if loops:
                with eng.Fori(0, loops) as i:
                    for u in range(unroll):
                        body(Lin(i, unroll, start + u))
            for j in range(start + loops * unroll, start + n):
                body(Lin(None, 0, j))

        def pe_wait_chunk(pe, g):
            pe.wait_ge(lo_ready, v(g + 1))
            pe.wait_ge(evac[g % SLOTS], v(g // SLOTS + 1))

        def pe_three(pe, dst, pairs):
            last = None
            for k, ((lh, ll), (rh, rl)) in enumerate(pairs):
                pe.matmul(dst, lh, rh, start=(k == 0), stop=False)
                pe.matmul(dst, lh, rl, start=False, stop=False)
                last = pe.matmul(dst, ll, rh, start=False, stop=(k == len(pairs) - 1))
            return last

        def wt(s, kt, c0=0, c1=P):
            return w_hi[:, s, kt * P + c0:kt * P + c1], w_lo[:, s, kt * P + c0:kt * P + c1]

        def rows(hi, lo, width, kt, c0, c1, base=0):
            o = base + kt * width
            return hi[:, o + c0:o + c1], lo[:, o + c0:o + c1]

        def pe_chunk(pe, g, src, width, n, kts=KD, k0=0):
            s = g % SLOTS
            pe_wait_chunk(pe, g)
            pe_three(pe, bank[s][:, 0:n], [(wt(s, k0 + kt), rows(*src, width, kt, 0, n)) for kt in range(kts)]
                     ).then_inc(chunk_done, 1)

        def pe_chunk_tokens(pe, g, src, width, n):
            s = g % SLOTS
            pe_wait_chunk(pe, g)
            for t in range(n // P):
                last = pe_three(pe, bank[s][:, t * P:(t + 1) * P],
                                [(rows(*src, width, kt, t * P, (t + 1) * P), wt(s, kt)) for kt in range(KD)])
            last.then_inc(chunk_done, 1)

        def act_hi_part(act, g):
            if not (isinstance(g, Lin) and g.a) and v(g) >= G_ALL:
                return
            s = g % SLOTS
            act.wait_ge(raw_full[s], v((g // SLOTS + 1) * 16))
            act.wait_ge(chunk_done, v(g + 1))
            act.activation(w_hi[:, s, :], w_raw[:, s, :], ACT.Copy).then_inc(hi_ready, 1)

        def done(g):
            return v(g + (1 + SLOTS))

        def ev(g):
            return evac[g % SLOTS], v(g // SLOTS + 2)

        H, B = (h_hi, h_lo), (b_hi, b_lo)

        def act_norm(act, name, src, n, width, src_ready=None, shift=None, dst=None, dst_free=None, eps=EPS):
            c = NORMS.index(name)
            kts, base = N_KT[c], N_BASE[c]
            if src_ready is not None:
                act.wait_ge(*src_ready)
            for kt in range(kts):
                if base + kt >= 2:
                    act.wait_ge(sq_used, base + kt - 1)
                act.activation(sq[:, kt % 2, 0:n], src(kt), ACT.Square).then_inc(sq_ready, 1)
            act.wait_ge(sq_used, base + kts)
            act.activation(rt[:, 0:n], pS[:, 0:n], ACT.Sqrt, bias=eps, scale=1.0 / (kts * P)).then_inc(rt_ready, 1)
            if dst is not None:
                if dst_free is not None:
                    act.wait_ge(chunk_done, dst_free)
                for kt in range(kts):
                    act.wait_ge(nt_ready, base + kt + 1)
                    o = dst[2] + kt * width
                    if shift is None:
                        act.activation(dst[0][:, o:o + n], nt[:, kt % 3, 0:n], ACT.Copy).then_inc(nhi_ready, 1)
                    else:
                        act.activation(dst[0][:, o:o + n], nt[:, kt % 3, 0:n], ACT.Identity, bias=shift(kt)).then_inc(nhi_ready, 1)

        def dve_norm(dve, name, src, n, width, gain, shift=None, dst=None):
            c = NORMS.index(name)
            kts, base = N_KT[c], N_BASE[c]
            dve.wait_ge(rt_ready, c + 1)
            dve.reciprocal(rstd[:, 0:n], rt[:, 0:n]).then_inc(rstd_ready, 1)
            dve.wait_ge(rstd_ready, c + 1)
            for kt in range(kts + 1):
                if kt < kts:
                    if kt >= 3:
                        dve.wait_ge(nlo_ready, N_OUT[c] + kt - 2)
                    dve.scalar_tensor_tensor(nt[:, kt % 3, 0:n], src(kt), gain(kt), rstd[:, 0:n], ALU.mult, ALU.mult
                                             ).then_inc(nt_ready, 1)
                if kt >= 1:
                    k = kt - 1
                    dve.wait_ge(nhi_ready, N_OUT[c] + k + 1)
                    o = dst[2] + k * width
                    hi, lo = dst[0][:, o:o + n], dst[1][:, o:o + n]
                    if shift is None:
                        dve.tensor_tensor(lo, nt[:, k % 3, 0:n], hi.bitcast(F32), ALU.subtract).then_inc(nlo_ready, 1)
                    else:
                        dve.scalar_tensor_tensor(lo, nt[:, k % 3, 0:n], shift(k), hi.bitcast(F32), ALU.add, ALU.subtract
                                                 ).then_inc(nlo_ready, 1)

        def pe_norm(pe, name, n):
            c = NORMS.index(name)
            kts, base = N_KT[c], N_BASE[c]
            if c:
                pe.wait_ge(rt_ready, c)
            for kt in range(kts):
                pe.wait_ge(sq_ready, base + kt + 1)
                pe.matmul(pS[:, 0:n], ones, sq[:, kt % 2, 0:n], start=(kt == 0), stop=(kt == kts - 1)).then_inc(sq_used, 1)

        def norm_done(name):
            c = NORMS.index(name)
            return N_OUT[c] + N_KT[c]

        adaring = view(0, 4, ADA_W * KD * P)
        n_ada = LAYERS * ADA_M // ADA_W

        PADW = (TAPS - 1) // 2
        up = [view(0, CT, T + 2 * PADW), view(2168, CT, C + 2 * PADW)]
        qm, km = view(3312, 2, TC), view(4848, 2, TC)
        vm = view(6384, 6, HEADS_M * (V_M + 1))
        sig_o = view(9480, HEADS_M, TC)
        cacc = view(12552, 1, T)
        sig_g = [nt[:, i, :] for i in range(3)]
        gt, ga = small[:, 128:224], small[:, 224:320]
        bcum, u_ = small[:, 320:368], small[:, 368:416]
        tmax, dmax, pmax, ncm, guard = (small[:, 416:422], small[:, 424:430], small[:, 432:439], small[:, 440:446],
                                        small[:, 448:454])
        den, rden = small[:, 456:457], small[:, 458:459]
        ss, rss = small[:, 460:466], small[:, 468:474]
        SEQ0 = {0: C, 1: 0}
        WIDTH = (T, C)

        def v_at(t, h):
            return vm[:, t, h * (V_M + 1):(h + 1) * (V_M + 1)]


        gpad, cbuf, vbuf = view(8400, 3, T + 2), view(9942, 3, T), view(11478, 3, T)
        f = view(4096, KD, T)
        masks, cos2, sin2 = view(0, TB, KEYS_DIL), view(3072, T), view(3584, T)
        qs = view(4096, 2, T)
        qr, kr = view(5120, 3, T), view(6656, 3, T)
        vt = view(8192, 3, TB, P)
        od = view(9728, TB, P)
        t1 = view(10240, T)
        sg = view(8192, 2, T)
        tm = view(9216, 2, T)
        o_all = view(0, TB, HEADS_A * 64)
        cq, ckv = view(0, 4, T), view(2048, 2, TC)
        qraw, kraw = view(4096, T), view(4608, TC)
        qf, kf = view(5376, 2, T), view(6400, 2, TC)
        va = view(7936, 2, 6, 64)
        hsq = view(8704, T + TC)
        hrt = view(9984, T + TC)
        mt1 = view(11264, T)
        cosm, sinm = view(11776, T), view(12288, T)
        mx, nm, esum, rsum, lam_r = small[:, 0:2], small[:, 2:4], small[:, 4:6], small[:, 6:8], small[:, 8:9]
        oss, orss = small[:, 16:20], small[:, 20:24]
        lam_s, neg_lam = small[:, 24:28], small[:, 28:32]
        CR = 8

        def pe_out(pe, g0, src, width, n, kts=KD):
            items(pe, KD, SLOTS, lambda m: pe_chunk(pe, m + g0, src, width, n, kts))

        def act_out(act, g0):
            items(act, KD, SLOTS, lambda m: act_hi_part(act, m + (g0 + 1)))

        def dve_out_residual(dve, g0, dst, n, layer, part, stream_):
            def body(m):
                dve.wait_ge(chunk_done, done(m + g0))
                xm = dst[:, dyn(m, 1), :].rearrange("p a b -> p (a b)")
                dve.scalar_tensor_tensor(xm, bank[(m + g0) % SLOTS][:, 0:n], modd(layer, part, m, stream_), xm,
                                         ALU.mult, ALU.add).then_inc(evac[(m + g0) % SLOTS], 1)
            items(dve, KD, SLOTS, body)

        def g_piece(call, p):
            return G_FFN[call] + sum(2 * n + KD for _, n in PIECES[:p])

        def pe_ffn(pe, call, norm, n, width):
            pe.wait_ge(nlo_ready, norm_done(norm))
            for p, (j0, nj) in enumerate(PIECES):
                g0 = g_piece(call, p)
                items(pe, 2 * nj, SLOTS, lambda m: pe_chunk(pe, m + g0, H, width, n))
                pe.wait_ge(act_lo, call * F_TILES + j0 + nj + SLOTS)
                pe_out(pe, g0 + 2 * nj, B, T, n, nj)

        def act_ffn(act, call, n, conv):
            for p, (j0, nj) in enumerate(PIECES):
                g0 = g_piece(call, p)
                if p:
                    act.wait_ge(chunk_done, done(g0 - 1))

                def body(j):
                    g = (j - j0) * 2 + g0
                    s = j % SLOTS
                    act_hi_part(act, g + 1)
                    act.wait_ge(chunk_done, done(g))
                    if conv:
                        act.wait_ge(conv_ready, v(j + (call * F_TILES + 1)))
                        act.activation(gpad[:, s, 1:1 + n], bank[g % SLOTS][:, 0:n], ACT.Copy).then_inc(evac[g % SLOTS], 1)
                        act_hi_part(act, g + 2)
                        act.wait_ge(conv_ready, v(j + (call * F_TILES + 1 + SLOTS)))
                        act.activation(cbuf[:, s, 0:n], cbuf[:, s, 0:n], ACT.Gelu_apprx_tanh).then_inc(gelu_ready, 1)
                    else:
                        act.wait_ge(act_lo, v(j + (call * F_TILES + 1)))
                        act.activation(cbuf[:, s, 0:n], bank[g % SLOTS][:, 0:n], ACT.Silu).then_inc(evac[g % SLOTS], 1)
                        act_hi_part(act, g + 2)
                    act.wait_ge(*ev(g + 1))
                    o = dyn(j - j0, T) if n == T else bass.ds(v((j - j0) * T), n)
                    act.activation(b_hi[:, o], vbuf[:, s, 0:n], ACT.Copy).then_inc(act_hi, 1)

                items(act, nj, SLOTS, body, j0)
                act_out(act, g0 + 2 * nj)

        def dve_ffn(dve, call, n, conv, layer, out_body):
            for p, (j0, nj) in enumerate(PIECES):
                g0 = g_piece(call, p)
                if p:
                    dve.wait_ge(chunk_done, done(g0 - 1))

                def body(j):
                    g = (j - j0) * 2 + g0
                    s = j % SLOTS
                    J = j + call * F_TILES
                    if conv:
                        w = [dcol("ffn_w", j + (layer * 3 + i) * F_TILES) for i in range(3)]
                        dve.wait_ge(*ev(g))
                        cj = cbuf[:, s, 0:n]
                        dve.tensor_scalar(cj, gpad[:, s, 1:1 + n], w[1], dcol("ffn_b", j + layer * F_TILES), ALU.mult, ALU.add
                                          ).then_inc(dve_step, 1)
                        dve.wait_ge(dve_step, v(J * 2 + 1))
                        dve.scalar_tensor_tensor(cj, gpad[:, s, 0:n], w[0], cj, ALU.mult, ALU.add).then_inc(dve_step, 1)
                        dve.wait_ge(dve_step, v(J * 2 + 2))
                        dve.scalar_tensor_tensor(cj, gpad[:, s, 2:2 + n], w[2], cj, ALU.mult, ALU.add).then_inc(conv_ready, 1)
                        dve.wait_ge(gelu_ready, v(J + 1))
                    else:
                        dve.wait_ge(*ev(g))
                    dve.wait_ge(chunk_done, done(g + 1))
                    dve.wait_ge(act_lo, v(J + 1))
                    dve.tensor_tensor(vbuf[:, s, 0:n], bank[(g + 1) % SLOTS][:, 0:n], cbuf[:, s, 0:n], ALU.mult).then_inc(evac[(g + 1) % SLOTS], 1)
                    dve.wait_ge(act_hi, v(J + 1))
                    o = bass.ds(v((j - j0) * T), n)
                    dve.tensor_tensor(b_lo[:, o], vbuf[:, s, 0:n], b_hi[:, o].bitcast(F32), ALU.subtract).then_inc(act_lo, 1)

                items(dve, nj, SLOTS, body, j0)
                items(dve, KD, SLOTS, lambda m: out_body(p, g0 + 2 * nj, m))

        def residual_body(dve, dst, n, layer, stream_):
            def body(p, g0, m):
                dve.wait_ge(chunk_done, done(m + g0))
                xm = dst[:, dyn(m, 1), :].rearrange("p a b -> p (a b)")
                dve.scalar_tensor_tensor(xm, bank[(m + g0) % SLOTS][:, 0:n], modd(layer, 5, m, stream_), xm,
                                         ALU.mult, ALU.add).then_inc(evac[(m + g0) % SLOTS], 1)
            return body

        def f_body(dve):
            def body(p, g0, m):
                dve.wait_ge(chunk_done, done(m + g0))
                fm = f[:, dyn(m, 1), :].rearrange("p a b -> p (a b)")
                if p == 0:
                    dve.tensor_copy(fm, bank[(m + g0) % SLOTS][:, :]).then_inc(evac[(m + g0) % SLOTS], 1)
                else:
                    dve.tensor_tensor(fm, bank[(m + g0) % SLOTS][:, :], fm, ALU.add).then_inc(evac[(m + g0) % SLOTS], 1)
            return body

        def g_ffn_end(call):
            return G_FFN[call] + FFN_CHUNKS - 1

        def keys(d, t):
            if d == 0:
                return [(0, t + 1)]
            return [(t, 2)] if t < 2 else [(0, 2), (t, 6)]

        def tiles(d, t):
            return [k for a, b in keys(d, t) for k in range(a, b)]

        ORDER = ((0, 1, 2, 3, 4, 5), (1, 0, 5, 4, 3, 2))

        def pe_gates(pe):
            pe.wait_ge(gate_w_lo, 1)
            for t in range(6):
                src, width, c0 = (B, C, t * P) if t < 2 else (H, T, (t - 2) * P)
                last = pe_three(pe, pS[:, t * 16:(t + 1) * 16],
                                [(rows(*src, width, kt, c0, c0 + P), (wg_hi[:, kt * 16:(kt + 1) * 16], wg_lo[:, kt * 16:(kt + 1) * 16]))
                                 for kt in range(KD)])
            last.then_inc(gates_sum, 1)
            pe.wait_ge(logf_ready, 1)
            for d in range(2):
                for i, t in enumerate(ORDER[d]):
                    for e, k in enumerate(ORDER[d][:i + 1]):
                        tri = ones if k != t else const("upto") if d == 0 else const("from")
                        last = pe.matmul(pS[:, 512 + t * 8 + d * 4:512 + t * 8 + d * 4 + 4], tri,
                                         ga[:, k * 16 + d * 8 + 4:k * 16 + d * 8 + 8], start=(e == 0), stop=(e == i))
            last.then_inc(prefix_sum, 1)

        def pe_mlstm(pe):
            pe_gates(pe)
            pe.wait_ge(u_ready, 1)
            pe.wait_ge(padded, 1)
            pe.wait_ge(*ev(G_QKVO[1] + 11))
            for h in range(HEADS_M):
                k0 = (h % 2) * 64
                for d in range(2):
                    q = h * 2 + d
                    if q:
                        pe.wait_ge(mtc_ready, q * 6)
                    if h and d == 0:
                        pe.wait_ge(hs_val, h)
                    for t in range(6):
                        c = t * 8 + d * 4 + h
                        last = pe.matmul(pT[:, t * P:(t + 1) * P], u_[:, c:c + 1].to_broadcast([P, P]), ident, start=True, stop=True)
                    last.then_inc(ubc_ready, 1)
                    for i in range(8):
                        if 1 <= i <= 6:
                            t, m = i - 1, q * 6 + i - 1
                            pe.wait_ge(mp_ready, m + 1)
                            if t:
                                pe.wait_ge(mtc_ready, m)
                            else:
                                pe.wait_ge(ud_ready, q + 1)
                            for e, kt in enumerate(tiles(d, t)):
                                last = pe.transpose(pT[:, e * P:(e + 1) * P], attP[:, m % 2, kt * P:(kt + 1) * P], ident)
                            last.then_inc(mt_ready, 1)
                        if i < 6:
                            t, m = i, q * 6 + i
                            if m:
                                pe.wait_ge(mp_ready, m)
                            for a, b in keys(d, t):
                                for c0, c1 in ((a * P, min(b * P, 512)), (max(a * P, 512), b * P)):
                                    if c0 < c1:
                                        last = pe.matmul(pS[:, c0:c1], qm[k0:k0 + 64, h // 2, t * P:(t + 1) * P],
                                                         km[k0:k0 + 64, h // 2, c0:c1], start=True, stop=True)
                            last.then_inc(ms_ready, 1)
                        if i >= 2:
                            t, m = i - 2, q * 6 + i - 2
                            pe.wait_ge(mtc_ready, m + 1)
                            if m:
                                pe.wait_ge(mh_ready, m)
                            ks = tiles(d, t)
                            for e, kt in enumerate(ks):
                                last = pe.matmul(pO[:, 0:V_M + 1], attT[:, m % 2, e * P:(e + 1) * P], v_at(kt, h),
                                                 start=(e == 0), stop=(e == len(ks) - 1))
                            last.then_inc(mpv_ready, 1)
                pe.wait_ge(hs_scaled, h + 1)
                for t in range(6):
                    last = pe.transpose(pT[:, t * P:(t + 1) * P], hsum[:, t, :], ident)
                last.then_inc(hs_turned, 1)

        def act_gates(act):
            act.wait_ge(gates_in, 1)
            act.activation(ga, gt, ACT.Abs).then_inc(act_step, 1)
            act.wait_ge(act_step, 1)
            act.activation(ga, ga, ACT.Exp, scale=-1.0).then_inc(act_step, 1)
            act.wait_ge(act_step, 2)
            act.activation(ga, ga, ACT.Ln, bias=1.0).then_inc(gates_log, 1)

        def act_mlstm(act):
            act_gates(act)
            for h in range(HEADS_M):
                for d in range(2):
                    q = h * 2 + d
                    act.wait_ge(ubc_ready, q + 1)
                    act.activation(attA[:, 0, :], pT[:, 0:TC], ACT.Copy).then_inc(u_copied, 1)
                    act.wait_ge(cmax_ready, q + 1)
                    act.activation(guard, den6, ACT.Exp, scale=-1.0).then_inc(guard_ready, 1)
                    for i in range(7):
                        if i < 6:
                            t, m = i, q * 6 + i
                            if m >= 2:
                                act.wait_ge(mt_ready, m - 1)
                            act.wait_ge(u_copied, q + 1)
                            runs = [(1, t, t + 1)]
                            for a, b in keys(d, t):
                                runs += [(0, r0, r1) for r0, r1 in ((a, min(b, t)), (max(a, t + 1), b)) if r0 < r1]
                            for k, (src, r0, r1) in enumerate(runs):
                                last = act.activation(attP[:, m % 2, r0 * P:r1 * P], attA[:, src, r0 * P:r1 * P], ACT.Exp,
                                                      bias=ncm[:, t:t + 1])
                            last.then_inc(me_ready, 1)
                        if i >= 1:
                            t, m = i - 1, q * 6 + i - 1
                            act.wait_ge(mt_ready, m + 1)
                            if m >= 2:
                                act.wait_ge(mpv_ready, m - 1)
                            n = len(tiles(d, t)) * P
                            act.activation(attT[:, m % 2, 0:n], pT[:, 0:n], ACT.Copy).then_inc(mtc_ready, 1)
                act.wait_ge(mh_ready, (h + 1) * 12)
                for t in range(6):
                    last = act.activation(attP[:, 0, t * P:(t + 1) * P], hsum[:, t, :], ACT.Square, accum_out=ss[:, t:t + 1])
                last.then_inc(act_step, 1)
                act.wait_ge(act_step, 3 + h)
                act.activation(ss, ss, ACT.Sqrt, bias=EPS, scale=1.0 / V_M).then_inc(hs_sq, 1)
                act.wait_ge(hs_val, h + 1)
                o = (CT + h)
                act.activation(b_hi[:, o * C:o * C + C], hflat[:, 0:C], ACT.Copy).then_inc(hs_hi, 1)
                act.activation(h_hi[:, o * T:o * T + T], hflat[:, C:TC], ACT.Copy).then_inc(hs_hi, 1)

        hflat = hsum[:, :, :].rearrange("p a b -> p (a b)")
        den6 = small[:, 476:482]

        def link_on(s):
            count = [0]

            def link(eng, ins):
                count[0] += 1
                ins.then_inc(s, 1)
                eng.wait_ge(s, count[0])
            return link

        def dve_gates(dve, link):
            dve.wait_ge(gates_sum, 1)
            g3 = gt.rearrange("p (a b) -> p a b", b=16)
            dve.tensor_tensor(g3, pS[:, 0:96].rearrange("p (a b) -> p a b", b=16),
                              pc[:, _cols["gate_bias"]:_cols["gate_bias"] + 16].unsqueeze(1).broadcast_to([P, 6, 16]), ALU.add
                              ).then_inc(gates_in, 1)
            dve.wait_ge(gates_log, 1)
            dve.scalar_tensor_tensor(ga, gt, 0.0, ga, ALU.min, ALU.subtract).then_inc(logf_ready, 1)
            dve.wait_ge(prefix_sum, 1)
            link(dve, dve.tensor_copy(bcum, pS[:, 512:560]))
            dve.tensor_tensor(u_.rearrange("p (a d h) -> p a d h", d=2, h=4),
                              gt.rearrange("p (a d e) -> p a d e", d=2, e=8)[:, :, :, 0:4],
                              bcum.rearrange("p (a d h) -> p a d h", d=2, h=4), ALU.subtract).then_inc(u_ready, 1)

        def dve_mlstm(dve, link):
            dve_gates(dve, link)
            for h in range(HEADS_M):
                if h:
                    dve.wait_ge(hs_lo, 2 * h)
                for d in range(2):
                    q = h * 2 + d
                    dve.wait_ge(u_copied, q + 1)
                    if q:
                        dve.wait_ge(me_ready, q * 6)
                    dve.tensor_tensor(attA[:, 1, :].rearrange("p (a b) -> p a b", b=P), pT[:, 0:TC].rearrange("p (a b) -> p a b", b=P),
                                      const("mask_f" if d == 0 else "mask_b").unsqueeze(1).broadcast_to([P, 6, P]), ALU.add
                                      ).then_inc(ud_ready, 1)
                    link(dve, dve.tensor_reduce(tmax, attA[:, 0, :].rearrange("p (a b) -> p a b", b=P), AX_X, ALU.max))
                    dve.wait_ge(ud_ready, q + 1)
                    link(dve, dve.tensor_reduce(dmax, attA[:, 1, :].rearrange("p (a b) -> p a b", b=P), AX_X, ALU.max))
                    link(dve, dve.memset(pmax[:, ORDER[d][0]:ORDER[d][0] + 1], -3e38))
                    for i in range(1, 6):
                        a, b = ORDER[d][i - 1], ORDER[d][i]
                        link(dve, dve.tensor_tensor(pmax[:, b:b + 1], pmax[:, a:a + 1], tmax[:, a:a + 1], ALU.max))
                    link(dve, dve.tensor_tensor(pmax[:, 0:6], pmax[:, 0:6], dmax, ALU.max))
                    link(dve, dve.tensor_scalar(ncm, pmax[:, 0:6], -1.0, None, ALU.mult))
                    dve.tensor_tensor(den6, bcum.rearrange("p (a e) -> p a e", e=8)[:, :, d * 4 + h], pmax[:, 0:6], ALU.add
                                      ).then_inc(cmax_ready, 1)
                    for i in range(8):
                        if i < 6:
                            t, m = i, q * 6 + i
                            dve.wait_ge(me_ready, m + 1)
                            dve.wait_ge(ms_ready, m + 1)
                            for a, b in keys(d, t):
                                pk = attP[:, m % 2, a * P:b * P]
                                last = dve.scalar_tensor_tensor(pk, pS[:, a * P:b * P], QK_M ** -0.5, pk, ALU.mult, ALU.mult)
                            last.then_inc(mp_ready, 1)
                        if i >= 2:
                            t, m = i - 2, q * 6 + i - 2
                            dve.wait_ge(mpv_ready, m + 1)
                            dve.wait_ge(guard_ready, q + 1)
                            if m:
                                dve.wait_ge(mh_ready, m)
                            link(dve, dve.tensor_scalar(rden, pO[:, V_M:V_M + 1], -1.0, guard[:, t:t + 1], ALU.mult, ALU.max))
                            link(dve, dve.tensor_scalar(den, pO[:, V_M:V_M + 1], rden, None, ALU.max))
                            link(dve, dve.reciprocal(rden, den))
                            if d == 0:
                                dve.tensor_scalar(hsum[:, t, :], pO[:, 0:V_M], rden, None, ALU.mult).then_inc(mh_ready, 1)
                            else:
                                dve.scalar_tensor_tensor(hsum[:, t, :], pO[:, 0:V_M], rden, hsum[:, t, :], ALU.mult, ALU.add
                                                         ).then_inc(mh_ready, 1)
                dve.wait_ge(hs_sq, h + 1)
                link(dve, dve.reciprocal(rss, ss))
                for t in range(6):
                    last = dve.tensor_scalar(hsum[:, t, :], hsum[:, t, :], rss[:, t:t + 1], None, ALU.mult)
                last.then_inc(hs_scaled, 1)
                dve.wait_ge(hs_turned, h + 1)
                dve.scalar_tensor_tensor(hflat, pT[:, 0:TC], col("head_gain", h), sig_o[:, h, :], ALU.mult, ALU.mult).then_inc(hs_val, 1)
                o = (CT + h)
                dve.wait_ge(hs_hi, 2 * h + 2)
                dve.tensor_tensor(b_lo[:, o * C:o * C + C], hflat[:, 0:C], b_hi[:, o * C:o * C + C].bitcast(F32), ALU.subtract).then_inc(hs_lo, 1)
                dve.tensor_tensor(h_lo[:, o * T:o * T + T], hflat[:, C:TC], h_hi[:, o * T:o * T + T].bitcast(F32), ALU.subtract).then_inc(hs_lo, 1)

        NTOK = (T, C)

        def dve_conv(dve, s):
            n = NTOK[s]

            def body(j):
                uj = up[s][:, dyn(j, 1), :].rearrange("p a b -> p (a b)")
                acc = cacc[:, 0, 0:n]
                k0 = (j + s * CT) * TAPS + 1
                dve.wait_ge(tap_done, v(k0))
                w = [dcol("conv_w", j * TAPS + k) for k in range(TAPS)]
                dve.tensor_scalar(acc, uj[:, 1:1 + n], w[1], dcol("conv_b", j), ALU.mult, ALU.add).then_inc(tap_done, 1)
                for k in range(2, TAPS):
                    dve.wait_ge(tap_done, v(k0 + (k - 1)))
                    dve.scalar_tensor_tensor(acc, uj[:, k:k + n], w[k], acc, ALU.mult, ALU.add).then_inc(tap_done, 1)
                dve.wait_ge(tap_done, v(k0 + (TAPS - 1)))
                dve.scalar_tensor_tensor(uj[:, 0:n], uj[:, 0:n], w[0], acc, ALU.mult, ALU.add).then_inc(tap_done, 1)

            items(dve, CT, 1, body)

        tap_done = sem("tap_done")

        def u_at(s):
            return lambda kt: up[s][:, kt, 0:NTOK[s]]

        def pe_ln(pe, s, name):
            n = NTOK[s]
            pe.wait_ge(tap_done, (s + 1) * CT * TAPS + 1)
            pe.wait_ge(rt_ready, NORMS.index(name))
            pe.wait_ge(mp_ready, 48)
            for kt in range(CT):
                last = pe.matmul(pS[:, 0:n], ones, u_at(s)(kt), start=(kt == 0), stop=(kt == CT - 1))
            last.then_inc(mean_sum, 1)
            pe.wait_ge(centred, (s + 1) * CT)
            pe_norm(pe, name, n)

        def act_ln(act, s, name, dst, width):
            n = NTOK[s]
            c = NORMS.index(name)
            act_norm(act, name, u_at(s), n, width, (centred, (s + 1) * CT))
            for kt in range(CT):
                act.wait_ge(nt_ready, N_BASE[c] + kt + 1)
                act.activation(u_at(s)(kt), nt[:, kt % 3, 0:n], ACT.Silu, scale=col("ln_g", kt), bias=col("ln_b", kt)
                               ).then_inc(ln_silu, 1)
                act.wait_ge(ln_silu, s * CT + kt + 1)
                act.activation(dst[0][:, kt * width:kt * width + n], u_at(s)(kt), ACT.Copy).then_inc(nhi_ready, 1)

        ln_silu = sem("ln_silu")

        def dve_ln(dve, s, name, dst, width):
            n = NTOK[s]
            c = NORMS.index(name)
            dve.wait_ge(mean_sum, s + 1)
            for kt in range(CT):
                dve.scalar_tensor_tensor(u_at(s)(kt), pS[:, 0:n], -1.0 / (CT * P), u_at(s)(kt), ALU.mult, ALU.add).then_inc(centred, 1)
            dve.wait_ge(rt_ready, c + 1)
            dve.reciprocal(rstd[:, 0:n], rt[:, 0:n]).then_inc(rstd_ready, 1)
            dve.wait_ge(rstd_ready, c + 1)
            for kt in range(CT + 1):
                if kt < CT:
                    dve.tensor_tensor(nt[:, kt % 3, 0:n], u_at(s)(kt), rstd[:, 0:n], ALU.mult).then_inc(nt_ready, 1)
                if kt >= 1:
                    k = kt - 1
                    dve.wait_ge(nhi_ready, N_OUT[c] + k + 1)
                    o = slice(k * width, k * width + n)
                    dve.tensor_tensor(dst[1][:, o], u_at(s)(k), dst[0][:, o].bitcast(F32), ALU.subtract).then_inc(nlo_ready, 1)

        SRC = ((H, T), (B, C))

        def pe_glu(pe, s):
            items(pe, 2 * CT, SLOTS, lambda m: pe_chunk(pe, m + G_GLU[s], *SRC[s], NTOK[s]))

        def pe_qkvo(pe, s):
            src, width = SRC[s]
            pe_chunks = lambda m: pe_chunk(pe, m + G_QKVO[s], src, width, NTOK[s])
            items(pe, 4, SLOTS, pe_chunks)
            items(pe, 4, SLOTS, lambda m: pe_chunk_tokens(pe, m + (G_QKVO[s]), src, width, NTOK[s]), 4)
            items(pe, 4, SLOTS, pe_chunks, 8)

        def act_glu(act, s):
            n = NTOK[s]
            act.wait_ge(nlo_ready, norm_done("mix_ctx"))
            for j in range(CT):
                g = G_GLU[s] + 2 * j
                act_hi_part(act, g + 1)
                act.wait_ge(chunk_done, done(g))
                if s * CT + j >= 3:
                    gp = g - 6 if j >= 3 else G_GLU[0] + 2 * (CT + j - 3)
                    act.wait_ge(*ev(gp + 1))
                act.activation(sig_g[(s * CT + j) % 3][:, 0:n], bank[g % SLOTS][:, 0:n], ACT.Sigmoid).then_inc(evac[g % SLOTS], 1)
                act_hi_part(act, g + 2)

        def dve_glu(dve, s):
            n = NTOK[s]
            for j in range(CT):
                g = G_GLU[s] + 2 * j
                dve.wait_ge(*ev(g))
                dve.wait_ge(chunk_done, done(g + 1))
                dve.tensor_tensor(up[s][:, j, PADW:PADW + n], bank[(g + 1) % SLOTS][:, 0:n], sig_g[(s * CT + j) % 3][:, 0:n], ALU.mult
                                  ).then_inc(evac[(g + 1) % SLOTS], 1)

        def act_qkvo(act, s):
            n, c0 = NTOK[s], SEQ0[s]
            for i in range(12):
                g = G_QKVO[s] + i
                act_hi_part(act, g + 1)
                act.wait_ge(chunk_done, done(g))
                b = bank[g % SLOTS][:, 0:n]
                if i < 4:
                    act.activation((qm if i < 2 else km)[:, i % 2, c0:c0 + n], b, ACT.Copy).then_inc(evac[g % SLOTS], 1)
                elif i < 8:
                    h = i - 4
                    act.activation(vm[:, c0 // P:(c0 + n) // P, h * (V_M + 1):h * (V_M + 1) + V_M],
                                   b.rearrange("p (a b) -> p a b", b=P), ACT.Copy).then_inc(evac[g % SLOTS], 1)
                else:
                    act.activation(sig_o[:, i - 8, c0:c0 + n], b, ACT.Sigmoid).then_inc(evac[g % SLOTS], 1)

        def unit_steps(n, between=()):
            between = dict(between)
            for k in ("S", "M", "E"):
                yield k, 0
            for a in range(n):
                for st in between.get(a, ()):
                    yield st
                yield "T", a
                yield "C", a
                if a + 1 < n:
                    for k in ("S", "M", "E"):
                        yield k, a + 1
                yield "PV", a
                yield "O", a

        def pe_S(pe, a, ops):
            pe.wait_ge(e_ready, v(a + 1))
            for lhs, rhs, dst in ops:
                last = pe.matmul(dst, lhs, rhs, start=True, stop=True)
            last.then_inc(s_ready, 1)

        def pe_T(pe, a, nk):
            pe.wait_ge(e_ready, v(a + 2))
            pe.wait_ge(ptc_act, v(a + 1))
            pe.wait_ge(ptc_dve, v(a + 1))
            half = nk // P // 2
            for k in range(nk // P):
                o = k * P if k < half else 512 + (k - half) * P
                last = pe.transpose(pT[:, o:o + P], attP[:, a % 2, k * P:(k + 1) * P], ident)
            last.then_inc(pt_ready, 1)

        def pe_PV(pe, a, values, nv):
            pe.wait_ge(ptc_act, v(a + 2))
            pe.wait_ge(ptc_dve, v(a + 2))
            pe.wait_ge(o_ready, v(a + 2))
            for k, val in enumerate(values):
                last = pe.matmul(pO[:, 0:nv], attT[:, a % 2, k * P:(k + 1) * P], val, start=(k == 0), stop=(k == len(values) - 1))
            last.then_inc(pv_ready, 1)

        def dve_M(dve, a, nk, scale, mask=None):
            dve.wait_ge(s_ready, v(a + 1))
            p = a % 2
            if mask is None:
                dve.tensor_reduce(mx[:, p:p + 1], pS[:, 0:nk], AX_X, ALU.max).then_inc(mx_ready, 1)
            else:
                dve.sem_inc(scores_seen, 1)
                dve.tensor_tensor_reduce(attA[:, p, 0:nk], pS[:, 0:nk], mask, scale, -3e38, ALU.add, ALU.max,
                                         mx[:, p:p + 1]).then_inc(mx_ready, 1)
            dve.wait_ge(mx_ready, v(a + 1))
            dve.tensor_scalar(nm[:, p:p + 1], mx[:, p:p + 1], -scale if mask is None else -1.0, None, ALU.mult).then_inc(nm_ready, 1)

        mx_ready, scores_seen = sem("mx_ready"), sem("scores_seen")

        def act_E(act, a, nk, scale, masked=False):
            p = a % 2
            act.wait_ge(nm_ready, v(a + 1))
            act.wait_ge(pt_ready, v(a + 1))
            act.wait_ge(o_ready, v(a + 1))
            src = attA[:, p, 0:nk] if masked else pS[:, 0:nk]
            act.activation(attP[:, p, 0:nk], src, ACT.Exp, bias=nm[:, p:p + 1], scale=1.0 if masked else scale,
                           accum_out=esum[:, p:p + 1]).then_inc(e_ready, 1)

        def act_C(act, a, nk):
            act.wait_ge(pt_ready, v(a + 3))
            act.wait_ge(pv_ready, v(a + (CR - 1)))
            act.activation(attT[:, a % 2, 0:nk // 2], pT[:, 0:nk // 2], ACT.Copy).then_inc(ptc_act, 1)

        def dve_C(dve, a, nk):
            dve.wait_ge(pt_ready, v(a + 3))
            dve.wait_ge(pv_ready, v(a + (CR - 1)))
            dve.tensor_copy(attT[:, a % 2, nk // 2:nk], pT[:, 512:512 + nk // 2]).then_inc(ptc_dve, 1)

        def dve_O(dve, a, store):
            p = a % 2
            dve.wait_ge(pv_ready, v(a + (CR + 1)))
            dve.reciprocal(rsum[:, p:p + 1], esum[:, p:p + 1]).then_inc(r_ready, 1)
            dve.wait_ge(r_ready, v(a + 1))
            store(a, rsum[:, p:p + 1])

        r_ready = sem("r_ready")

        HB = 4
        UA = HB * TB

        def mla_schedule():
            between = {}
            for e in range(1, HB):
                between[(e - 1) * TB] = [("proj", e), ("copy", e)]
                between[(e - 1) * TB + 1] = [("sums", e), ("rt", e)]
                between[(e - 1) * TB + 2] = [("norm", e), ("rot", e)]
                between[(e - 1) * TB + 3] = [("rope", e)]
            first = [(k, 0) for k in ("proj", "copy", "sums", "rt", "norm", "rot", "rope")]
            return first + list(unit_steps(UA, between.items()))

        q_src = (b_hi[:, KD * T // 2:], b_lo[:, KD * T // 2:])

        def g_heads(i, c):
            return i * SLOTS + (G_HEADS + c)

        def pe_mla_heads(pe):
            pe.wait_ge(nlo_ready, norm_done("ckv_lat"))
            pe.wait_ge(rope_in, 32)

            def body(i):
                a0 = i * UA
                for step, k in mla_schedule():
                    e = k if step in ("proj", "sums", "rot") else k // TB
                    n = i * HB + e
                    if step == "proj":
                        qc, off = g_heads(i, e // 2), (e % 2) * 4
                        kc = g_heads(i, 2)
                        if e % 2 == 0:
                            pe_wait_chunk(pe, qc)
                        if e == 0:
                            pe.wait_ge(lo_ready, v(kc + 1))
                        pe.wait_ge(hq_ready, v(n + 1))
                        pe.wait_ge(o_ready, v(a0 + (max(e - 1, 0) * TB + 2)))
                        sq_, sk = qc % SLOTS, kc % SLOTS
                        last = pe_three(pe, bank[0][:, :], [(wt(sq_, off + kt), rows(*q_src, T, kt, 0, T)) for kt in range(4)])
                        if e % 2:
                            last.then_inc(chunk_done, 1)
                        kt2 = [(wt(sk, e * 2 + kt), rows(h_hi, h_lo, TC, kt, C, TC)) for kt in range(2)]
                        pe_three(pe, bank[1][:, :], kt2)
                        for t in range(6):
                            dst = pO[:, 256 + t * 64:320 + t * 64] if t < 2 else bank[2][:, t * 64 + 128:t * 64 + 192]
                            pe_three(pe, dst, [(rows(h_hi, h_lo, TC, kt, t * P, (t + 1) * P), wt(sk, e * 2 + kt, 64, 128)) for kt in range(2)])
                        pe_three(pe, bank[2][:, 0:C], [(wt(sk, e * 2 + kt), rows(h_hi, h_lo, TC, kt, 0, C)) for kt in range(2)]
                                 ).then_inc(hq_proj, 1)
                    elif step == "sums":
                        pe.wait_ge(hq_sq, v(n + 1))
                        o96 = ones[0:QK_A, 0:QK_A]
                        last = pe.matmul(bank[0][0:QK_A, :], o96, hsq[0:QK_A, 0:T], start=True, stop=True)
                        if e == HB - 1:
                            last.then_inc(chunk_done, 1)
                        pe.matmul(bank[1][0:QK_A, :], o96, hsq[0:QK_A, T + C:T + TC], start=True, stop=True)
                        pe.matmul(bank[2][0:QK_A, 0:C], o96, hsq[0:QK_A, T:T + C], start=True, stop=True).then_inc(hq_sums, 1)
                    elif step == "rot":
                        pe.wait_ge(hq_norm, v(n + 1))
                        R = const("rotm", QK_A, QK_A)
                        pe.matmul(bank[0][0:QK_A, :], R, qf[0:QK_A, e % 2, :], start=True, stop=True)
                        last = pe.matmul(bank[1][0:QK_A, :], R, kf[0:QK_A, e % 2, C:TC], start=True, stop=True)
                        last.then_inc(hq_rot, 1)
                    elif step == "S":
                        t, sl = k % TB, e % 2
                        if t == 0:
                            pe.wait_ge(hq_ready, v(n + 2))
                        lhs = qf[0:QK_A, sl, t * P:(t + 1) * P]
                        pe_S(pe, a0 + k, [(lhs, kf[0:QK_A, sl, 0:512], pS[:, 0:512]), (lhs, kf[0:QK_A, sl, 512:TC], pS[:, 512:TC])])
                    elif step == "T":
                        pe_T(pe, a0 + k, TC)
                    elif step == "PV":
                        if k % TB == 0 and e + 1 < HB:
                            pe.wait_ge(hq_copied, v(n + 2))
                        pe_PV(pe, a0 + k, [va[:, e % 2, kt, :] for kt in range(6)], 64)

            items(pe, HEADS_A // HB, 1, body)
            for m in range(KD):
                half = pT[:, (m % 2) * 512:(m % 2) * 512 + 512]
                if m == 0:
                    pe.wait_ge(o_ready, HEADS_A * TB + 2)
                if m >= 2:
                    pe.wait_ge(o_lo, m - 1)
                for t in range(TB):
                    last = pe.transpose(half[:, t * P:(t + 1) * P], o_all[:, t, m * P:(m + 1) * P], ident)
                last.then_inc(o_turned, 1)

        hq_proj = sem("hq_proj")

        def act_mla_heads(act):
            def body(i):
                a0 = i * UA
                for step, k in mla_schedule():
                    e = k if step in ("copy", "rt") else k // TB
                    n = i * HB + e
                    sl = e % 2
                    if step == "copy":
                        if e == 0:
                            act_hi_part(act, g_heads(i, 1))
                            act_hi_part(act, g_heads(i, 2))
                        if e == 2:
                            act_hi_part(act, g_heads(i, 3))
                        act.wait_ge(hq_proj, v(n + 1))
                        act.wait_ge(pv_ready, v(n * TB + (CR - TB)))
                        act.activation(qraw[0:QK_A, :], bank[0][0:QK_A, :], ACT.Copy)
                        act.activation(kraw[0:NOPE, C:TC], bank[1][0:NOPE, :], ACT.Copy)
                        act.activation(kraw[0:NOPE, 0:C], bank[2][0:NOPE, 0:C], ACT.Copy)
                        act.activation(va[:, sl, 2:6, :], bank[2][:, 256:512].rearrange("p (a b) -> p a b", b=64), ACT.Copy)
                        act.activation(va[:, sl, 0:2, :], pO[:, 256:384].rearrange("p (a b) -> p a b", b=64), ACT.Copy
                                       ).then_inc(hq_copied, 1)
                        act.wait_ge(hq_copied, v(n + 1))
                        act.activation(hsq[0:QK_A, 0:T], qraw[0:QK_A, :], ACT.Square)
                        act.activation(hsq[0:QK_A, T:T + TC], kraw[0:QK_A, :], ACT.Square).then_inc(hq_sq, 1)
                    elif step == "rt":
                        act.wait_ge(hq_sums, v(n + 1))
                        w = dict(bias=EPS, scale=1.0 / QK_A)
                        r0 = act.activation(hrt[0:QK_A, 0:T], bank[0][0:QK_A, :], ACT.Sqrt, **w)
                        r1 = act.activation(hrt[0:QK_A, T + C:T + TC], bank[1][0:QK_A, :], ACT.Sqrt, **w)
                        if e == HB - 1:
                            r0.then_inc(evac[0], 1)
                            r1.then_inc(evac[1], 1)
                        act.activation(hrt[0:QK_A, T:T + C], bank[2][0:QK_A, 0:C], ACT.Sqrt, **w).then_inc(hq_rt, 1)
                    elif step == "E":
                        act_E(act, a0 + k, TC, QK_A ** -0.5)
                    elif step == "C":
                        act_C(act, a0 + k, TC)

            items(act, HEADS_A // HB, 1, body)
            for m in range(KD):
                act.wait_ge(o_turned, m + 1)
                act.activation(b_hi[:, m * T:(m + 1) * T], pT[:, (m % 2) * 512:(m % 2) * 512 + 512], ACT.Copy).then_inc(o_hi, 1)

        def dve_mla_heads(dve):
            def body(i):
                a0 = i * UA
                for step, k in mla_schedule():
                    e = k if step in ("norm", "rope") else k // TB
                    n = i * HB + e
                    sl = e % 2
                    if step == "norm":
                        dve.wait_ge(hq_rt, v(n + 1))
                        dve.reciprocal(hrt[0:QK_A, :], hrt[0:QK_A, :]).then_inc(hq_step, 1)
                        dve.wait_ge(hq_step, v(n * 3 + 1))
                        pq = slice(0, QK_A)
                        dve.scalar_tensor_tensor(qf[0:QK_A, sl, :], qraw[0:QK_A, :], col("q_gain", 0, pq), hrt[0:QK_A, 0:T], ALU.mult, ALU.mult)
                        dve.scalar_tensor_tensor(kf[0:QK_A, sl, :], kraw[0:QK_A, :], col("k_gain", 0, pq), hrt[0:QK_A, T:T + TC], ALU.mult, ALU.mult
                                                 ).then_inc(hq_norm, 1)
                    elif step == "rope":
                        dve.wait_ge(hq_rot, v(n + 1))
                        r = slice(NOPE, QK_A)
                        qv, kv = qf[r, sl, :], kf[r, sl, C:TC]
                        last = dve.tensor_tensor(mt1[r, :], bank[0][r, :], sinm[r, :], ALU.mult)
                        if e == HB - 1:
                            last.then_inc(evac[2], 1)
                        dve.tensor_tensor(qv, qv, cosm[r, :], ALU.mult)
                        dve.tensor_tensor(hsq[r, 0:T], bank[1][r, :], sinm[r, :], ALU.mult)
                        dve.tensor_tensor(kv, kv, cosm[r, :], ALU.mult).then_inc(hq_step, 1)
                        dve.wait_ge(hq_step, v(n * 3 + 2))
                        dve.tensor_tensor(qv, qv, mt1[r, :], ALU.add).then_inc(hq_step, 1)
                        dve.tensor_tensor(kv, kv, hsq[r, 0:T], ALU.add).then_inc(hq_ready, 1)
                    elif step == "M":
                        dve_M(dve, a0 + k, TC, QK_A ** -0.5)
                    elif step == "C":
                        dve_C(dve, a0 + k, TC)
                    elif step == "O":
                        t = k % TB
                        dve_O(dve, a0 + k, lambda a, r: dve.tensor_scalar(o_all[:, t, dyn(n, 64)], pO[:, 0:64], r, None, ALU.mult
                                                                          ).then_inc(o_ready, 1))

            items(dve, HEADS_A // HB, 1, body)
            for m in range(KD):
                dve.wait_ge(o_hi, m + 1)
                bm = slice(m * T, (m + 1) * T)
                dve.tensor_tensor(b_lo[:, bm], pT[:, (m % 2) * 512:(m % 2) * 512 + 512], b_hi[:, bm].bitcast(F32), ALU.subtract).then_inc(o_lo, 1)

        hq_step = sem("hq_step")

        def pe_mla_in(pe):
            pe.wait_ge(nlo_ready, norm_done("mla_lat"))
            items(pe, 7, SLOTS, lambda m: pe_chunk(pe, m + G_MLA[0], H, T, T))
            pe.wait_ge(nlo_ready, norm_done("mla_ctx"))
            items(pe, 3, SLOTS, lambda m: pe_chunk(pe, m + G_MLA[1], B, C, C))

        def act_mla_in(act):
            r = slice(NOPE, QK_A)
            dsts = [cq[:, j, :] for j in range(4)] + [ckv[:, j, C:TC] for j in range(2)] + [kraw[r, C:TC]]
            for g0, n, ds_ in ((G_MLA[0], T, dsts), (G_MLA[1], C, [ckv[:, j, 0:C] for j in range(2)] + [kraw[r, 0:C]])):
                for j, dst in enumerate(ds_):
                    act_hi_part(act, g0 + j + 1)
                    act.wait_ge(chunk_done, done(g0 + j))
                    rows_ = r if j == len(ds_) - 1 else slice(0, P)
                    act.activation(dst, bank[(g0 + j) % SLOTS][rows_, 0:n], ACT.Copy).then_inc(evac[(g0 + j) % SLOTS], 1)

        def dve_permute(dve):
            for kt in range(KD):
                dve.wait_ge(perm_a, kt + 1)
                dve.tensor_copy(x[:, kt, :], nt[:, kt % 3, :]).then_inc(perm_b, 1)

        def act_permute(act):
            act.wait_ge(*ev(g_ffn_end(2)))
            for kt in range(KD):
                if kt >= 3:
                    act.wait_ge(perm_b, kt - 2)
                act.activation(nt[:, kt % 3, :].rearrange("p (j t) -> p j t", j=TB),
                               x[:, kt, :].rearrange("p (t j) -> p j t", j=TB), ACT.Copy).then_inc(perm_a, 1)

        A_MLA = HEADS_A * TB
        UB = 2 * TB

        def a_diff(l):
            return A_MLA + l * (HEADS_D + 4) * UB

        def a_dil(l):
            return a_diff(l) + HEADS_D * UB

        R_DIFF, R_DIL = 2, 6

        def r_diff(l):
            return l * (HEADS_D * R_DIFF + 4 * R_DIL)

        def r_dil(l):
            return r_diff(l) + HEADS_D * R_DIFF

        def pe_rot(pe, g, r, par):
            pe.wait_ge(*ev(g))
            pe.wait_ge(rope_done, v(r + 1))
            pe.matmul(pT[:, par * 512:par * 512 + 512], const("rot2"), qs[:, par, :], start=True, stop=True).then_inc(rot_ready, 1)

        def act_qs(act, g, r, par):
            act.wait_ge(chunk_done, done(g))
            act.wait_ge(rope_done, v(r + 1))
            act.activation(qs[:, par, :], bank[g % SLOTS][:, :], ACT.Copy).then_inc(evac[g % SLOTS], 1)

        def dve_rope(dve, r, par, dst):
            dve.wait_ge(rot_ready, v(r + 1))
            dve.wait_ge(rope_done, v(r + 2))
            dve.tensor_tensor(t1, pT[:, par * 512:par * 512 + 512], sin2, ALU.mult)
            dve.tensor_tensor(dst, qs[:, par, :], cos2, ALU.mult).then_inc(rope_step, 1)
            dve.wait_ge(rope_step, v(r + 1))
            dve.tensor_tensor(dst, dst, t1, ALU.add).then_inc(rope_done, 1)

        rope_step = sem("rope_step")

        def halves(c):
            return slice(c * 64, c * 64 + 64)

        def turn_gs(g0, i, groups):
            return [(gi, [i * (3 * groups) + (g0 + 3 * gi + c) for c in range(3)]) for gi in range(groups)]

        def pe_pairs(pe, l, groups, g0, a00, r00, units):
            def body(i):
                for gi, (gq, gk, gv) in turn_gs(g0, i, groups):
                    r = i * (2 * groups) + (r00 + 2 * gi)
                    pe_chunk(pe, gq, H, T, T)
                    pe_chunk(pe, gk, H, T, T)
                    pe_chunk_tokens(pe, gv, H, T, T)
                    for e in range(2):
                        if gi == 0:
                            pe.wait_ge(ptc_act, v(i * UB + (a00 + 1)))
                            pe.wait_ge(ptc_dve, v(i * UB + (a00 + 1)))
                            pe.wait_ge(o_lo, v(i + o_base(l, groups)))
                        pe_rot(pe, (gq, gk)[e], r + e, e)
                pe.wait_ge(rope_done, v(i * (2 * groups) + (r00 + 2 * groups + 2)))
                pe.wait_ge(v_copied, v(i + (v_base(l, groups) + 1)))
                nk = KEYS_DIL if groups == 3 else T
                for step, k in unit_steps(UB):
                    a = i * UB + (a00 + k)
                    t, c = k // 2, k % 2
                    tok = slice(t * P, (t + 1) * P)
                    if step == "S":
                        ops = [(qr[halves(c), 0, tok], kr[halves(c), 0, :], pS[:, 0:T])]
                        for gi in range(1, groups):
                            ops.append((qr[halves(c), gi, tok], kr[halves(c), gi, tok], pS[:, T + (gi - 1) * P:T + gi * P]))
                        pe_S(pe, a, ops)
                    elif step == "T":
                        pe_T(pe, a, nk)
                    elif step == "PV":
                        if groups == 1:
                            pe_PV(pe, a, [vt[:, 0, kt, :] for kt in range(TB)], P)
                        else:
                            pe_PV(pe, a, [vt[:, 0, kt, halves(c)] for kt in range(TB)] + [vt[:, gi, t, halves(c)] for gi in (1, 2)], 64)
                if groups == 1:
                    pe.wait_ge(o_scaled, v(i + (l * HEADS_D + 1)))
                else:
                    pe.wait_ge(o_ready, v(i * UB + (a00 + UB + 2)))
                for t in range(TB):
                    last = pe.transpose(pT[:, t * P:(t + 1) * P], od[:, t, :], ident)
                last.then_inc(o_turned, 1)

            items(pe, 4, 1, body)

        def o_base(l, groups):
            return KD + l * (HEADS_D + 4) + (HEADS_D if groups == 3 else 0)

        def v_base(l, groups):
            return l * (HEADS_D + 4) + (HEADS_D if groups == 3 else 0)

        def act_pairs(act, l, groups, g0, a00, r00):
            def body(i):
                nk = KEYS_DIL if groups == 3 else T
                for gi, (gq, gk, gv) in turn_gs(g0, i, groups):
                    r = i * (2 * groups) + (r00 + 2 * gi)
                    for e, g in enumerate((gq, gk)):
                        act_hi_part(act, g + 1)
                        act_qs(act, g, r + e, e)
                    act_hi_part(act, gv + 1)
                    act.wait_ge(chunk_done, done(gv))
                    act.wait_ge(pv_ready, v(i * UB + (a00 + CR)))
                    act.activation(vt[:, gi, :, :], bank[gv % SLOTS][:, :].rearrange("p (a b) -> p a b", b=P), ACT.Copy
                                   ).then_inc(evac[gv % SLOTS], 1)
                act.wait_ge(*ev(gv))
                act.sem_inc(v_copied, 1)
                for step, k in unit_steps(UB):
                    a = i * UB + (a00 + k)
                    if step == "E":
                        act_E(act, a, nk, 64 ** -0.5, groups == 3)
                    elif step == "C":
                        act_C(act, a, nk)
                ob = o_base(l, groups)
                if groups == 1:
                    act.wait_ge(o_ready, v(i * UB + (a00 + UB + 2)))
                    for t in range(TB):
                        last = act.activation(attP[:, 0, t * P:(t + 1) * P], od[:, t, :], ACT.Square, accum_out=oss[:, t:t + 1])
                    last.then_inc(o_sq, 1)
                    act.wait_ge(o_sq, v(i * 2 + (l * 2 * HEADS_D + 1)))
                    act.activation(oss, oss, ACT.Sqrt, bias=SUBLN_EPS, scale=1.0 / P).then_inc(o_sq, 1)
                    act.wait_ge(o_val, v(i + (l * HEADS_D + 1)))
                    act.activation(b_hi[:, dyn(i, T)], t1, ACT.Copy).then_inc(o_hi, 1)
                else:
                    act.wait_ge(o_turned, v(i + (ob + 1)))
                    act.activation(b_hi[:, dyn(i, T, 4 * T)], pT[:, 0:T], ACT.Copy).then_inc(o_hi, 1)

            items(act, 4, 1, body)

        def dve_pairs(dve, l, groups, g0, a00, r00):
            def body(i):
                nk = KEYS_DIL if groups == 3 else T
                dve.wait_ge(o_lo, v(i + o_base(l, groups)))
                for gi in range(groups):
                    r = i * (2 * groups) + (r00 + 2 * gi)
                    dve_rope(dve, r, 0, qr[:, gi, :])
                    dve_rope(dve, r + 1, 1, kr[:, gi, :])
                for step, k in unit_steps(UB):
                    a = i * UB + (a00 + k)
                    t, c = k // 2, k % 2
                    if step == "M":
                        dve_M(dve, a, nk, 64 ** -0.5, masks[:, t, :] if groups == 3 else None)
                    elif step == "C":
                        dve_C(dve, a, nk)
                    elif step == "O":
                        def store(a, r):
                            if groups == 3:
                                dve.tensor_scalar(od[:, t, halves(c)], pO[:, 0:64], r, None, ALU.mult).then_inc(o_ready, 1)
                            elif c == 0:
                                dve.tensor_scalar(od[:, t, :], pO[:, 0:P], r, None, ALU.mult).then_inc(o_ready, 1)
                            else:
                                dve.tensor_scalar(lam_r, r, neg_lam[:, l:l + 1], None, ALU.mult).then_inc(lam_step, 1)
                                dve.wait_ge(lam_step, v(i * TB + (l * TB * HEADS_D + t + 1)))
                                dve.wait_ge(o_ready, v(a + 2))
                                dve.scalar_tensor_tensor(od[:, t, :], pO[:, 0:P], lam_r, od[:, t, :], ALU.mult, ALU.add).then_inc(o_ready, 1)
                        dve_O(dve, a, store)
                ob = o_base(l, groups)
                if groups == 1:
                    dve.wait_ge(o_sq, v(i * 2 + (l * 2 * HEADS_D + 2)))
                    dve.reciprocal(orss, oss).then_inc(ors_ready, 1)
                    dve.wait_ge(ors_ready, v(i + (l * HEADS_D + 1)))
                    for t in range(TB):
                        last = dve.tensor_scalar(od[:, t, :], od[:, t, :], orss[:, t:t + 1], None, ALU.mult)
                    last.then_inc(o_scaled, 1)
                    dve.wait_ge(o_turned, v(i + (ob + 1)))
                    dve.tensor_scalar(t1, pT[:, 0:T], col("subln", l), 1.0 - lambda_init(l), ALU.mult, ALU.mult).then_inc(o_val, 1)
                    dve.wait_ge(o_hi, v(i + (ob + 1)))
                    dve.tensor_tensor(b_lo[:, dyn(i, T)], t1, b_hi[:, dyn(i, T)].bitcast(F32), ALU.subtract).then_inc(o_lo, 1)
                else:
                    dve.wait_ge(o_hi, v(i + (ob + 1)))
                    o = dyn(i, T, 4 * T)
                    dve.tensor_tensor(b_lo[:, o], pT[:, 0:T], b_hi[:, o].bitcast(F32), ALU.subtract).then_inc(o_lo, 1)

            items(dve, 4, 1, body)

        lam_step, ors_ready = sem("lam_step"), sem("ors_ready")

        def lambda_init(l):
            return 0.8 - 0.6 * float(np.exp(-0.3 * l))

        def pe_merge(pe, l):
            pe.wait_ge(o_lo, KD + (l + 1) * 8)

            def body(m):
                g = m * 3 + G_MERGE[l]
                pe_chunk(pe, g, H, T, T)
                pe_chunk(pe, g + 1, H, T, T)
                s = (g + 2) % SLOTS
                pe_wait_chunk(pe, g + 2)
                pe_three(pe, bank[s][:, :], [(wt(s, kt), rows(*B, T, kt, 0, T)) for kt in range(4)])
                pe_three(pe, pO[:, :], [(wt(s, kt), rows(*B, T, kt, 0, T)) for kt in range(4, 8)]).then_inc(chunk_done, 1)

            items(pe, KD, 1, body)

        def act_merge(act, l):
            def body(m):
                g = m * 3 + G_MERGE[l]
                act.wait_ge(*ev(g - 1))
                for c in range(2):
                    act_hi_part(act, g + (c + 1))
                    act.wait_ge(chunk_done, done(g + c))
                    act.activation(sg[:, c, :], bank[(g + c) % SLOTS][:, :], ACT.Sigmoid).then_inc(evac[(g + c) % SLOTS], 1)
                act_hi_part(act, g + 3)

            items(act, KD, 1, body)
            act.wait_ge(chunk_done, done(G_MERGE[l] + 3 * KD - 1))
            for m in range(KD):
                act.wait_ge(merged, l * KD + m + 2)
                act.activation(h_hi[:, m * T:(m + 1) * T], f[:, m, :], ACT.Copy).then_inc(m_hi, 1)

        def dve_merge(dve, l):
            def body(m):
                g = m * 3 + G_MERGE[l]
                s = (g + 2) % SLOTS
                dve.wait_ge(*ev(g + 1))
                dve.wait_ge(chunk_done, done(g + 2))
                dve.wait_ge(merged, v(m + (l * KD + 1)))
                dve.tensor_tensor(tm[:, 0, :], bank[s][:, :], sg[:, 0, :], ALU.mult)
                dve.tensor_tensor(tm[:, 1, :], pO[:, :], sg[:, 1, :], ALU.mult).then_inc(evac[s], 1)
                dve.wait_ge(*ev(g + 2))
                fm = f[:, dyn(m, 1), :].rearrange("p a b -> p (a b)")
                dve.tensor_tensor(fm, tm[:, 0, :], tm[:, 1, :], ALU.add).then_inc(merged, 1)

            items(dve, KD, 1, body)
            for m in range(KD):
                dve.wait_ge(m_hi, l * KD + m + 1)
                o = slice(m * T, (m + 1) * T)
                dve.tensor_tensor(h_lo[:, o], f[:, m, :], h_hi[:, o].bitcast(F32), ALU.subtract).then_inc(m_lo, 1)

        def dve_wout(dve, l):
            def body(m):
                dve.wait_ge(chunk_done, done(m + G_OUT[l]))
                dve.tensor_copy(f[:, dyn(m, 1), :].rearrange("p a b -> p (a b)"), bank[(m + G_OUT[l]) % SLOTS][:, :]).then_inc(evac[(m + G_OUT[l]) % SLOTS], 1)
            items(dve, KD, SLOTS, body)

        def dve_post(dve, name, l, gain, before):
            c = NORMS.index(name)
            dve.wait_ge(rt_ready, c + 1)
            dve.reciprocal(rstd, rt).then_inc(rstd_ready, 1)
            dve.wait_ge(rstd_ready, c + 1)
            for kt in range(KD + 1):
                if kt < KD:
                    if kt >= 3:
                        dve.wait_ge(x_ready, before * KD + kt - 2)
                    dve.scalar_tensor_tensor(nt[:, kt % 3, :], f[:, kt, :], col(gain, l * KD + kt), rstd, ALU.mult, ALU.mult
                                             ).then_inc(nt_ready, 1)
                if kt >= 1:
                    k = kt - 1
                    dve.wait_ge(nt_ready, N_BASE[c] + k + 1)
                    dve.tensor_tensor(x[:, k, :], x[:, k, :], nt[:, k % 3, :], ALU.add).then_inc(x_ready, 1)

        def tile_of(t_, n=T):
            return lambda kt: t_[:, kt, 0:n]

        def gains(name, l):
            return lambda kt: col(name, l * KD + kt)

        block = ctx.enter_context(nc.Block())

        @block.sync
        def _(sp):
            for dst, src in ((pc[:, :], pcol), (cm[:, :], cmat), (x[:, :, :], xT), (xc[:, :, :], cT),
                             (cond_sb[:, :], cond), (wg_raw, wgate), (lam_in, lam)):
                sp.dma_start(dst, src).then_inc(consts_in, 16)

            def load_ada(i, s):
                sp.dma_start(adaring[:, s, :], ada[i]).then_inc(ada_in[s], 16)

            for g in range(SLOTS):
                sp.dma_start(w_raw[:, g, :], stream[g]).then_inc(raw_full[g], 16)
            for i in range(4):
                load_ada(i, i)
            with sp.Fori(1, n_ada // 4) as r:
                for s in range(4):
                    sp.wait_ge(ada_done, r * 4 + (s - 3))
                    sp.dma_start(adaring[:, s, :], ada[r * 4 + s]).then_inc(ada_in[s], 16)
            with sp.Fori(1, G_ALL // SLOTS) as r:
                for s in range(SLOTS):
                    sp.wait_ge(lo_ready, r * SLOTS + (s + 1 - SLOTS))
                    sp.dma_start(w_raw[:, s, :], stream[r * SLOTS + s]).then_inc(raw_full[s], 16)
            for g in range(G_ALL // SLOTS * SLOTS, G_ALL):
                sp.wait_ge(lo_ready, g - SLOTS + 1)
                sp.dma_start(w_raw[:, g % SLOTS, :], stream[g]).then_inc(raw_full[g % SLOTS], 16)
            sp.wait_ge(x_ready, 2 * LAYERS * KD)
            sp.dma_start(out, x[:, :, :]).then_inc(stored, 16)
            sp.wait_ge(stored, 16)

        @block.gpsimd
        def _(pool):
            def lo_part(g, s):
                pool.wait_ge(hi_ready, g + 1)
                pool.tensor_tensor(w_lo[:, s, :], w_raw[:, s, :], w_hi[:, s, :].bitcast(F32), ALU.subtract
                                   ).then_inc(lo_ready, 1)

            with pool.Fori(0, G_ALL // SLOTS) as r:
                for s in range(SLOTS):
                    lo_part(r * SLOTS + s, s)
            for g in range(G_ALL // SLOTS * SLOTS, G_ALL):
                lo_part(g, g % SLOTS)
        @block.tensor
        def _(pe):
            pe.sem_inc(chunk_done, SLOTS)
            pe.sem_inc(pt_ready, 2)
            pe.sem_inc(pv_ready, CR)
            pe.wait_ge(consts_in, 112)
            pe.wait_ge(silu_done, 1)

            def ada_body(i):
                s = i % 4
                pe.wait_ge(ada_in[s], v((i // 4 + 1) * 16))
                for mm in range(ADA_W):
                    for kt in range(KD):
                        o = (mm * KD + kt) * P
                        last = pe.matmul(pO[:, bass.ds(v(i * (2 * ADA_W) + 2 * mm), 2)], adaring[:, s, o:o + P],
                                         small[:, 484 + 2 * kt:486 + 2 * kt], start=(kt == 0), stop=(kt == KD - 1))
                last.then_inc(ada_done, 1)

            items(pe, n_ada, 4, ada_body)
            pe_norm(pe, "mix_lat", T)
            pe_norm(pe, "mix_ctx", C)
            pe.wait_ge(nlo_ready, norm_done("mix_lat"))
            pe_glu(pe, 0)
            pe.wait_ge(nlo_ready, norm_done("mix_ctx"))
            pe_glu(pe, 1)
            pe_qkvo(pe, 0)
            pe_qkvo(pe, 1)
            pe_mlstm(pe)
            pe_ln(pe, 0, "ln_lat")
            pe_ln(pe, 1, "ln_ctx")
            pe.wait_ge(hs_lo, 2 * HEADS_M)
            pe.wait_ge(nlo_ready, norm_done("ln_ctx"))
            pe_out(pe, G_ABOUT[0], H, T, T)
            pe_out(pe, G_ABOUT[1], B, C, C)
            pe_norm(pe, "ffn_lat", T)
            pe_ffn(pe, 0, "ffn_lat", T, T)
            pe_norm(pe, "ffn_ctx", C)
            pe_ffn(pe, 1, "ffn_ctx", C, C)
            pe_norm(pe, "mla_lat", T)
            pe_norm(pe, "mla_ctx", C)
            pe_mla_in(pe)
            pe_norm(pe, "cq", T)
            pe_norm(pe, "ckv_ctx", C)
            pe_norm(pe, "ckv_lat", T)
            pe_mla_heads(pe)
            pe.wait_ge(o_lo, KD)
            pe_out(pe, G_MLAOUT, B, T, T)
            pe_norm(pe, "mla_ffn", T)
            pe_ffn(pe, 2, "mla_ffn", T, T)
            for l in range(LAYERS):
                pe_norm(pe, f"mixpre{l}", T)
                pe.wait_ge(nlo_ready, norm_done(f"mixpre{l}"))
                pe.wait_ge(rope_in, 32 + 48)
                pe_pairs(pe, l, 1, G_DIFF[l], a_diff(l), r_diff(l), None)
                pe_pairs(pe, l, 3, G_DIL[l], a_dil(l), r_dil(l), None)
                pe_merge(pe, l)
                pe.wait_ge(m_lo, (l + 1) * KD)
                pe_out(pe, G_OUT[l], H, T, T)
                pe_norm(pe, f"mixpost{l}", T)
                pe_norm(pe, f"ffnpre{l}", T)
                pe_ffn(pe, 3 + l, f"ffnpre{l}", T, T)
                pe_norm(pe, f"ffnpost{l}", T)

        @block.scalar
        def _(act):
            act.sem_inc(ptc_act, 1)
            act.sem_inc(e_ready, 1)
            act.wait_ge(consts_in, 112)
            act.activation(small[:, 484:500], cond_sb[:, :], ACT.Silu).then_inc(silu_done, 1)
            act.activation(wg_hi[:, :], wg_raw, ACT.Copy).then_inc(gate_w_hi, 1)
            act_hi_part(act, 0)
            act.wait_ge(mod_ready, 1)
            xt, xct = tile_of(x), tile_of(xc, C)
            act_norm(act, "mix_lat", xt, T, T, None, lambda kt: modc(0, 0, kt, 0), (*H, 0))
            act_norm(act, "mix_ctx", xct, C, C, None, lambda kt: modc(0, 0, kt, 1), (*B, 0))
            act_glu(act, 0)
            act_glu(act, 1)
            act_qkvo(act, 0)
            act_qkvo(act, 1)
            act_mlstm(act)
            act_ln(act, 0, "ln_lat", H, T)
            act_ln(act, 1, "ln_ctx", B, C)
            act_out(act, G_ABOUT[0])
            act_out(act, G_ABOUT[1])
            act_norm(act, "ffn_lat", xt, T, T, ev(G_ABOUT[0] + KD - 1), lambda kt: modc(0, 3, kt, 0), (*H, 0),
                     done(G_ABOUT[0] + KD - 1))
            act.wait_ge(padded, 2)
            act.wait_ge(chunk_done, done(G_ABOUT[1] + KD - 1))
            act_ffn(act, 0, T, True)
            act_norm(act, "ffn_ctx", xct, C, C, ev(G_ABOUT[1] + KD - 1), lambda kt: modc(0, 3, kt, 1), (*H, 0),
                     done(g_ffn_end(0)))
            act.wait_ge(padded, 3)
            act_ffn(act, 1, C, True)
            act.dma_start(cosm[0:QK_A, :], trope[0]).then_inc(rope_in, 16)
            act.dma_start(sinm[0:QK_A, :], trope[1]).then_inc(rope_in, 16)
            act_norm(act, "mla_lat", xt, T, T, ev(g_ffn_end(0)), lambda kt: modc(1, 0, kt, 0), (*H, 0), done(g_ffn_end(1)))
            act_norm(act, "mla_ctx", xct, C, C, ev(g_ffn_end(1)), lambda kt: modc(1, 0, kt, 1), (*B, 0), done(g_ffn_end(1)))
            act_mla_in(act)
            act_norm(act, "cq", tile_of(cq), T, T, ev(G_MLA[1] + 2), None, (*B, KD * T // 2), done(G_MLA[1] + 2))
            act_norm(act, "ckv_ctx", tile_of(ckv, C), C, TC, None, None, (*H, 0))
            act_norm(act, "ckv_lat", lambda kt: ckv[:, kt, C:TC], T, TC, None, None, (*H, C))
            act_mla_heads(act)
            act.wait_ge(o_turned, KD)
            for dst, src in ((masks, bmask), (cos2, brope[0]), (sin2, brope[1])):
                act.dma_start(dst, src).then_inc(rope_in, 16)
            act_out(act, G_MLAOUT)
            act_norm(act, "mla_ffn", xt, T, T, ev(G_MLAOUT + KD - 1), lambda kt: modc(1, 3, kt, 0), (*H, 0),
                     done(G_MLAOUT + KD - 1))
            act.wait_ge(padded, 4)
            act_ffn(act, 2, T, True)
            act_permute(act)
            act.wait_ge(lam_sums, 2 * LAYERS)
            act.activation(lam_s, lam_s, ACT.Exp).then_inc(lam_exp, 1)
            act.wait_ge(perm_b, KD)
            ft = tile_of(f)
            for l in range(LAYERS):
                act_norm(act, f"mixpre{l}", xt, T, T, (x_ready, 2 * l * KD) if l else None, None, (*H, 0), done(G_DIFF[l] - 1))
                act_pairs(act, l, 1, G_DIFF[l], a_diff(l), r_diff(l))
                act_pairs(act, l, 3, G_DIL[l], a_dil(l), r_dil(l))
                act_merge(act, l)
                act_out(act, G_OUT[l])
                act_norm(act, f"mixpost{l}", ft, T, T, ev(G_OUT[l] + KD - 1))
                act_norm(act, f"ffnpre{l}", xt, T, T, (x_ready, (2 * l + 1) * KD), None, (*H, 0), done(G_OUT[l] + KD - 1))
                act_ffn(act, 3 + l, T, False)
                act_norm(act, f"ffnpost{l}", ft, T, T, ev(g_ffn_end(3 + l)))

        @block.vector
        def _(dve):
            for b in range(SLOTS):
                dve.sem_inc(evac[b], 1)
            dve.sem_inc(conv_ready, SLOTS)
            dve.sem_inc(act_lo, SLOTS)
            dve.sem_inc(tap_done, 1)
            dve.sem_inc(merged, 1)
            dve.sem_inc(ptc_dve, 1)
            dve.sem_inc(o_ready, 2)
            dve.sem_inc(hq_ready, 1)
            dve.sem_inc(rope_done, 2)
            link = link_on(dve_link)
            dve.wait_ge(consts_in, 112)
            dve.wait_ge(gate_w_hi, 1)
            dve.tensor_tensor(wg_lo[:, :], wg_raw, wg_hi[:, :].bitcast(F32), ALU.subtract).then_inc(gate_w_lo, 1)
            for l in range(LAYERS):
                for e in range(2):
                    o = l * 256 + e * 128
                    dve.tensor_tensor_reduce(lam_junk[:, :], lam_in[:, o:o + 64], lam_in[:, o + 64:o + 128], 1.0, 0.0, ALU.mult, ALU.add,
                                             lam_s[:, 2 * l + e:2 * l + e + 1]).then_inc(lam_sums, 1)
                    dve.wait_ge(lam_sums, 2 * l + e + 1)
            dve.wait_ge(ada_done, n_ada)
            link(dve, dve.tensor_tensor(mod[:, :, :], pO[:, 0:2 * LAYERS * ADA_M].rearrange("p (a b) -> p a b", b=2),
                                        pc[:, _cols["ada_b"]:_cols["ada_b"] + LAYERS * ADA_M].unsqueeze(2).broadcast_to([P, LAYERS * ADA_M, 2]),
                                        ALU.add))
            for l in range(LAYERS):
                for part in (1, 4):
                    o = l * ADA_M + part * KD
                    mp = mod[:, o:o + KD, :]
                    last = dve.tensor_scalar(mp, mp, 1.0, None, ALU.add)
            last.then_inc(mod_ready, 1)
            dve.wait_ge(mod_ready, 1)
            for s in range(2):
                dve.memset(up[s][:, :, 0:PADW], 0.0)
                dve.memset(up[s][:, :, PADW + NTOK[s]:2 * PADW + NTOK[s]], 0.0)
            dve.memset(vm.rearrange("p a (h e) -> p (a h) e", e=V_M + 1)[:, :, V_M:V_M + 1], 1.0).then_inc(padded, 1)
            dve.wait_ge(padded, 1)
            xt, xct = tile_of(x), tile_of(xc, C)

            def mods(l, part, s):
                return lambda kt: modc(l, part, kt, s)

            def pad_gates(n, count):
                dve.memset(gpad[:, :, 0:1], 0.0)
                dve.memset(gpad[:, :, n + 1:n + 2], 0.0).then_inc(padded, 1)
                dve.wait_ge(padded, count)

            dve_norm(dve, "mix_lat", xt, T, T, mods(0, 1, 0), mods(0, 0, 0), (*H, 0))
            dve_norm(dve, "mix_ctx", xct, C, C, mods(0, 1, 1), mods(0, 0, 1), (*B, 0))
            dve_glu(dve, 0)
            dve_glu(dve, 1)
            dve.wait_ge(*ev(G_GLU[1] + 7))
            dve_conv(dve, 0)
            dve_conv(dve, 1)
            dve_mlstm(dve, link)
            dve_ln(dve, 0, "ln_lat", H, T)
            dve_ln(dve, 1, "ln_ctx", B, C)
            dve_out_residual(dve, G_ABOUT[0], x, T, 0, 2, 0)
            dve_out_residual(dve, G_ABOUT[1], xc, C, 0, 2, 1)
            dve_norm(dve, "ffn_lat", xt, T, T, mods(0, 4, 0), mods(0, 3, 0), (*H, 0))
            pad_gates(T, 2)
            dve_ffn(dve, 0, T, True, 0, residual_body(dve, x, T, 0, 0))
            dve_norm(dve, "ffn_ctx", xct, C, C, mods(0, 4, 1), mods(0, 3, 1), (*H, 0))
            pad_gates(C, 3)
            dve_ffn(dve, 1, C, True, 0, residual_body(dve, xc, C, 0, 1))
            dve_norm(dve, "mla_lat", xt, T, T, mods(1, 1, 0), mods(1, 0, 0), (*H, 0))
            dve_norm(dve, "mla_ctx", xct, C, C, mods(1, 1, 1), mods(1, 0, 1), (*B, 0))
            dve_norm(dve, "cq", tile_of(cq), T, T, lambda kt: col("q_norm", kt), None, (*B, KD * T // 2))
            dve_norm(dve, "ckv_ctx", tile_of(ckv, C), C, TC, lambda kt: col("kv_norm", kt), None, (*H, 0))
            dve_norm(dve, "ckv_lat", lambda kt: ckv[:, kt, C:TC], T, TC, lambda kt: col("kv_norm", kt), None, (*H, C))
            dve.wait_ge(rope_in, 32)
            dve_mla_heads(dve)
            dve_out_residual(dve, G_MLAOUT, x, T, 1, 2, 0)
            dve_norm(dve, "mla_ffn", xt, T, T, mods(1, 4, 0), mods(1, 3, 0), (*H, 0))
            pad_gates(T, 4)
            dve_ffn(dve, 2, T, True, 1, residual_body(dve, x, T, 1, 0))
            dve_permute(dve)
            dve.wait_ge(lam_exp, 1)
            for l in range(LAYERS):
                nl = neg_lam[:, l:l + 1]
                link(dve, dve.tensor_tensor(nl, lam_s[:, 2 * l + 1:2 * l + 2], lam_s[:, 2 * l:2 * l + 1], ALU.subtract))
                link(dve, dve.tensor_scalar(nl, nl, lambda_init(l), None, ALU.subtract))
            dve.wait_ge(rope_in, 32 + 48)
            for l in range(LAYERS):
                dve_norm(dve, f"mixpre{l}", xt, T, T, gains("mix_pre", l), None, (*H, 0))
                dve_pairs(dve, l, 1, G_DIFF[l], a_diff(l), r_diff(l))
                dve_pairs(dve, l, 3, G_DIL[l], a_dil(l), r_dil(l))
                dve_merge(dve, l)
                dve_wout(dve, l)
                dve_post(dve, f"mixpost{l}", l, "mix_post", 2 * l)
                dve_norm(dve, f"ffnpre{l}", xt, T, T, gains("ffn_pre", l), None, (*H, 0))
                dve_ffn(dve, 3 + l, T, False, None, f_body(dve))
                dve_post(dve, f"ffnpost{l}", l, "ffn_post", 2 * l + 1)


def chunk(w, cols=P):
    k, n = w.shape
    c = np.zeros((P, KD, P), w.dtype)
    c[:, :k // P, :n] = w.reshape(k // P, P, n).transpose(1, 0, 2)
    return c.reshape(P, KD * P)


def columns(w):
    return [chunk(w[:, i:i + P]) for i in range(0, w.shape[1], P)]


def ffn_chunks(w_in, w_out):
    hidden = w_in.shape[1] // 2
    out = []
    for j0, nj in PIECES:
        for j in range(j0, j0 + nj):
            out.append(chunk(w_in[:, j * P:(j + 1) * P]))
            out.append(chunk(w_in[:, hidden + j * P:hidden + (j + 1) * P]))
        out += columns(w_out[j0 * P:(j0 + nj) * P])
    return out


def weight_stream(a):
    out = []
    w = a["ab_w_in"][0]
    glu = []
    for j in range(CT):
        glu += [chunk(w[:, 512 + j * P:512 + (j + 1) * P]), chunk(w[:, j * P:(j + 1) * P])]
    qkvo = columns(w[:, 1024:1024 + 12 * P])
    out += glu + glu + qkvo + qkvo
    out += columns(a["ab_w_out"][0]) * 2
    out += ffn_chunks(a["ffn_w_in"][0], a["ffn_w_out"][0]) * 2
    w = a["mla_w_in"][0]
    rope = np.zeros((D, P), w.dtype)
    rope[:, NOPE:QK_A] = w[:, 768:800]
    out += columns(w[:, :512])
    kv = columns(w[:, 512:768]) + [chunk(rope)]
    out += kv + kv
    uq, ukv = a["mla_w_uq"][0], a["mla_w_ukv"][0]
    for h0 in range(0, HEADS_A, 4):
        for h in (h0, h0 + 2):
            pair = np.zeros((P, KD, P), uq.dtype)
            for e in range(2):
                pair[:, e * 4:e * 4 + 4, :QK_A] = uq[:, (h + e) * QK_A:(h + e + 1) * QK_A].reshape(4, P, QK_A).transpose(1, 0, 2)
            out.append(pair.reshape(P, KD * P))
        out.append(np.concatenate([ukv[:, h * P:(h + 1) * P].reshape(2, P, P).transpose(1, 0, 2) for h in range(h0, h0 + 4)], 1
                                  ).reshape(P, KD * P))
    out += columns(a["mla_w_out"][0])
    out += ffn_chunks(a["ffn_w_in"][1], a["ffn_w_out"][1])
    for l in range(LAYERS):
        w = a["w_in_2"][l]
        at = lambda part, j: chunk(w[:, part * 512 + j * P:part * 512 + (j + 1) * P])
        for j in range(HEADS_D):
            out += [at(0, j), at(1, j), at(2, j)]
        for j in range(4):
            for gi in range(3):
                out += [at(3 + 3 * gi + c, j) for c in range(3)]
        for m in range(KD):
            cs = slice(m * P, (m + 1) * P)
            gates = w[:, 12 * 512:]
            out += [chunk(gates[:, cs]), chunk(gates[:, D:][:, cs]), chunk(np.concatenate([a["w_a_2"][l][:, cs], a["w_b_2"][l][:, cs]], 0))]
        out += columns(a["w_out_2"][l])
        out += ffn_chunks(a["w_gate_up_2"][l], a["w_down_2"][l])
    assert len(out) == G_ALL
    return np.stack(out)


def feature_columns(a):
    p = np.zeros((P, N_PCOL), np.float32)

    def put(name, w):
        p[:, _cols[name]:_cols[name] + w.shape[1]] = w

    def cols_of(w):
        return w.reshape(-1, P).T

    put("ada_b", cols_of(a["ada_b"]))
    put("conv_w", a["ab_conv_w"][0].reshape(TAPS, CT, P).transpose(2, 1, 0).reshape(P, CT * TAPS))
    for n, k in (("conv_b", "ab_conv_b"), ("ln_g", "ab_ln_g"), ("ln_b", "ab_ln_b"), ("head_gain", "ab_head_gain"),
                 ("q_norm", "mla_q_norm"), ("kv_norm", "mla_kv_norm")):
        put(n, cols_of(a[k][0]))
    p[:QK_A, _cols["q_gain"]] = a["mla_q_gain"][0]
    p[:QK_A, _cols["k_gain"]] = a["mla_k_gain"][0]
    put("ffn_w", a["ffn_conv_w"].reshape(LAYERS * 3 * F_TILES, P).T)
    put("ffn_b", cols_of(a["ffn_conv_b"]))
    put("gate_bias", np.broadcast_to(a["ab_gate_bias"][0], (P, 16)))
    for n, k in (("mix_pre", "norm_mix_pre_2"), ("mix_post", "norm_mix_post_2"), ("ffn_pre", "norm_ffn_pre_2"), ("ffn_post", "norm_ffn_post_2"),
                 ("subln", "subln_g_2")):
        put(n, cols_of(a[k]))
    return p


def shape_constants():
    i = np.arange(P)
    cm = np.zeros((P, N_CM), np.float32)

    def put(name, m):
        cm[:m.shape[0], CM[name]:CM[name] + m.shape[1]] = m

    put("ident", np.eye(P))
    put("ones", np.ones((P, P)))
    put("upto", i[:, None] <= i[None, :])
    put("from", i[:, None] >= i[None, :])
    put("mask_f", np.where(i[None, :] <= i[:, None], 0.0, NEG))
    put("mask_b", np.where(i[None, :] >= i[:, None], 0.0, NEG))
    rot = np.zeros((P, P))
    for m in range(P):
        lo = m % 64 < 32
        rot[m + 32 if lo else m - 32, m] = -1.0 if lo else 1.0
    put("rot2", rot)
    rotm = np.zeros((QK_A, QK_A))
    for m in range(NOPE, QK_A):
        even = m % 2 == 0
        rotm[m + 1 if even else m - 1, m] = -1.0 if even else 1.0
    put("rotm", rotm)
    s = np.arange(T)
    inv = 10000.0 ** (-np.arange(0, 16, 2, dtype=np.float32) / 16)
    ang = np.concatenate([(s // 64)[:, None] * inv, (s % 64)[:, None] * inv], 1).astype(np.float32)
    trope = np.zeros((2, QK_A, T), np.float32)
    trope[0, NOPE:] = np.repeat(np.cos(ang).T, 2, 0)
    trope[1, NOPE:] = np.repeat(np.sin(ang).T, 2, 0)
    tok = np.concatenate([np.arange(j, T, TB) for j in range(TB)])
    inv = 1.0 / (10000.0 ** (np.arange(0, 64, 2, dtype=np.float32) / 64))
    ang = (tok.astype(np.float32)[None, :] * inv[:, None]).astype(np.float32)
    brope = np.stack([np.tile(np.cos(ang), (4, 1)), np.tile(np.sin(ang), (4, 1))]).astype(np.float32)
    mask = np.full((P, TB, KEYS_DIL), NEG, np.float32)
    for j in range(TB):
        q = tok[j * P:(j + 1) * P]
        for k0, keys_, dil in ((0, tok, 1), (T, q, 4), (T + P, q, 16)):
            near = ((q[:, None] - keys_[None, :]) % dil == 0) & (np.abs(q[:, None] - keys_[None, :]) <= SIDE * dil)
            mask[:, j, k0:k0 + len(keys_)] = np.where(near, 0.0, NEG)
    return cm, trope, brope, mask, tok


def kernel(**inputs):
    import concourse.bacc as bacc
    from concourse.bass_utils import run_bass_kernel_spmd

    a = {k: np.asarray(w) for k, w in inputs.items()}
    cm, trope, brope, mask, tok = shape_constants()
    tiles_of = lambda m: np.ascontiguousarray(m.T.reshape(-1, P, m.shape[0]).transpose(1, 0, 2))
    ada = a["ada_w"].reshape(LAYERS, KD, P, ADA_M // ADA_W, ADA_W, P).transpose(0, 3, 2, 4, 1, 5).reshape(-1, P, ADA_W * KD * P)
    arrays = {
        "stream": weight_stream(a),
        "ada": np.ascontiguousarray(ada),
        "xT": tiles_of(a["x"][0]),
        "cT": tiles_of(a["ctx"][0]),
        "cond": np.stack([a["c"][0].reshape(KD, P).T, a["c_ctx"].reshape(KD, P).T], 2).reshape(P, 2 * KD),
        "wgate": np.ascontiguousarray(a["ab_w_in"][0][:, 2560:2576].reshape(KD, P, 16).transpose(1, 0, 2).reshape(P, KD * 16)),
        "lam": np.ascontiguousarray(np.broadcast_to(a["lam_2"].reshape(1, -1), (P, LAYERS * 256))),
        "pcol": feature_columns(a),
        "cmat": cm, "trope": trope, "brope": brope, "bmask": mask,
    }
    nc = bacc.Bacc("TRN2", target_bir_lowering=False, num_devices=1)
    d = {k: nc.dram_tensor(k, w.shape, F32, kind="ExternalInput").ap() for k, w in arrays.items()}
    out = nc.dram_tensor("out", (P, KD, T), F32, kind="ExternalOutput").ap()
    program(nc, d["stream"], d["ada"], d["xT"], d["cT"], d["cond"], d["wgate"], d["lam"], d["pcol"], d["cmat"], d["trope"], d["brope"],
            d["bmask"], out)
    got = run_bass_kernel_spmd(nc, [arrays], core_ids=[0]).results[0]["out"]
    y = np.empty((T, D), got.dtype)
    y[tok] = got.transpose(2, 1, 0).reshape(T, D)
    return y[None]
```

```python
from contextlib import ExitStack

import concourse.bass as bass
import numpy as np
from concourse import mybir

F32 = mybir.dt.float32
F32R = mybir.dt.float32r
ACT = mybir.ActivationFunctionType
ALU = mybir.AluOpType
AX_X = mybir.AxisListType.X

P = 128
D = 1024
KD = D // P
T, C = 512, 256
TC = T + C
SLOTS = 3
LN_EXP = "natural_log_exp_and_others"
EPS = 1e-6
SUBLN_EPS = 1e-5
NEG = -1e30
HEADS_M, QK_M, V_M = 4, 64, 128
TAPS = 31
CT = 4
HEADS_A, NOPE, ROPE = 16, 64, 32
QK_A = NOPE + ROPE
F_TILES = 22
PIECES = ((0, 8), (8, 8), (16, 6))
LAYERS = 2
HEADS_D = 4
GROUPS = (1, 4, 16)
SIDE = 64
KEYS_DIL = T + 2 * P
TB = T // P



class Lin:

    def __init__(self, reg, a, b):
        self.reg, self.a, self.b = reg, a, b

    def __add__(self, n):
        return Lin(self.reg, self.a, self.b + n)

    def __sub__(self, n):
        return Lin(self.reg, self.a, self.b - n)

    def __mul__(self, n):
        return Lin(self.reg, self.a * n, self.b * n)

    def __mod__(self, n):
        assert self.a % n == 0
        return self.b % n

    def __floordiv__(self, n):
        assert self.a % n == 0
        return Lin(self.reg, self.a // n, self.b // n)


def v(i):
    if isinstance(i, Lin):
        return i.reg * i.a + i.b if i.a else i.b
    return i


_at = 0


def _take(n):
    global _at
    g, _at = _at, _at + n
    return g


FFN_CHUNKS = sum(2 * n + KD for _, n in PIECES)
G_GLU = [_take(2 * CT), _take(2 * CT)]
G_QKVO = [_take(12), _take(12)]
G_ABOUT = [_take(KD), _take(KD)]
G_FFN = [_take(FFN_CHUNKS), _take(FFN_CHUNKS)]
G_MLA = [_take(7), _take(3)]
G_HEADS = _take(HEADS_A * 6 // KD)
G_MLAOUT = _take(KD)
G_FFN.append(_take(FFN_CHUNKS))
G_DIFF, G_DIL, G_MERGE, G_OUT = [], [], [], []
for _l in range(LAYERS):
    G_DIFF.append(_take(3 * HEADS_D))
    G_DIL.append(_take(9 * 4))
    G_MERGE.append(_take(3 * KD))
    G_OUT.append(_take(KD))
    G_FFN.append(_take(FFN_CHUNKS))
G_ALL = _at
ADA_M = 6 * KD
ADA_G = 4
ADA_FIRST = 2 * 2 * KD // ADA_G

_cols = {}
_nc = 0
for _name, _n in (("ada_b", LAYERS * ADA_M), ("conv_w", CT * TAPS), ("conv_b", CT), ("ln_g", CT), ("ln_b", CT),
                  ("head_gain", HEADS_M), ("q_norm", 4), ("kv_norm", 2), ("q_gain", 1), ("k_gain", 1),
                  ("ffn_w", LAYERS * 3 * F_TILES), ("ffn_b", LAYERS * F_TILES), ("gate_bias", 16),
                  ("mix_pre", LAYERS * KD), ("mix_post", LAYERS * KD), ("ffn_pre", LAYERS * KD),
                  ("ffn_post", LAYERS * KD), ("subln", LAYERS)):
    _cols[_name] = _nc
    _nc += _n
N_PCOL = _nc
CM = {n: i * P for i, n in enumerate(("ident", "ones", "upto", "from", "mask_f", "mask_b"))}
N_CM = len(CM) * P

NORMS = ["mix_lat", "mix_ctx", "ln_lat", "ln_ctx", "ffn_lat", "ffn_ctx", "mla_lat", "mla_ctx", "cq", "ckv_ctx", "ckv_lat", "mla_ffn"]
NORMS += [f"{w}{l}" for l in range(LAYERS) for w in ("mixpre", "mixpost", "ffnpre", "ffnpost")]
_k = {"ln_lat": CT, "ln_ctx": CT, "cq": 4, "ckv_ctx": 2, "ckv_lat": 2}
N_KT = [_k.get(n, KD) for n in NORMS]
N_BASE = [sum(N_KT[:i]) for i in range(len(NORMS))]
N_OUT = [sum(k for k, n in zip(N_KT[:i], NORMS) if "post" not in n) for i in range(len(NORMS))]

ARENA = 13300


def program(nc, stream, ada, xT, cT, cond, wgate, lam, pcol, cmat, trope, brope, bmask, out):
    with ExitStack() as ctx:
        def sb(name, shape, dt=F32):
            return ctx.enter_context(nc.sbuf_tensor(name, shape, dt))

        def sem(name):
            return ctx.enter_context(nc.semaphore(name))

        x = sb("x", [P, KD, T])
        xc = sb("xc", [P, KD, C])
        with nc.sbuf_tensor("under", [P, 4, KD * T], F32) as under:
            pass
        h_hi, h_lo = sb("h_hi", [P, KD * T], F32R), sb("h_lo", [P, KD * T], F32R)
        b_hi, b_lo = sb("b_hi", [P, KD * T], F32R), sb("b_lo", [P, KD * T], F32R)
        w_raw = sb("w_raw", [P, SLOTS, KD * P])
        w_hi, w_lo = sb("w_hi", [P, SLOTS, KD * P], F32R), sb("w_lo", [P, SLOTS, KD * P], F32R)
        pc = sb("pc", [P, N_PCOL])
        cm = sb("cm", [P, N_CM])
        mod = sb("mod", [P, LAYERS * ADA_M, 2])
        attA, attP, attT = sb("attA", [P, 2, TC]), sb("attP", [P, 2, TC]), sb("attT", [P, 2, TC])
        hsum = sb("hsum", [P, 6, P])
        small = sb("small", [P, 512])
        wg_raw = sb("wg_raw", [P, P])[:, :]
        wg_hi, wg_lo = sb("wg_hi", [P, 128], F32R), sb("wg_lo", [P, 128], F32R)
        cond_sb = sb("cond_sb", [P, 2 * KD])
        lam_junk = sb("lam_junk", [P, 64])
        arena = sb("arena", [P, ARENA])
        pB = ctx.enter_context(nc.psum_tensor("pB", [P, 1024], F32))
        pB2 = ctx.enter_context(nc.psum_tensor("pB2", [P, 512], F32))
        bank = [pB[:, 0:512], pB[:, 512:1024], pB2[:, :]]
        pS = ctx.enter_context(nc.psum_tensor("pS", [P, 1024], F32))
        pT = ctx.enter_context(nc.psum_tensor("pT", [P, 1024], F32))
        pO = ctx.enter_context(nc.psum_tensor("pO", [P, 512], F32))

        def view(off, *shape):
            n = int(np.prod(shape))
            assert off + n <= ARENA, (off, shape)
            v = arena[:, off:off + n]
            if len(shape) == 2:
                v = v.rearrange("p (a b) -> p a b", b=shape[1])
            elif len(shape) == 3:
                v = v.rearrange("p (a b c) -> p a b c", b=shape[1], c=shape[2])
            return v

        def flat(t):
            return t[:, :, :].rearrange("p a b -> p (a b)")

        sq = flat(attT)[:, 0:1024].rearrange("p (a b) -> p a b", b=512)
        rt, rstd = flat(attA)[:, 0:512], flat(attA)[:, 512:1024]
        nt = flat(attP)[:, 0:1536].rearrange("p (a b) -> p a b", b=512)

        lam_in = flat(attT)[:, 1024:1024 + LAYERS * 256]

        def col(name, i=0, parts=slice(0, P)):
            return pc[parts, _cols[name] + i:_cols[name] + i + 1]

        def dcol(name, i):
            return pc[:, bass.ds(v(i + _cols[name]), 1)]

        def modd(layer, part, kt, stream_):
            return mod[:, bass.ds(v(kt + (layer * ADA_M + part * KD)), 1), stream_:stream_ + 1].rearrange("p a b -> p (a b)")

        def modc(layer, part, kt, stream_):
            return mod[:, layer * ADA_M + part * KD + kt, stream_:stream_ + 1]

        def dyn(j, n, base=0):
            return bass.ds(v(j * n + base), n)

        ident, ones = cm[:, CM["ident"]:CM["ident"] + P], cm[:, CM["ones"]:CM["ones"] + P]

        def const(name, rows=P, cols=P):
            return cm[0:rows, CM[name]:CM[name] + cols]

        consts_in = sem("consts_in")
        rope_in = sem("rope_in")
        raw_full = [sem(f"raw_full{s}") for s in range(SLOTS)]
        hi_ready = sem("hi_ready")
        lo_ready = sem("lo_ready")
        chunk_done = sem("chunk_done")
        evac = [sem(f"evac{b}") for b in range(SLOTS)]
        ada_first = [sem(f"ada_first{k}") for k in range(ADA_FIRST)]
        ada_in = [sem(f"ada_in{s}") for s in range(SLOTS)]
        ada_used, ada_row, ada_turned = sem("ada_used"), sem("ada_row"), sem("ada_turned")
        silu_done = sem("silu_done")
        mod_ready = sem("mod_ready")
        gate_w_hi, gate_w_lo = sem("gate_w_hi"), sem("gate_w_lo")
        sq_ready, sq_used, rt_ready, rstd_ready = sem("sq_ready"), sem("sq_used"), sem("rt_ready"), sem("rstd_ready")
        nt_ready, nhi_ready, nlo_ready = sem("nt_ready"), sem("nhi_ready"), sem("nlo_ready")
        mean_sum, centred = sem("mean_sum"), sem("centred")
        conv_ready, gelu_ready, act_hi, act_lo = sem("conv_ready"), sem("gelu_ready"), sem("act_hi"), sem("act_lo")
        dve_step, act_step, dve_link = sem("dve_step"), sem("act_step"), sem("dve_link")
        gates_sum, gates_in, gates_log, logf_ready = sem("gates_sum"), sem("gates_in"), sem("gates_log"), sem("logf_ready")
        prefix_sum, u_ready = sem("prefix_sum"), sem("u_ready")
        ubc_ready, u_copied, ud_ready, cmax_ready, guard_ready = (sem("ubc_ready"), sem("u_copied"), sem("ud_ready"),
                                                                  sem("cmax_ready"), sem("guard_ready"))
        ms_ready, me_ready, mp_ready, mt_ready, mtc_ready, mpv_ready, mh_ready = (
            sem("ms_ready"), sem("me_ready"), sem("mp_ready"), sem("mt_ready"), sem("mtc_ready"), sem("mpv_ready"), sem("mh_ready"))
        hs_sq, hs_scaled, hs_turned, hs_val, hs_hi, hs_lo = (sem("hs_sq"), sem("hs_scaled"), sem("hs_turned"), sem("hs_val"),
                                                             sem("hs_hi"), sem("hs_lo"))
        padded = sem("padded")
        s_ready, nm_ready, e_ready, pt_ready, ptc_act, ptc_dve, pv_ready, o_ready = (
            sem("s_ready"), sem("nm_ready"), sem("e_ready"), sem("pt_ready"), sem("ptc_act"), sem("ptc_dve"),
            sem("pv_ready"), sem("o_ready"))
        hq_sq, hq_rs, hq_sums, hq_rt, hq_ready = sem("hq_sq"), sem("hq_rs"), sem("hq_sums"), sem("hq_rt"), sem("hq_ready")
        rope_done = sem("rope_done")
        o_turned, o_val, o_hi, o_lo, o_sq, o_scaled = (sem("o_turned"), sem("o_val"), sem("o_hi"), sem("o_lo"), sem("o_sq"),
                                                       sem("o_scaled"))
        vm_turned, vm_copied = sem("vm_turned"), sem("vm_copied")
        v_turned, v_copied = sem("v_turned"), sem("v_copied")
        lam_sums, lam_exp = sem("lam_sums"), sem("lam_exp")
        merged = sem("merged")
        m_hi, m_lo = sem("m_hi"), sem("m_lo")
        perm_a, perm_b = sem("perm_a"), sem("perm_b")
        x_ready = sem("x_ready")
        stored = sem("stored")

        def items(eng, n, unroll, body, start=0):
            loops = n // unroll if n // unroll >= 2 else 0
            if loops:
                with eng.Fori(0, loops) as i:
                    for u in range(unroll):
                        body(Lin(i, unroll, start + u))
            for j in range(start + loops * unroll, start + n):
                body(Lin(None, 0, j))

        def pe_wait_chunk(pe, g):
            pe.wait_ge(lo_ready, v(g + 1))
            pe.wait_ge(evac[g % SLOTS], v(g // SLOTS + 1))

        def pe_three(pe, dst, pairs, begin=True, end=True):
            last = None
            for k, ((lh, ll), (rh, rl)) in enumerate(pairs):
                pe.matmul(dst, lh, rh, start=(begin and k == 0), stop=False)
                pe.matmul(dst, lh, rl, start=False, stop=False)
                last = pe.matmul(dst, ll, rh, start=False, stop=(end and k == len(pairs) - 1))
            return last

        def wt(s, kt, c0=0, c1=P):
            return w_hi[:, s, kt * P + c0:kt * P + c1], w_lo[:, s, kt * P + c0:kt * P + c1]

        def rows(hi, lo, width, kt, c0, c1, base=0):
            o = base + kt * width
            return hi[:, o + c0:o + c1], lo[:, o + c0:o + c1]

        def pe_chunk(pe, g, src, width, n, kts=KD):
            s = g % SLOTS
            pe_wait_chunk(pe, g)
            pe_three(pe, bank[s][:, 0:n], [(wt(s, kt), rows(*src, width, kt, 0, n)) for kt in range(kts)]
                     ).then_inc(chunk_done, 1)

        def pe_first_chunks(pe, g, count, ready, src, width, n, kts=KD):
            for e in range(count):
                pe_wait_chunk(pe, g + e)
            for kt in range(kts):
                pe.wait_ge(*ready(kt))
                for e in range(count):
                    s = (g + e) % SLOTS
                    last = pe_three(pe, bank[s][:, 0:n], [(wt(s, kt), rows(*src, width, kt, 0, n))], kt == 0, kt == kts - 1)
                    if kt == kts - 1:
                        last.then_inc(chunk_done, 1)

        def act_hi_part(act, g):
            if not (isinstance(g, Lin) and g.a) and v(g) >= G_ALL:
                return
            s = g % SLOTS
            act.wait_ge(raw_full[s], v((g // SLOTS + 1) * 16))
            act.wait_ge(chunk_done, v(g + 1))
            act.activation(w_hi[:, s, :], w_raw[:, s, :], ACT.Copy).then_inc(hi_ready, 1)

        def done(g):
            return v(g + (1 + SLOTS))

        def ev(g):
            return evac[g % SLOTS], v(g // SLOTS + 2)

        H, B = (h_hi, h_lo), (b_hi, b_lo)

        def act_norm(act, name, src, n, width, src_ready=None, shift=None, dst=None, dst_free=None, eps=EPS):
            c = NORMS.index(name)
            kts, base = N_KT[c], N_BASE[c]
            act.preload_act_table_set(LN_EXP)
            if src_ready is not None:
                act.wait_ge(*src_ready)
            for kt in range(kts):
                if base + kt >= 2:
                    act.wait_ge(sq_used, base + kt - 1)
                act.activation(sq[:, kt % 2, 0:n], src(kt), ACT.Square).then_inc(sq_ready, 1)
            act.wait_ge(sq_used, base + kts)
            if c:
                act.wait_ge(nt_ready, base)
            act.activation(rt[:, 0:n], pS[:, 0:n], ACT.Ln, bias=eps, scale=1.0 / (kts * P)).then_inc(rt_ready, 1)
            act.wait_ge(rt_ready, c + 1)
            act.activation(rstd[:, 0:n], rt[:, 0:n], ACT.Exp, scale=-0.5).then_inc(rstd_ready, 1)
            if dst is not None:
                if dst_free is not None:
                    act.wait_ge(chunk_done, dst_free)
                for kt in range(kts):
                    act.wait_ge(nt_ready, base + kt + 1)
                    o = dst[2] + kt * width
                    if shift is None:
                        act.activation(dst[0][:, o:o + n], nt[:, kt % 3, 0:n], ACT.Copy).then_inc(nhi_ready, 1)
                    else:
                        act.activation(dst[0][:, o:o + n], nt[:, kt % 3, 0:n], ACT.Identity, bias=shift(kt)).then_inc(nhi_ready, 1)

        def dve_norm(dve, name, src, n, width, gain, shift=None, dst=None):
            c = NORMS.index(name)
            kts, base = N_KT[c], N_BASE[c]
            dve.wait_ge(rstd_ready, c + 1)
            if N_OUT[c]:
                dve.wait_ge(nlo_ready, N_OUT[c])
            for kt in range(kts + 1):
                if kt < kts:
                    if kt >= 3:
                        dve.wait_ge(nlo_ready, N_OUT[c] + kt - 2)
                    dve.scalar_tensor_tensor(nt[:, kt % 3, 0:n], src(kt), gain(kt), rstd[:, 0:n], ALU.mult, ALU.mult
                                             ).then_inc(nt_ready, 1)
                if kt >= 1:
                    k = kt - 1
                    dve.wait_ge(nhi_ready, N_OUT[c] + k + 1)
                    o = dst[2] + k * width
                    hi, lo = dst[0][:, o:o + n], dst[1][:, o:o + n]
                    if shift is None:
                        dve.tensor_tensor(lo, nt[:, k % 3, 0:n], hi.bitcast(F32), ALU.subtract).then_inc(nlo_ready, 1)
                    else:
                        dve.scalar_tensor_tensor(lo, nt[:, k % 3, 0:n], shift(k), hi.bitcast(F32), ALU.add, ALU.subtract
                                                 ).then_inc(nlo_ready, 1)

        def pe_norm(pe, name, n):
            c = NORMS.index(name)
            kts, base = N_KT[c], N_BASE[c]
            if c:
                pe.wait_ge(rt_ready, c)
            for kt in range(kts):
                pe.wait_ge(sq_ready, base + kt + 1)
                pe.matmul(pS[:, 0:n], ones, sq[:, kt % 2, 0:n], start=(kt == 0), stop=(kt == kts - 1)).then_inc(sq_used, 1)

        def normed(name):
            return lambda kt: (nlo_ready, N_OUT[NORMS.index(name)] + kt + 1)

        def norm_done(name):
            c = NORMS.index(name)
            return N_OUT[c] + N_KT[c]

        n_ada = LAYERS * ADA_M // ADA_G * 2
        half = KD * T // 2
        spare = [under[:, 1, 0:half], under[:, 2, half:], under[:, 3, half:]]
        row = [under[0:2, 0, i * 512:i * 512 + 512] for i in range(2)]

        def ada_place(k):
            if k < ADA_FIRST:
                return view(k * half, half) if k < 6 else spare[k - 5]
            return spare[(k - ADA_FIRST) % SLOTS]

        def pe_ada(pe, k):
            g = k // 2
            if k < ADA_FIRST:
                pe.wait_ge(ada_first[k], 16)
            else:
                pe.wait_ge(ada_in[(k - ADA_FIRST) % SLOTS], ((k - ADA_FIRST) // SLOTS + 1) * 16)
            if k % 2 == 0 and g >= 2:
                pe.wait_ge(ada_row, g - 1)
            for e in range(KD // 2):
                kt = k % 2 * (KD // 2) + e
                last = pe.matmul(bank[g % 2][0:2, :], small[:, 484 + 2 * kt:486 + 2 * kt], ada_place(k)[:, e * 512:e * 512 + 512],
                                 start=(kt == 0), stop=(kt == KD - 1))
            last.then_inc(ada_used, 1)

        def pe_ada_turn(pe, g):
            pe.wait_ge(ada_row, g + 1)
            for e in range(ADA_G):
                o = 2 * (g * ADA_G + e)
                last = pe.matmul(bank[2][:, o:o + 2], row[g % 2][:, e * P:(e + 1) * P], ident[0:2, 0:2], start=True, stop=True)
            last.then_inc(ada_turned, 1)

        def dve_ada(dve, g):
            dve.wait_ge(ada_used, 2 * g + 2)
            if g >= 2:
                dve.wait_ge(ada_turned, g - 1)
            dve.tensor_copy(row[g % 2], bank[g % 2][0:2, :]).then_inc(ada_row, 1)

        ADA_SCANS = 2 * HEADS_M
        ADA_SCAN = (n_ada - ADA_FIRST) // ADA_SCANS

        def ada_loads(q, spot):
            k0 = ADA_FIRST + q * ADA_SCAN
            return range(k0, k0 + 2) if spot == 0 else range(k0 + 1 + spot, k0 + 2 + spot)

        def ada_groups(q, late):
            k0 = ADA_FIRST + q * ADA_SCAN
            return [k // 2 for k in (range(k0 + 2, k0 + ADA_SCAN) if late else range(k0, k0 + 2)) if k % 2]

        def dve_mod(dve, link, g0, g1, count):
            m0, m1 = g0 * ADA_G, g1 * ADA_G
            dve.wait_ge(ada_turned, g1)
            link(dve, dve.tensor_tensor(mod[:, m0:m1, :], bank[2][:, 2 * m0:2 * m1].rearrange("p (a b) -> p a b", b=2),
                                        pc[:, _cols["ada_b"] + m0:_cols["ada_b"] + m1].unsqueeze(2).broadcast_to([P, m1 - m0, 2]),
                                        ALU.add))
            for l in range(LAYERS):
                for part in (1, 4):
                    o = l * ADA_M + part * KD
                    if m0 <= o < m1:
                        mp = mod[:, o:o + KD, :]
                        last = dve.tensor_scalar(mp, mp, 1.0, None, ALU.add)
            last.then_inc(mod_ready, 1)
            dve.wait_ge(mod_ready, count)

        PADW = (TAPS - 1) // 2
        up = [view(0, CT, T + 2 * PADW), view(2168, CT, C + 2 * PADW)]
        qm, km = view(3312, 2, TC), view(4848, 2, TC)
        vm = view(6384, 6, HEADS_M * (V_M + 1))
        sig_o = view(9480, HEADS_M, TC)
        cacc = view(12552, 1, T)
        vfeat = [flat(attA)[:, i * 512:i * 512 + 512] for i in range(2)]
        sig_g = [nt[:, i, :] for i in range(3)]
        gt, ga = small[:, 128:224], small[:, 224:320]
        bcum, u_ = small[:, 320:368], small[:, 368:416]
        tmax, dmax, pmax, ncm, guard = (small[:, 416:422], small[:, 424:430], small[:, 432:439], small[:, 440:446],
                                        small[:, 448:454])
        den, rden = small[:, 456:457], small[:, 458:459]
        ss, rss = small[:, 460:466], small[:, 468:474]
        SEQ0 = {0: C, 1: 0}
        WIDTH = (T, C)

        def v_at(t, h):
            return vm[:, t, h * (V_M + 1):(h + 1) * (V_M + 1)]


        gpad, cbuf, vbuf = view(8400, 3, T + 2), view(9942, 3, T), view(11478, 3, T)
        f = view(4096, KD, T)
        masks, cos2, sin2 = view(0, TB, KEYS_DIL), view(3072, T), view(3584, T)
        qs = view(4096, 2, T)
        qz = view(5120, 3, T), flat(xc)[:, 0:3 * T].rearrange("p (a b) -> p a b", b=T)
        kr = view(6656, 3, T)
        vt = view(8192, 3, TB, P)
        od = view(9728, TB, P)
        vfm = view(10752, 2, T)
        of = view(11776, T)
        t1 = view(10240, T)
        sg = view(8192, 2, T)
        tm = view(9216, 2, T)
        HB = 4
        o_all = view(0, TB, HEADS_A * 64)
        cq, ckv = view(0, 4, T), view(2048, 2, TC)
        free = 2 * TC
        qraw = [view(4096, T), under[:, 1, free + TC:free + TC + T]]
        kraw = [view(4608, TC), under[:, 1, free:free + TC]]
        qf, kf = view(5376, HB, T), view(7424, HB, TC)
        va = view(10496, 6, HB * 64)
        mt1 = view(12032, T)
        cosm = flat(attA)[:, 1024:1024 + T]
        sinm = view(12544, T)
        hsq = [under[:, 2, 0:T + TC], under[:, 0, free:free + T + TC]]
        hrt = under[:, 3, 0:T + TC]
        mx, nm, esum, rsum = small[:, 0:4], small[:, 4:8], small[:, 8:12], small[:, 12:16]
        lam_r = small[:, 40:41]
        oss, orss = small[:, 16:20], small[:, 20:24]
        lam_s, neg_lam = small[:, 24:28], small[:, 28:32]
        CR = 8

        def pe_out(pe, g0, src, width, n, kts=KD, ready=None):
            if ready is not None:
                pe_first_chunks(pe, g0, 1, ready, src, width, n, kts)
            first = 0 if ready is None else 1
            items(pe, KD - first, SLOTS, lambda m: pe_chunk(pe, m + g0, src, width, n, kts), first)

        def act_out(act, g0, made=2):
            items(act, KD + 2 - made, SLOTS, lambda m: act_hi_part(act, m + (g0 + made)))

        def dve_out_residual(dve, g0, dst, n, layer, part, stream_):
            def body(m):
                dve.wait_ge(chunk_done, done(m + g0))
                xm = dst[:, dyn(m, 1), :].rearrange("p a b -> p (a b)")
                dve.scalar_tensor_tensor(xm, bank[(m + g0) % SLOTS][:, 0:n], modd(layer, part, m, stream_), xm,
                                         ALU.mult, ALU.add).then_inc(evac[(m + g0) % SLOTS], 1)
            items(dve, KD, SLOTS, body)

        def g_piece(call, p):
            return G_FFN[call] + sum(2 * n + KD for _, n in PIECES[:p])

        def pe_ffn(pe, call, norm, n, width):
            for p, (j0, nj) in enumerate(PIECES):
                g0 = g_piece(call, p)
                first = 0 if p else 2
                if first:
                    pe_first_chunks(pe, g0, first, normed(norm), H, width, n)
                items(pe, 2 * nj - first, SLOTS, lambda m: pe_chunk(pe, m + g0, H, width, n), first)
                pe_out(pe, g0 + 2 * nj, B, T, n, nj, lambda kt: (act_lo, call * F_TILES + j0 + kt + 1 + SLOTS))

        def act_ffn(act, call, n, conv):
            for p, (j0, nj) in enumerate(PIECES):
                g0 = g_piece(call, p)
                if p:
                    act.wait_ge(chunk_done, done(g0 - 1))

                def body(j):
                    g = (j - j0) * 2 + g0
                    s = j % SLOTS
                    act_hi_part(act, g + 2)
                    act.wait_ge(chunk_done, done(g))
                    if conv:
                        act.wait_ge(conv_ready, v(j + (call * F_TILES + 1)))
                        act.activation(gpad[:, s, 1:1 + n], bank[g % SLOTS][:, 0:n], ACT.Copy).then_inc(evac[g % SLOTS], 1)
                        act_hi_part(act, g + 3)
                        act.wait_ge(conv_ready, v(j + (call * F_TILES + 1 + SLOTS)))
                        act.activation(cbuf[:, s, 0:n], cbuf[:, s, 0:n], ACT.Gelu_apprx_tanh).then_inc(gelu_ready, 1)
                    else:
                        act.wait_ge(act_lo, v(j + (call * F_TILES + 1)))
                        act.activation(cbuf[:, s, 0:n], bank[g % SLOTS][:, 0:n], ACT.Silu).then_inc(evac[g % SLOTS], 1)
                        act_hi_part(act, g + 3)
                    act.wait_ge(*ev(g + 1))
                    o = dyn(j - j0, T) if n == T else bass.ds(v((j - j0) * T), n)
                    act.activation(b_hi[:, o], vbuf[:, s, 0:n], ACT.Copy).then_inc(act_hi, 1)

                items(act, nj, SLOTS, body, j0)
                act_out(act, g0 + 2 * nj)

        def dve_ffn(dve, call, n, conv, layer, out_body):
            for p, (j0, nj) in enumerate(PIECES):
                g0 = g_piece(call, p)
                if p:
                    dve.wait_ge(chunk_done, done(g0 - 1))

                def body(j):
                    g = (j - j0) * 2 + g0
                    s = j % SLOTS
                    J = j + call * F_TILES
                    if conv:
                        w = [dcol("ffn_w", j + (layer * 3 + i) * F_TILES) for i in range(3)]
                        dve.wait_ge(*ev(g))
                        cj = cbuf[:, s, 0:n]
                        dve.tensor_scalar(cj, gpad[:, s, 1:1 + n], w[1], dcol("ffn_b", j + layer * F_TILES), ALU.mult, ALU.add
                                          ).then_inc(dve_step, 1)
                        dve.wait_ge(dve_step, v(J * 2 + 1))
                        dve.scalar_tensor_tensor(cj, gpad[:, s, 0:n], w[0], cj, ALU.mult, ALU.add).then_inc(dve_step, 1)
                        dve.wait_ge(dve_step, v(J * 2 + 2))
                        dve.scalar_tensor_tensor(cj, gpad[:, s, 2:2 + n], w[2], cj, ALU.mult, ALU.add).then_inc(conv_ready, 1)
                        dve.wait_ge(gelu_ready, v(J + 1))
                    else:
                        dve.wait_ge(*ev(g))
                    dve.wait_ge(chunk_done, done(g + 1))
                    dve.wait_ge(act_lo, v(J + 1))
                    dve.tensor_tensor(vbuf[:, s, 0:n], bank[(g + 1) % SLOTS][:, 0:n], cbuf[:, s, 0:n], ALU.mult).then_inc(evac[(g + 1) % SLOTS], 1)
                    dve.wait_ge(act_hi, v(J + 1))
                    o = bass.ds(v((j - j0) * T), n)
                    dve.tensor_tensor(b_lo[:, o], vbuf[:, s, 0:n], b_hi[:, o].bitcast(F32), ALU.subtract).then_inc(act_lo, 1)

                items(dve, nj, SLOTS, body, j0)
                items(dve, KD, SLOTS, lambda m: out_body(p, g0 + 2 * nj, m))

        def residual_body(dve, dst, n, layer, stream_):
            def body(p, g0, m):
                dve.wait_ge(chunk_done, done(m + g0))
                xm = dst[:, dyn(m, 1), :].rearrange("p a b -> p (a b)")
                dve.scalar_tensor_tensor(xm, bank[(m + g0) % SLOTS][:, 0:n], modd(layer, 5, m, stream_), xm,
                                         ALU.mult, ALU.add).then_inc(evac[(m + g0) % SLOTS], 1)
            return body

        def f_body(dve):
            def body(p, g0, m):
                dve.wait_ge(chunk_done, done(m + g0))
                fm = f[:, dyn(m, 1), :].rearrange("p a b -> p (a b)")
                if p == 0:
                    dve.tensor_copy(fm, bank[(m + g0) % SLOTS][:, :]).then_inc(evac[(m + g0) % SLOTS], 1)
                else:
                    dve.tensor_tensor(fm, bank[(m + g0) % SLOTS][:, :], fm, ALU.add).then_inc(evac[(m + g0) % SLOTS], 1)
            return body

        def g_ffn_end(call):
            return G_FFN[call] + FFN_CHUNKS - 1

        def keys(d, t):
            if d == 0:
                return [(0, t + 1)]
            return [(t, 2)] if t < 2 else [(0, 2), (t, 6)]

        def tiles(d, t):
            return [k for a, b in keys(d, t) for k in range(a, b)]

        ORDER = ((0, 1, 2, 3, 4, 5), (1, 0, 5, 4, 3, 2))

        def pe_gates(pe):
            pe.wait_ge(gate_w_lo, 1)
            for t in range(6):
                src, width, c0 = (B, C, t * P) if t < 2 else (H, T, (t - 2) * P)
                last = pe_three(pe, pS[:, t * 16:(t + 1) * 16],
                                [(rows(*src, width, kt, c0, c0 + P), (wg_hi[:, kt * 16:(kt + 1) * 16], wg_lo[:, kt * 16:(kt + 1) * 16]))
                                 for kt in range(KD)])
            last.then_inc(gates_sum, 1)
            pe.wait_ge(logf_ready, 1)
            b4 = pS[:, 512:560].rearrange("p (t d h) -> p d t h", d=2, h=HEADS_M)
            g4 = ga.rearrange("p (t d e) -> p d t e", d=2, e=2 * HEADS_M)[:, :, :, HEADS_M:]
            shifts = [("upto", 0, (0, 6), (0, 6))] + [("ones", 0, (k, 6), (0, 6 - k)) for k in range(1, 6)]
            shifts += [("from", 1, (0, 6), (0, 6)), ("ones", 1, (0, 1), (1, 2))]
            shifts += [("ones", 1, (2, 6 - k), (2 + k, 6)) for k in range(1, 4)] + [("ones", 1, (2, 6), k) for k in range(2)]
            for k, (tri, d, to, of) in enumerate(shifts):
                src = g4[:, d, of[0]:of[1], :] if isinstance(of, tuple) else g4[:, d, of:of + 1, :].broadcast_to([P, 4, HEADS_M])
                last = pe.matmul(b4[:, d, to[0]:to[1], :], const(tri), src, start=(tri != "ones"),
                                 stop=(k == len(shifts) - 1 or shifts[k + 1][1] != d))
            last.then_inc(prefix_sum, 1)

        def pe_mlstm(pe):
            pe_gates(pe)
            pe.wait_ge(u_ready, 1)
            pe.wait_ge(padded, 1)
            pe.wait_ge(*ev(G_QKVO[1] + 11))
            pe.wait_ge(vm_copied, 2 * HEADS_M)
            for h in range(HEADS_M):
                k0 = (h % 2) * 64
                for d in range(2):
                    q = h * 2 + d
                    if q:
                        pe.wait_ge(mtc_ready, q * 6)
                    if h and d == 0:
                        pe.wait_ge(hs_val, h)
                    for t in range(6):
                        c = t * 8 + d * 4 + h
                        last = pe.matmul(pT[:, t * P:(t + 1) * P], u_[:, c:c + 1].to_broadcast([P, P]), ident, start=True, stop=True)
                    last.then_inc(ubc_ready, 1)
                    for k in ada_loads(q, 0):
                        pe_ada(pe, k)
                    if q:
                        for g in ada_groups(q - 1, 1):
                            pe_ada_turn(pe, g)
                    for i in range(8):
                        if 1 <= i <= 6:
                            t, m = i - 1, q * 6 + i - 1
                            pe.wait_ge(mp_ready, m + 1)
                            if t:
                                pe.wait_ge(mtc_ready, m)
                            else:
                                pe.wait_ge(ud_ready, q + 1)
                            for e, kt in enumerate(tiles(d, t)):
                                last = pe.transpose(pT[:, e * P:(e + 1) * P], attP[:, m % 2, kt * P:(kt + 1) * P], ident)
                            last.then_inc(mt_ready, 1)
                        if i < 6:
                            t, m = i, q * 6 + i
                            if m:
                                pe.wait_ge(mp_ready, m)
                            for a, b in keys(d, t):
                                for c0, c1 in ((a * P, min(b * P, 512)), (max(a * P, 512), b * P)):
                                    if c0 < c1:
                                        last = pe.matmul(pS[:, c0:c1], qm[k0:k0 + 64, h // 2, t * P:(t + 1) * P],
                                                         km[k0:k0 + 64, h // 2, c0:c1], start=True, stop=True)
                            last.then_inc(ms_ready, 1)
                            if i == 3:
                                for g in ada_groups(q, 0):
                                    pe_ada_turn(pe, g)
                            if i >= 3:
                                for k in ada_loads(q, i - 2):
                                    pe_ada(pe, k)
                        if i >= 2:
                            t, m = i - 2, q * 6 + i - 2
                            pe.wait_ge(mtc_ready, m + 1)
                            if m:
                                pe.wait_ge(mh_ready, m)
                            ks = tiles(d, t)
                            for e, kt in enumerate(ks):
                                last = pe.matmul(pO[:, 0:V_M + 1], attT[:, m % 2, e * P:(e + 1) * P], v_at(kt, h),
                                                 start=(e == 0), stop=(e == len(ks) - 1))
                            last.then_inc(mpv_ready, 1)
                if h == HEADS_M - 1:
                    for g in ada_groups(ADA_SCANS - 1, 1):
                        pe_ada_turn(pe, g)
                pe.wait_ge(hs_scaled, h + 1)
                for t in range(6):
                    last = pe.transpose(pT[:, t * P:(t + 1) * P], hsum[:, t, :], ident)
                last.then_inc(hs_turned, 1)

        def act_gates(act):
            act.preload_act_table_set(LN_EXP)
            act.wait_ge(gates_in, 1)
            act.activation(ga, gt, ACT.Abs).then_inc(act_step, 1)
            act.wait_ge(act_step, 1)
            act.activation(ga, ga, ACT.Exp, scale=-1.0).then_inc(act_step, 1)
            act.wait_ge(act_step, 2)
            act.activation(ga, ga, ACT.Ln, bias=1.0).then_inc(gates_log, 1)

        def act_mlstm(act):
            act_gates(act)
            for h in range(HEADS_M):
                for d in range(2):
                    q = h * 2 + d
                    act.wait_ge(ubc_ready, q + 1)
                    act.activation(attA[:, 0, :], pT[:, 0:TC], ACT.Copy).then_inc(u_copied, 1)
                    act.wait_ge(cmax_ready, q + 1)
                    act.activation(guard, den6, ACT.Exp, scale=-1.0).then_inc(guard_ready, 1)
                    for i in range(7):
                        if i < 6:
                            t, m = i, q * 6 + i
                            if m >= 2:
                                act.wait_ge(mt_ready, m - 1)
                            act.wait_ge(u_copied, q + 1)
                            runs = [(1, t, t + 1)]
                            for a, b in keys(d, t):
                                runs += [(0, r0, r1) for r0, r1 in ((a, min(b, t)), (max(a, t + 1), b)) if r0 < r1]
                            for k, (src, r0, r1) in enumerate(runs):
                                last = act.activation(attP[:, m % 2, r0 * P:r1 * P], attA[:, src, r0 * P:r1 * P], ACT.Exp,
                                                      bias=ncm[:, t:t + 1])
                            last.then_inc(me_ready, 1)
                        if i >= 1:
                            t, m = i - 1, q * 6 + i - 1
                            act.wait_ge(mt_ready, m + 1)
                            if m >= 2:
                                act.wait_ge(mpv_ready, m - 1)
                            n = len(tiles(d, t)) * P
                            act.activation(attT[:, m % 2, 0:n], pT[:, 0:n], ACT.Copy).then_inc(mtc_ready, 1)
                act.wait_ge(mh_ready, (h + 1) * 12)
                for t in range(6):
                    last = act.activation(attP[:, 0, t * P:(t + 1) * P], hsum[:, t, :], ACT.Square, accum_out=ss[:, t:t + 1])
                last.then_inc(act_step, 1)
                act.wait_ge(act_step, 3 + 2 * h)
                act.activation(ss, ss, ACT.Ln, bias=EPS, scale=1.0 / V_M).then_inc(act_step, 1)
                act.wait_ge(act_step, 4 + 2 * h)
                act.activation(rss, ss, ACT.Exp, scale=-0.5).then_inc(hs_sq, 1)
                act.wait_ge(hs_val, h + 1)
                o = (CT + h)
                act.activation(b_hi[:, o * C:o * C + C], hflat[:, 0:C], ACT.Copy).then_inc(hs_hi, 1)
                act.activation(h_hi[:, o * T:o * T + T], hflat[:, C:TC], ACT.Copy).then_inc(hs_hi, 1)

        hflat = hsum[:, :, :].rearrange("p a b -> p (a b)")
        den6 = small[:, 476:482]

        def link_on(s):
            count = [0]

            def link(eng, ins):
                count[0] += 1
                ins.then_inc(s, 1)
                eng.wait_ge(s, count[0])
            return link

        def dve_gates(dve, link):
            dve.wait_ge(gates_sum, 1)
            g3 = gt.rearrange("p (a b) -> p a b", b=16)
            dve.tensor_tensor(g3, pS[:, 0:96].rearrange("p (a b) -> p a b", b=16),
                              pc[:, _cols["gate_bias"]:_cols["gate_bias"] + 16].unsqueeze(1).broadcast_to([P, 6, 16]), ALU.add
                              ).then_inc(gates_in, 1)
            dve.wait_ge(gates_log, 1)
            dve.scalar_tensor_tensor(ga, gt, 0.0, ga, ALU.min, ALU.subtract).then_inc(logf_ready, 1)
            dve.wait_ge(prefix_sum, 1)
            link(dve, dve.tensor_copy(bcum, pS[:, 512:560]))
            dve.tensor_tensor(u_.rearrange("p (a d h) -> p a d h", d=2, h=4),
                              gt.rearrange("p (a d e) -> p a d e", d=2, e=8)[:, :, :, 0:4],
                              bcum.rearrange("p (a d h) -> p a d h", d=2, h=4), ALU.subtract).then_inc(u_ready, 1)

        def dve_mlstm(dve, link):
            dve_gates(dve, link)
            for h in range(HEADS_M):
                if h:
                    dve.wait_ge(hs_lo, 2 * h)
                for d in range(2):
                    q = h * 2 + d
                    if q:
                        for g in ada_groups(q - 1, 1):
                            dve_ada(dve, g)
                    dve.wait_ge(u_copied, q + 1)
                    if q:
                        dve.wait_ge(me_ready, q * 6)
                    dve.tensor_tensor(attA[:, 1, :].rearrange("p (a b) -> p a b", b=P), pT[:, 0:TC].rearrange("p (a b) -> p a b", b=P),
                                      const("mask_f" if d == 0 else "mask_b").unsqueeze(1).broadcast_to([P, 6, P]), ALU.add
                                      ).then_inc(ud_ready, 1)
                    link(dve, dve.tensor_reduce(tmax, attA[:, 0, :].rearrange("p (a b) -> p a b", b=P), AX_X, ALU.max))
                    dve.wait_ge(ud_ready, q + 1)
                    link(dve, dve.tensor_reduce(dmax, attA[:, 1, :].rearrange("p (a b) -> p a b", b=P), AX_X, ALU.max))
                    link(dve, dve.memset(pmax[:, ORDER[d][0]:ORDER[d][0] + 1], -3e38))
                    for i in range(1, 6):
                        a, b = ORDER[d][i - 1], ORDER[d][i]
                        link(dve, dve.tensor_tensor(pmax[:, b:b + 1], pmax[:, a:a + 1], tmax[:, a:a + 1], ALU.max))
                    link(dve, dve.tensor_tensor(pmax[:, 0:6], pmax[:, 0:6], dmax, ALU.max))
                    link(dve, dve.tensor_scalar(ncm, pmax[:, 0:6], -1.0, None, ALU.mult))
                    dve.tensor_tensor(den6, bcum.rearrange("p (a e) -> p a e", e=8)[:, :, d * 4 + h], pmax[:, 0:6], ALU.add
                                      ).then_inc(cmax_ready, 1)
                    for i in range(8):
                        if i < 6:
                            t, m = i, q * 6 + i
                            dve.wait_ge(me_ready, m + 1)
                            dve.wait_ge(ms_ready, m + 1)
                            for a, b in keys(d, t):
                                pk = attP[:, m % 2, a * P:b * P]
                                last = dve.scalar_tensor_tensor(pk, pS[:, a * P:b * P], QK_M ** -0.5, pk, ALU.mult, ALU.mult)
                            last.then_inc(mp_ready, 1)
                            if i == 1:
                                for g in ada_groups(q, 0):
                                    dve_ada(dve, g)
                        if i >= 2:
                            t, m = i - 2, q * 6 + i - 2
                            dve.wait_ge(mpv_ready, m + 1)
                            dve.wait_ge(guard_ready, q + 1)
                            if m:
                                dve.wait_ge(mh_ready, m)
                            link(dve, dve.tensor_scalar(rden, pO[:, V_M:V_M + 1], -1.0, guard[:, t:t + 1], ALU.mult, ALU.max))
                            link(dve, dve.tensor_scalar(den, pO[:, V_M:V_M + 1], rden, None, ALU.max))
                            link(dve, dve.reciprocal(rden, den))
                            if d == 0:
                                dve.tensor_scalar(hsum[:, t, :], pO[:, 0:V_M], rden, None, ALU.mult).then_inc(mh_ready, 1)
                            else:
                                dve.scalar_tensor_tensor(hsum[:, t, :], pO[:, 0:V_M], rden, hsum[:, t, :], ALU.mult, ALU.add
                                                         ).then_inc(mh_ready, 1)
                if h == HEADS_M - 1:
                    for g in ada_groups(ADA_SCANS - 1, 1):
                        dve_ada(dve, g)
                dve.wait_ge(hs_sq, h + 1)
                for t in range(6):
                    last = dve.tensor_scalar(hsum[:, t, :], hsum[:, t, :], rss[:, t:t + 1], None, ALU.mult)
                last.then_inc(hs_scaled, 1)
                dve.wait_ge(hs_turned, h + 1)
                dve.scalar_tensor_tensor(hflat, pT[:, 0:TC], col("head_gain", h), sig_o[:, h, :], ALU.mult, ALU.mult).then_inc(hs_val, 1)
                o = (CT + h)
                dve.wait_ge(hs_hi, 2 * h + 2)
                dve.tensor_tensor(b_lo[:, o * C:o * C + C], hflat[:, 0:C], b_hi[:, o * C:o * C + C].bitcast(F32), ALU.subtract).then_inc(hs_lo, 1)
                dve.tensor_tensor(h_lo[:, o * T:o * T + T], hflat[:, C:TC], h_hi[:, o * T:o * T + T].bitcast(F32), ALU.subtract).then_inc(hs_lo, 1)

        NTOK = (T, C)

        DVE_TILES = [(0, 0), (0, 1)] + [(1, j) for j in range(CT)]
        POOL_TILES = [(0, 2), (0, 3)]
        pool_acc, pool_tap = under[:, 0, 1024:1024 + T], under[:, 0, 1536:1536 + T]

        def conv_at(s, j):
            return NTOK[s], up[s][:, j, :], [col("conv_w", j * TAPS + k) for k in range(TAPS)]

        def dve_conv(dve):
            count = 0
            for s, j in DVE_TILES:
                n, uj, w = conv_at(s, j)
                acc = cacc[:, 0, 0:n]
                for k in list(range(1, TAPS)) + [0]:
                    if count:
                        dve.wait_ge(tap_done, count)
                    if k == 1:
                        ins = dve.tensor_scalar(acc, uj[:, 1:1 + n], w[1], col("conv_b", j), ALU.mult, ALU.add)
                    else:
                        ins = dve.scalar_tensor_tensor(acc if k else uj[:, 0:n], uj[:, k:k + n], w[k], acc, ALU.mult, ALU.add)
                    ins.then_inc(tap_done, 1)
                    count += 1

        def pool_conv(pool):
            count = 0
            for s, j in POOL_TILES:
                n, uj, w = conv_at(s, j)
                acc, tap = pool_acc[:, 0:n], pool_tap[:, 0:n]
                for k in list(range(1, TAPS)) + [0]:
                    if count:
                        pool.wait_ge(pool_tap_done, count)
                    if k == 1:
                        pool.tensor_scalar(acc, uj[:, 1:1 + n], w[1], col("conv_b", j), ALU.mult, ALU.add).then_inc(pool_tap_done, 1)
                        count += 1
                        continue
                    pool.tensor_scalar(tap, uj[:, k:k + n], w[k], None, ALU.mult).then_inc(pool_tap_done, 1)
                    pool.wait_ge(pool_tap_done, count + 1)
                    pool.tensor_tensor(acc if k else uj[:, 0:n], acc, tap, ALU.add).then_inc(pool_tap_done, 1)
                    count += 2

        tap_done, pool_tap_done = sem("tap_done"), sem("pool_tap_done")

        def u_at(s):
            return lambda kt: up[s][:, kt, 0:NTOK[s]]

        def pe_ln(pe, s, name):
            n = NTOK[s]
            pe.wait_ge(tap_done, len(DVE_TILES) * TAPS)
            pe.wait_ge(pool_tap_done, len(POOL_TILES) * (2 * TAPS - 1))
            pe.wait_ge(rt_ready, NORMS.index(name))
            pe.wait_ge(mp_ready, 48)
            for kt in range(CT):
                last = pe.matmul(pS[:, 0:n], ones, u_at(s)(kt), start=(kt == 0), stop=(kt == CT - 1))
            last.then_inc(mean_sum, 1)
            pe.wait_ge(centred, (s + 1) * CT)
            pe_norm(pe, name, n)

        def act_ln(act, s, name, dst, width):
            n = NTOK[s]
            c = NORMS.index(name)
            act_norm(act, name, u_at(s), n, width, (centred, (s + 1) * CT))
            for kt in range(CT):
                act.wait_ge(nt_ready, N_BASE[c] + kt + 1)
                act.activation(u_at(s)(kt), nt[:, kt % 3, 0:n], ACT.Silu, scale=col("ln_g", kt), bias=col("ln_b", kt)
                               ).then_inc(ln_silu, 1)
                act.wait_ge(ln_silu, s * CT + kt + 1)
                act.activation(dst[0][:, kt * width:kt * width + n], u_at(s)(kt), ACT.Copy).then_inc(nhi_ready, 1)

        ln_silu = sem("ln_silu")

        def dve_ln(dve, s, name, dst, width):
            n = NTOK[s]
            c = NORMS.index(name)
            dve.wait_ge(mean_sum, s + 1)
            for kt in range(CT):
                dve.scalar_tensor_tensor(u_at(s)(kt), pS[:, 0:n], -1.0 / (CT * P), u_at(s)(kt), ALU.mult, ALU.add).then_inc(centred, 1)
            dve.wait_ge(rstd_ready, c + 1)
            for kt in range(CT + 1):
                if kt < CT:
                    dve.tensor_tensor(nt[:, kt % 3, 0:n], u_at(s)(kt), rstd[:, 0:n], ALU.mult).then_inc(nt_ready, 1)
                if kt >= 1:
                    k = kt - 1
                    dve.wait_ge(nhi_ready, N_OUT[c] + k + 1)
                    o = slice(k * width, k * width + n)
                    dve.tensor_tensor(dst[1][:, o], u_at(s)(k), dst[0][:, o].bitcast(F32), ALU.subtract).then_inc(nlo_ready, 1)

        SRC = ((H, T), (B, C))

        def pe_glu(pe, s, first=0):
            items(pe, 2 * CT - first, SLOTS, lambda m: pe_chunk(pe, m + G_GLU[s], *SRC[s], NTOK[s]), first)

        def pe_qkvo(pe, s):
            src, width = SRC[s]
            for i in range(12):
                pe_chunk(pe, G_QKVO[s] + i, src, width, NTOK[s])
                if 4 < i <= 8:
                    k = s * HEADS_M + i - 5
                    pe.wait_ge(*ev(G_QKVO[s] + i - 1))
                    if k >= 2:
                        pe.wait_ge(vm_copied, k - 1)
                    for t in range(NTOK[s] // P):
                        o = k % 2 * 512 + t * P
                        last = pe.transpose(pT[:, o:o + P], vfeat[k % 2][:, t * P:(t + 1) * P], ident)
                    last.then_inc(vm_turned, 1)

        def act_glu(act, s):
            n = NTOK[s]
            act.wait_ge(nlo_ready, norm_done("mix_ctx"))
            for j in range(CT):
                g = G_GLU[s] + 2 * j
                act_hi_part(act, g + 2)
                act.wait_ge(chunk_done, done(g))
                if s * CT + j >= 3:
                    gp = g - 6 if j >= 3 else G_GLU[0] + 2 * (CT + j - 3)
                    act.wait_ge(*ev(gp + 1))
                act.activation(sig_g[(s * CT + j) % 3][:, 0:n], bank[g % SLOTS][:, 0:n], ACT.Sigmoid).then_inc(evac[g % SLOTS], 1)
                act_hi_part(act, g + 3)

        def dve_glu(dve, s):
            n = NTOK[s]
            for j in range(CT):
                g = G_GLU[s] + 2 * j
                dve.wait_ge(*ev(g))
                dve.wait_ge(chunk_done, done(g + 1))
                dve.tensor_tensor(up[s][:, j, PADW:PADW + n], bank[(g + 1) % SLOTS][:, 0:n], sig_g[(s * CT + j) % 3][:, 0:n], ALU.mult
                                  ).then_inc(evac[(g + 1) % SLOTS], 1)

        def act_qkvo(act, s):
            n, c0 = NTOK[s], SEQ0[s]
            for i in range(12):
                g = G_QKVO[s] + i
                act_hi_part(act, g + 2)
                act.wait_ge(chunk_done, done(g))
                b = bank[g % SLOTS][:, 0:n]
                if i < 4:
                    act.activation((qm if i < 2 else km)[:, i % 2, c0:c0 + n], b, ACT.Copy).then_inc(evac[g % SLOTS], 1)
                elif i < 8:
                    if s * HEADS_M + i >= 6:
                        act.wait_ge(vm_turned, s * HEADS_M + i - 5)
                    act.activation(vfeat[i % 2][:, 0:n], b, ACT.Copy).then_inc(evac[g % SLOTS], 1)
                else:
                    act.activation(sig_o[:, i - 8, c0:c0 + n], b, ACT.Sigmoid).then_inc(evac[g % SLOTS], 1)
                if 4 < i <= 8:
                    h, k = i - 5, s * HEADS_M + i - 5
                    act.wait_ge(vm_turned, k + 1)
                    act.activation(vm[:, c0 // P:(c0 + n) // P, h * (V_M + 1):h * (V_M + 1) + V_M],
                                   pT[:, k % 2 * 512:k % 2 * 512 + n].rearrange("p (a b) -> p a b", b=P), ACT.Copy).then_inc(vm_copied, 1)

        def unit_steps(n, first=True):
            if first:
                for a in range(2):
                    for k in ("S", "M", "E"):
                        yield k, a
            for a in range(n):
                yield "T", a
                yield "C", a
                if a + 2 < n:
                    for k in ("S", "M", "E"):
                        yield k, a + 2
                yield "PV", a
                yield "O", a

        score = (pS, pB)

        def pe_S(pe, a, ops):
            pe.wait_ge(e_ready, v(a + 1))
            for lhs, rhs, c0, c1 in ops:
                last = pe.matmul(score[a % 2][:, c0:c1], lhs, rhs, start=True, stop=True)
            last.then_inc(s_ready, 1)

        def pe_T(pe, a, nk):
            pe.wait_ge(e_ready, v(a + 3))
            pe.wait_ge(ptc_act, v(a + 1))
            pe.wait_ge(ptc_dve, v(a + 1))
            half = nk // P // 2
            for k in range(nk // P):
                o = k * P if k < half else 512 + (k - half) * P
                last = pe.transpose(pT[:, o:o + P], attP[:, a % 2, k * P:(k + 1) * P], ident)
            last.then_inc(pt_ready, 1)

        def pe_PV(pe, a, values, nv):
            pe.wait_ge(ptc_act, v(a + 2))
            pe.wait_ge(ptc_dve, v(a + 2))
            pe.wait_ge(o_ready, v(a + 2))
            for k, val in enumerate(values):
                last = pe.matmul(pO[:, 0:nv], attT[:, a % 2, k * P:(k + 1) * P], val, start=(k == 0), stop=(k == len(values) - 1))
            last.then_inc(pv_ready, 1)

        def dve_M(dve, a, nk, scale, mask=None):
            dve.wait_ge(s_ready, v(a + 1))
            p, q = a % 4, a % 2
            if mask is None:
                dve.tensor_reduce(mx[:, p:p + 1], score[q][:, 0:nk], AX_X, ALU.max).then_inc(mx_ready, 1)
            else:
                dve.sem_inc(scores_seen, 1)
                dve.wait_ge(e_ready, v(a + 1))
                dve.sem_inc(scores_seen, 1)
                dve.tensor_tensor_reduce(attA[:, q, 0:nk], score[q][:, 0:nk], mask, scale, -3e38, ALU.add, ALU.max,
                                         mx[:, p:p + 1]).then_inc(mx_ready, 1)
            dve.wait_ge(mx_ready, v(a + 1))
            dve.tensor_scalar(nm[:, p:p + 1], mx[:, p:p + 1], -scale if mask is None else -1.0, None, ALU.mult).then_inc(nm_ready, 1)

        mx_ready, scores_seen = sem("mx_ready"), sem("scores_seen")

        def act_E(act, a, nk, scale, masked=False):
            p, q = a % 4, a % 2
            act.wait_ge(nm_ready, v(a + 1))
            act.wait_ge(pt_ready, v(a + 1))
            src = attA[:, q, 0:nk] if masked else score[q][:, 0:nk]
            act.activation(attP[:, q, 0:nk], src, ACT.Exp, bias=nm[:, p:p + 1], scale=1.0 if masked else scale,
                           accum_out=esum[:, p:p + 1]).then_inc(e_ready, 1)

        def act_C(act, a, nk):
            act.wait_ge(pt_ready, v(a + 3))
            act.wait_ge(pv_ready, v(a + (CR - 1)))
            act.activation(attT[:, a % 2, 0:nk // 2], pT[:, 0:nk // 2], ACT.Copy).then_inc(ptc_act, 1)

        def dve_C(dve, a, nk):
            dve.wait_ge(pt_ready, v(a + 3))
            dve.wait_ge(pv_ready, v(a + (CR - 1)))
            dve.tensor_copy(attT[:, a % 2, nk // 2:nk], pT[:, 512:512 + nk // 2]).then_inc(ptc_dve, 1)

        def dve_O(dve, a, store):
            p = a % 4
            dve.wait_ge(pv_ready, v(a + (CR + 1)))
            dve.reciprocal(rsum[:, p:p + 1], esum[:, p:p + 1]).then_inc(r_ready, 1)
            dve.wait_ge(r_ready, v(a + 1))
            store(a, rsum[:, p:p + 1])

        r_ready = sem("r_ready")

        UA = HB * TB

        q_src = (b_hi[:, KD * T // 2:], b_lo[:, KD * T // 2:])
        HQ, HK, HC = (bank[0], pS[:, 0:512]), (bank[1], pS[:, 512:1024]), (bank[2][:, 0:C], pO[:, 0:C])

        def g_heads(i, c):
            return i * SLOTS + (G_HEADS + c)

        def pe_mla_heads(pe):
            pe.wait_ge(nlo_ready, norm_done("ckv_lat"))

            def sums(i, e):
                pe.wait_ge(hq_raw, v(i * HB + (e + 1)))
                o96, b = ones[0:QK_A, 0:QK_A], e % 2
                pe.matmul(HQ[b][0:QK_A, :], o96, hsq[b][0:QK_A, 0:T], start=True, stop=True)
                pe.matmul(HK[b][0:QK_A, :], o96, hsq[b][0:QK_A, T + C:T + TC], start=True, stop=True)
                pe.matmul(HC[b][0:QK_A, :], o96, hsq[b][0:QK_A, T:T + C], start=True, stop=True).then_inc(hq_sums, 1)

            def body(i):
                a0 = i * UA
                gk = g_heads(i, 2)
                sk = gk % SLOTS
                for c in range(SLOTS):
                    pe_wait_chunk(pe, g_heads(i, c))
                pe.wait_ge(ptc_act, v(a0 + 1))
                pe.wait_ge(ptc_dve, v(a0 + 1))
                wv = [w_[:, sk, :].rearrange("p (e k c) -> p k e c", e=HB, k=2) for w_ in (w_hi, w_lo)]
                for t in range(6):
                    o = (t - 2) * HB * 64
                    dst = pS[:, t * HB * 64:(t + 1) * HB * 64] if t < 2 else pT[:, o:o + HB * 64]
                    last = pe_three(pe, dst.rearrange("p (e c) -> p e c", e=HB),
                                    [(rows(h_hi, h_lo, TC, kt, t * P, (t + 1) * P), tuple(w_[:, kt, :, 64:128] for w_ in wv)) for kt in range(2)])
                    if t % 4 == 1:
                        last.then_inc(va_proj, 1)
                for e in range(HB):
                    b, n = e % 2, i * HB + e
                    gq, off = g_heads(i, e // 2), (e % 2) * 4
                    if e == 1:
                        pe.wait_ge(va_act, v(i + 1))
                        pe.wait_ge(o_ready, v(a0 + 2))
                    if e >= 2:
                        pe.wait_ge(hq_rt, v(n - 1))
                    last = pe_three(pe, HQ[b][:, :], [(wt(gq % SLOTS, off + kt), rows(*q_src, T, kt, 0, T)) for kt in range(4)])
                    if e % 2:
                        last.then_inc(chunk_done, 1)
                    pe_three(pe, HK[b][:, :], [(wt(sk, e * 2 + kt), rows(h_hi, h_lo, TC, kt, C, TC)) for kt in range(2)])
                    last = pe_three(pe, HC[b][:, :], [(wt(sk, e * 2 + kt), rows(h_hi, h_lo, TC, kt, 0, C)) for kt in range(2)])
                    last.then_inc(hq_proj, 1)
                    if e:
                        sums(i, e - 1)
                pe.wait_ge(hq_proj, v(i * HB + HB))
                pe.sem_inc(chunk_done, 1)
                sums(i, HB - 1)
                pe.wait_ge(hq_rt, v(i * HB + HB))
                pe.wait_ge(va_dve, v(i + 1))
                for step, k in unit_steps(UA):
                    e, t = k // TB, k % TB
                    if step == "S":
                        if t == 0:
                            pe.wait_ge(hq_ready, v(i * HB + (e + 2)))
                        lhs = qf[0:QK_A, e, t * P:(t + 1) * P]
                        pe_S(pe, a0 + k, [(lhs, kf[0:QK_A, e, 0:512], 0, 512), (lhs, kf[0:QK_A, e, 512:TC], 512, TC)])
                    elif step == "T":
                        pe_T(pe, a0 + k, TC)
                    elif step == "PV":
                        pe_PV(pe, a0 + k, [va[:, kt, e // 2 * P:(e // 2 + 1) * P] for kt in range(6)], P)

            items(pe, HEADS_A // HB, 1, body)
            for m in range(KD):
                half = pT[:, (m % 2) * 512:(m % 2) * 512 + 512]
                if m == 0:
                    pe.wait_ge(o_ready, HEADS_A * TB + 2)
                if m >= 2:
                    pe.wait_ge(o_lo, m - 1)
                for t in range(TB):
                    last = pe.transpose(half[:, t * P:(t + 1) * P], o_all[:, t, m * P:(m + 1) * P], ident)
                last.then_inc(o_turned, 1)

        hq_proj, hq_raw, va_proj, va_act, va_dve = sem("hq_proj"), sem("hq_raw"), sem("va_proj"), sem("va_act"), sem("va_dve")

        def act_mla_heads(act):
            for b in range(2):
                last = act.activation(hsq[b][NOPE:QK_A, T:T + TC], kraw[0][NOPE:QK_A, :], ACT.Square)
            last.then_inc(kr_sq, 1)
            act_hi_part(act, G_HEADS + 2)

            def squares(i, e):
                b = e % 2
                act.wait_ge(hq_proj, v(i * HB + (e + 1)))
                if e >= 2:
                    act.wait_ge(hq_sums, v(i * HB + e - 1))
                act.activation(hsq[b][0:QK_A, 0:T], HQ[b][0:QK_A, :], ACT.Square)
                act.activation(hsq[b][0:NOPE, T + C:T + TC], HK[b][0:NOPE, :], ACT.Square)
                act.activation(hsq[b][0:NOPE, T:T + C], HC[b][0:NOPE, :], ACT.Square).then_inc(hq_sq, 1)

            def roots(i, e):
                b = e % 2
                act.wait_ge(hq_sums, v(i * HB + (e + 1)))
                act.wait_ge(hq_ready, v(i * HB + (e + 1)))
                w = dict(bias=EPS, scale=1.0 / QK_A)
                r0 = act.activation(hrt[0:QK_A, 0:T], HQ[b][0:QK_A, :], ACT.Ln, **w)
                r1 = act.activation(hrt[0:QK_A, T + C:T + TC], HK[b][0:QK_A, :], ACT.Ln, **w)
                if e == HB - 2:
                    r0.then_inc(evac[0], 1)
                    r1.then_inc(evac[1], 1)
                if e == HB - 1:
                    r0.then_inc(evac[2], 1)
                act.activation(hrt[0:QK_A, T:T + C], HC[b][0:QK_A, :], ACT.Ln, **w).then_inc(hq_rt, 1)
                act.wait_ge(hq_rt, v(i * HB + (e + 1)))
                act.activation(hrt[0:QK_A, :], hrt[0:QK_A, :], ACT.Exp, scale=-0.5).then_inc(hq_rs, 1)

            def body(i):
                a0 = i * UA
                act.wait_ge(va_proj, v(i * 2 + 1))
                act.wait_ge(pv_ready, v(a0 + CR))
                act.activation(va[:, 0:2, :], pS[:, 0:512].rearrange("p (a b) -> p a b", a=2), ACT.Copy).then_inc(va_act, 1)
                for e in range(HB):
                    squares(i, e)
                    if e:
                        roots(i, e - 1)
                roots(i, HB - 1)
                for step, k in unit_steps(UA):
                    if step == "E":
                        act_E(act, a0 + k, TC, QK_A ** -0.5)
                    elif step == "C":
                        act_C(act, a0 + k, TC)
                        if k in (2, 6, 10):
                            act_hi_part(act, g_heads(i, SLOTS + k // 4))

            items(act, HEADS_A // HB, 1, body)
            for m in range(KD):
                act.wait_ge(o_turned, m + 1)
                act.activation(b_hi[:, m * T:(m + 1) * T], pT[:, (m % 2) * 512:(m % 2) * 512 + 512], ACT.Copy).then_inc(o_hi, 1)

        def dve_mla_heads(dve):
            r, r2 = slice(NOPE, QK_A), slice(QK_A, P)
            dve.wait_ge(kr_sq, 1)
            kr = kraw[0]
            dve.tensor_scalar(kr[NOPE:P, :], kr[NOPE:P, :], col("k_gain", 0, slice(NOPE, P)), None, ALU.mult).then_inc(kr_step, 1)
            dve.wait_ge(kr_step, 1)
            dve.tensor_tensor(mt1[r, :], kr[r2, C:TC], sinm[r2, :], ALU.mult)
            dve.tensor_tensor(kr[r, C:TC], kr[r, C:TC], cosm[r, :], ALU.mult).then_inc(kr_step, 1)
            dve.wait_ge(kr_step, 2)
            dve.tensor_tensor(kr[r, C:TC], kr[r, C:TC], mt1[r, :], ALU.add).then_inc(kr_step, 1)
            dve.wait_ge(kr_step, 3)
            dve.tensor_copy(kraw[1][r, :], kr[r, :]).then_inc(kr_step, 1)
            dve.wait_ge(kr_step, 4)

            def raw(i, e):
                b, n = e % 2, i * HB + e
                qr_, kr_ = qraw[b], kraw[b]
                dve.wait_ge(hq_sq, v(n + 1))
                if e >= 2:
                    dve.wait_ge(hq_ready, v(n))
                dve.tensor_scalar(qr_, HQ[b][:, :], col("q_gain"), None, ALU.mult)
                kg = col("k_gain", 0, slice(0, NOPE))
                dve.tensor_scalar(kr_[0:NOPE, C:TC], HK[b][0:NOPE, :], kg, None, ALU.mult)
                dve.tensor_scalar(kr_[0:NOPE, 0:C], HC[b][0:NOPE, :], kg, None, ALU.mult).then_inc(hq_raw, 1)
                dve.wait_ge(hq_raw, v(n + 1))
                dve.wait_ge(hq_step, v(n * 2 + 1))
                dve.tensor_tensor(mt1[r, :], qr_[r2, :], sinm[r2, :], ALU.mult)
                dve.tensor_tensor(qr_[r, :], qr_[r, :], cosm[r, :], ALU.mult).then_inc(hq_step, 1)
                dve.wait_ge(hq_step, v(n * 2 + 2))
                dve.tensor_tensor(qr_[r, :], qr_[r, :], mt1[r, :], ALU.add).then_inc(hq_step, 1)

            def norm(i, e):
                b, n = e % 2, i * HB + e
                dve.wait_ge(hq_rs, v(n + 1))
                if e == 0:
                    dve.wait_ge(pt_ready, v(i * UA + 2))
                dve.wait_ge(hq_step, v(n * 2 + 3))
                dve.tensor_tensor(qf[0:QK_A, e, :], qraw[b][0:QK_A, :], hrt[0:QK_A, 0:T], ALU.mult)
                dve.tensor_tensor(kf[0:QK_A, e, :], kraw[b][0:QK_A, :], hrt[0:QK_A, T:T + TC], ALU.mult).then_inc(hq_ready, 1)

            def body(i):
                a0 = i * UA
                dve.wait_ge(va_proj, v(i * 2 + 2))
                dve.wait_ge(pv_ready, v(a0 + CR))
                dve.tensor_copy(va[:, 2:6, :], pT[:, :].rearrange("p (a b) -> p a b", a=4)).then_inc(va_dve, 1)
                raw(i, 0)
                for e in range(1, HB):
                    raw(i, e)
                    norm(i, e - 1)
                norm(i, HB - 1)
                for step, k in unit_steps(UA):
                    e = k // TB
                    n = i * HB + e
                    if step == "M":
                        dve_M(dve, a0 + k, TC, QK_A ** -0.5)
                    elif step == "C":
                        dve_C(dve, a0 + k, TC)
                    elif step == "O":
                        t = k % TB
                        dve_O(dve, a0 + k, lambda a, r: dve.tensor_scalar(o_all[:, t, dyn(n, 64)], pO[:, e % 2 * 64:e % 2 * 64 + 64], r, None, ALU.mult
                                                                          ).then_inc(o_ready, 1))

            items(dve, HEADS_A // HB, 1, body)
            for m in range(KD):
                dve.wait_ge(o_hi, m + 1)
                bm = slice(m * T, (m + 1) * T)
                dve.tensor_tensor(b_lo[:, bm], pT[:, (m % 2) * 512:(m % 2) * 512 + 512], b_hi[:, bm].bitcast(F32), ALU.subtract).then_inc(o_lo, 1)

        hq_step, kr_sq, kr_step = sem("hq_step"), sem("kr_sq"), sem("kr_step")

        def pe_mla_in(pe):
            pe_first_chunks(pe, G_MLA[0], 2, normed("mla_lat"), H, T, T)
            pe_norm(pe, "mla_ctx", C)
            items(pe, 5, SLOTS, lambda m: pe_chunk(pe, m + G_MLA[0], H, T, T), 2)
            pe.wait_ge(nlo_ready, norm_done("mla_ctx"))
            items(pe, 3, SLOTS, lambda m: pe_chunk(pe, m + G_MLA[1], B, C, C))

        def act_mla_in(act):
            r = slice(NOPE, P)
            dsts = [cq[:, j, :] for j in range(4)] + [ckv[:, j, C:TC] for j in range(2)] + [kraw[0][r, C:TC]]
            for g0, n, ds_ in ((G_MLA[0], T, dsts), (G_MLA[1], C, [ckv[:, j, 0:C] for j in range(2)] + [kraw[0][r, 0:C]])):
                for j, dst in enumerate(ds_):
                    act_hi_part(act, g0 + j + 2)
                    act.wait_ge(chunk_done, done(g0 + j))
                    rows_ = r if j == len(ds_) - 1 else slice(0, P)
                    act.activation(dst, bank[(g0 + j) % SLOTS][rows_, 0:n], ACT.Copy).then_inc(evac[(g0 + j) % SLOTS], 1)

        def dve_permute(dve):
            for kt in range(KD):
                dve.wait_ge(perm_a, kt + 1)
                dve.tensor_copy(x[:, kt, :], nt[:, kt % 3, :]).then_inc(perm_b, 1)

        def act_permute(act):
            act.wait_ge(*ev(g_ffn_end(2)))
            for kt in range(KD):
                if kt >= 3:
                    act.wait_ge(perm_b, kt - 2)
                act.activation(nt[:, kt % 3, :].rearrange("p (j t) -> p j t", j=TB),
                               x[:, kt, :].rearrange("p (t j) -> p j t", j=TB), ACT.Copy).then_inc(perm_a, 1)

        A_MLA = HEADS_A * TB
        UB = 2 * TB

        def a_diff(l):
            return A_MLA + l * (HEADS_D + 4) * UB

        def a_dil(l):
            return a_diff(l) + HEADS_D * UB

        R_DIFF, R_DIL = 2, 6

        def r_diff(l):
            return l * (HEADS_D * R_DIFF + 4 * R_DIL)

        def r_dil(l):
            return r_diff(l) + HEADS_D * R_DIFF

        def act_qs(act, g, r, par):
            act.wait_ge(chunk_done, done(g))
            act.wait_ge(rope_done, v(r + 1))
            act.activation(qs[:, par, :], bank[g % SLOTS][:, :], ACT.Copy).then_inc(evac[g % SLOTS], 1)

        def dve_zeros(dve):
            dve.memset(qz[0][64:P, :, :], 0.0)
            dve.memset(qz[1][0:64, :, :], 0.0).then_inc(zeroed, 1)

        zeroed = sem("zeroed")

        def dve_rope(dve, g, r, par, dsts):
            dve.wait_ge(*ev(g))
            dve.wait_ge(rope_done, v(r + 2))
            for q in range(0, P, 64):
                for a, b in ((q, q + 32), (q + 32, q)):
                    dve.tensor_tensor(t1[a:a + 32, :], qs[b:b + 32, par, :], sin2[b:b + 32, :], ALU.mult)
            for p, dst in dsts:
                last = dve.tensor_tensor(dst, qs[p, par, :], cos2[p, :], ALU.mult)
            last.then_inc(rope_step, 1)
            dve.wait_ge(rope_step, v(r + 1))
            for p, dst in dsts:
                last = dve.tensor_tensor(dst, dst, t1[p, :], ALU.add)
            last.then_inc(rope_done, 1)

        rope_step = sem("rope_step")

        def halves(c):
            return slice(c * 64, c * 64 + 64)

        def turn_gs(g0, i, groups):
            g = i * (3 * groups) + g0
            return [g + c for c in range(2 * groups)], [g + (2 * groups + gi) for gi in range(groups)]

        TURNS = 4

        def turns(eng, body, finish):
            body(Lin(None, 0, 0), False)
            with eng.Fori(1, TURNS) as i:
                body(Lin(i, 1, 0), True)
            finish(Lin(None, 0, TURNS - 1))

        def pe_pairs(pe, l, groups, g0, a00, r00):
            def finish(i):
                if groups == 1:
                    pe.wait_ge(o_scaled, v(i + (l * HEADS_D + 1)))
                else:
                    pe.wait_ge(o_ready, v(i * UB + (a00 + UB + 2)))
                pe.wait_ge(ptc_act, v(i * UB + (a00 + UB + 1)))
                pe.wait_ge(ptc_dve, v(i * UB + (a00 + UB + 1)))
                for t in range(TB):
                    last = pe.transpose(pT[:, t * P:(t + 1) * P], od[:, t, :], ident)
                last.then_inc(o_turned, 1)

            def body(i, later):
                qk, vs = turn_gs(g0, i, groups)

                def turn_values(gi):
                    pe.wait_ge(*ev(vs[gi]))
                    if gi:
                        pe.wait_ge(v_copied, v(i * groups + (v_base(l, groups) + gi)))
                    else:
                        pe.wait_ge(o_ready, v(i * UB + (a00 + 2)))
                    for t in range(TB):
                        last = pe.transpose(pO[:, t * P:(t + 1) * P], vfm[:, gi % 2, t * P:(t + 1) * P], ident)
                    last.then_inc(v_turned, 1)

                def scores(k):
                    t, c = k // 2, k % 2
                    tok = slice(t * P, (t + 1) * P)
                    ops = [(qz[c][:, 0, tok], kr[:, 0, :], 0, T)]
                    for gi in range(1, groups):
                        ops.append((qz[c][:, gi, tok], kr[:, gi, tok], T + (gi - 1) * P, T + gi * P))
                    pe_S(pe, i * UB + (a00 + k), ops)

                for j, g in enumerate(qk):
                    pe_chunk(pe, g, H, T, T)
                    if j == 1 and later:
                        finish(i - 1)
                for gi, g in enumerate(vs):
                    if gi == 2:
                        pe.wait_ge(rope_done, v(i * (2 * groups) + (r00 + 2 * groups + 2)))
                        scores(0)
                    pe_chunk(pe, g, H, T, T)
                    if gi:
                        turn_values(gi - 1)
                if groups == 1:
                    pe.wait_ge(rope_done, v(i * (2 * groups) + (r00 + 2 * groups + 2)))
                    scores(0)
                turn_values(groups - 1)
                scores(1)
                pe.wait_ge(v_copied, v(i * groups + (v_base(l, groups) + groups)))
                pe.wait_ge(o_lo, v(i + o_base(l, groups)))
                nk = KEYS_DIL if groups == 3 else T
                for step, k in unit_steps(UB, False):
                    a = i * UB + (a00 + k)
                    t, c = k // 2, k % 2
                    if step == "S":
                        scores(k)
                    elif step == "T":
                        pe_T(pe, a, nk)
                    elif step == "PV":
                        if groups == 1:
                            pe_PV(pe, a, [vt[:, 0, kt, :] for kt in range(TB)], P)
                        else:
                            pe_PV(pe, a, [vt[:, 0, kt, :] for kt in range(TB)] + [vt[:, gi, t, :] for gi in (1, 2)], P)

            turns(pe, body, finish)

        def o_base(l, groups):
            return KD + l * (HEADS_D + 4) + (HEADS_D if groups == 3 else 0)

        def v_base(l, groups):
            return l * (HEADS_D + 3 * 4) + (HEADS_D if groups == 3 else 0)

        def act_pairs(act, l, groups, g0, a00, r00):
            nk = KEYS_DIL if groups == 3 else T
            ob = o_base(l, groups)

            def finish(i):
                if groups == 1:
                    act.wait_ge(o_val, v(i + (l * HEADS_D + 1)))
                    act.activation(b_hi[:, dyn(i, T)], of, ACT.Copy).then_inc(o_hi, 1)
                else:
                    act.wait_ge(o_turned, v(i + (ob + 1)))
                    act.activation(b_hi[:, dyn(i, T, 4 * T)], pT[:, 0:T], ACT.Copy).then_inc(o_hi, 1)

            def body(i, later):
                qk, vs = turn_gs(g0, i, groups)

                def copy_values(gi):
                    act.wait_ge(v_turned, v(i * groups + (v_base(l, groups) + gi + 1)))
                    act.wait_ge(pv_ready, v(i * UB + (a00 + CR)))
                    act.activation(vt[:, gi, :, :], pO[:, :].rearrange("p (a b) -> p a b", b=P), ACT.Copy).then_inc(v_copied, 1)

                def exps(k):
                    act_E(act, i * UB + (a00 + k), nk, 64 ** -0.5, groups == 3)

                for j, g in enumerate(qk):
                    act_hi_part(act, g + 2)
                    act_qs(act, g, i * (2 * groups) + (r00 + j), j % 2)
                    if j == 1 and later:
                        finish(i - 1)
                for gi, g in enumerate(vs):
                    act_hi_part(act, g + 2)
                    act.wait_ge(chunk_done, done(g))
                    act.activation(vfm[:, gi % 2, :], bank[g % SLOTS][:, :], ACT.Copy).then_inc(evac[g % SLOTS], 1)
                    if gi == 2:
                        exps(0)
                    if gi:
                        copy_values(gi - 1)
                copy_values(groups - 1)
                if groups == 1:
                    exps(0)
                exps(1)
                for step, k in unit_steps(UB, False):
                    if step == "E":
                        exps(k)
                    elif step == "C":
                        act_C(act, i * UB + (a00 + k), nk)
                if groups == 1:
                    act.wait_ge(o_ready, v(i * UB + (a00 + UB + 2)))
                    for t in range(TB):
                        last = act.activation(attP[:, 0, t * P:(t + 1) * P], od[:, t, :], ACT.Square, accum_out=oss[:, t:t + 1])
                    last.then_inc(o_sq, 1)
                    act.wait_ge(o_sq, v(i * 3 + (l * 3 * HEADS_D + 1)))
                    act.activation(oss, oss, ACT.Ln, bias=SUBLN_EPS, scale=1.0 / P).then_inc(o_sq, 1)
                    act.wait_ge(o_sq, v(i * 3 + (l * 3 * HEADS_D + 2)))
                    act.activation(orss, oss, ACT.Exp, scale=-0.5).then_inc(o_sq, 1)

            turns(act, body, finish)

        def dve_pairs(dve, l, groups, g0, a00, r00):
            nk = KEYS_DIL if groups == 3 else T
            ob = o_base(l, groups)

            def finish(i):
                if groups == 1:
                    dve.wait_ge(o_turned, v(i + (ob + 1)))
                    dve.wait_ge(o_lo, v(i + ob))
                    dve.tensor_scalar(of, pT[:, 0:T], col("subln", l), 1.0 - lambda_init(l), ALU.mult, ALU.mult).then_inc(o_val, 1)
                    dve.wait_ge(o_hi, v(i + (ob + 1)))
                    dve.tensor_tensor(b_lo[:, dyn(i, T)], of, b_hi[:, dyn(i, T)].bitcast(F32), ALU.subtract).then_inc(o_lo, 1)
                else:
                    dve.wait_ge(o_hi, v(i + (ob + 1)))
                    o = dyn(i, T, 4 * T)
                    dve.tensor_tensor(b_lo[:, o], pT[:, 0:T], b_hi[:, o].bitcast(F32), ALU.subtract).then_inc(o_lo, 1)

            def body(i, later):
                qk, _ = turn_gs(g0, i, groups)

                def maxima(k):
                    dve_M(dve, i * UB + (a00 + k), nk, 64 ** -0.5, masks[:, k // 2, :] if groups == 3 else None)

                for j, g in enumerate(qk):
                    dve_rope(dve, g, i * (2 * groups) + (r00 + j), j % 2,
                             [(halves(c), qz[c][halves(c), j // 2, :]) for c in range(2)] if j % 2 == 0 else [(slice(0, P), kr[:, j // 2, :])])
                    if j == 1 and later:
                        finish(i - 1)
                maxima(0)
                maxima(1)
                for step, k in unit_steps(UB, False):
                    a = i * UB + (a00 + k)
                    t, c = k // 2, k % 2
                    if step == "M":
                        maxima(k)
                    elif step == "C":
                        dve_C(dve, a, nk)
                    elif step == "O":
                        def store(a, r):
                            if groups == 3:
                                dve.tensor_scalar(od[:, t, halves(c)], pO[:, halves(c)], r, None, ALU.mult).then_inc(o_ready, 1)
                            elif c == 0:
                                dve.tensor_scalar(od[:, t, :], pO[:, 0:P], r, None, ALU.mult).then_inc(o_ready, 1)
                            else:
                                dve.tensor_scalar(lam_r, r, neg_lam[:, l:l + 1], None, ALU.mult).then_inc(lam_step, 1)
                                dve.wait_ge(lam_step, v(i * TB + (l * TB * HEADS_D + t + 1)))
                                dve.wait_ge(o_ready, v(a + 2))
                                dve.scalar_tensor_tensor(od[:, t, :], pO[:, 0:P], lam_r, od[:, t, :], ALU.mult, ALU.add).then_inc(o_ready, 1)
                        dve_O(dve, a, store)
                if groups == 1:
                    dve.wait_ge(o_sq, v(i * 3 + (l * 3 * HEADS_D + 3)))
                    for t in range(TB):
                        last = dve.tensor_scalar(od[:, t, :], od[:, t, :], orss[:, t:t + 1], None, ALU.mult)
                    last.then_inc(o_scaled, 1)

            if groups == 1:
                dve_zeros(dve)
                dve.wait_ge(zeroed, l + 1)
            turns(dve, body, finish)

        lam_step = sem("lam_step")

        def lambda_init(l):
            return 0.8 - 0.6 * float(np.exp(-0.3 * l))

        def pe_merge(pe, l):
            pe.wait_ge(o_lo, KD + (l + 1) * 8)

            def body(m):
                g = m * 3 + G_MERGE[l]
                pe_chunk(pe, g, H, T, T)
                pe_chunk(pe, g + 1, H, T, T)
                s = (g + 2) % SLOTS
                pe_wait_chunk(pe, g + 2)
                pe_three(pe, bank[s][:, :], [(wt(s, kt), rows(*B, T, kt, 0, T)) for kt in range(4)])
                pe_three(pe, pO[:, :], [(wt(s, kt), rows(*B, T, kt, 0, T)) for kt in range(4, 8)]).then_inc(chunk_done, 1)

            items(pe, KD, 1, body)

        def act_merge(act, l):
            def body(m):
                g = m * 3 + G_MERGE[l]
                act.wait_ge(*ev(g - 1))
                for c in range(2):
                    act_hi_part(act, g + (c + 2))
                    act.wait_ge(chunk_done, done(g + c))
                    act.activation(sg[:, c, :], bank[(g + c) % SLOTS][:, :], ACT.Sigmoid).then_inc(evac[(g + c) % SLOTS], 1)
                act_hi_part(act, g + 4)

            items(act, KD, 1, body)
            act.wait_ge(chunk_done, done(G_MERGE[l] + 3 * KD - 1))
            for m in range(KD):
                act.wait_ge(merged, l * KD + m + 2)
                act.activation(h_hi[:, m * T:(m + 1) * T], f[:, m, :], ACT.Copy).then_inc(m_hi, 1)

        def dve_merge(dve, l):
            def body(m):
                g = m * 3 + G_MERGE[l]
                s = (g + 2) % SLOTS
                dve.wait_ge(*ev(g + 1))
                dve.wait_ge(chunk_done, done(g + 2))
                dve.wait_ge(merged, v(m + (l * KD + 1)))
                dve.tensor_tensor(tm[:, 0, :], bank[s][:, :], sg[:, 0, :], ALU.mult)
                dve.tensor_tensor(tm[:, 1, :], pO[:, :], sg[:, 1, :], ALU.mult).then_inc(evac[s], 1)
                dve.wait_ge(*ev(g + 2))
                fm = f[:, dyn(m, 1), :].rearrange("p a b -> p (a b)")
                dve.tensor_tensor(fm, tm[:, 0, :], tm[:, 1, :], ALU.add).then_inc(merged, 1)

            items(dve, KD, 1, body)
            for m in range(KD):
                dve.wait_ge(m_hi, l * KD + m + 1)
                o = slice(m * T, (m + 1) * T)
                dve.tensor_tensor(h_lo[:, o], f[:, m, :], h_hi[:, o].bitcast(F32), ALU.subtract).then_inc(m_lo, 1)

        def dve_wout(dve, l):
            def body(m):
                dve.wait_ge(chunk_done, done(m + G_OUT[l]))
                dve.tensor_copy(f[:, dyn(m, 1), :].rearrange("p a b -> p (a b)"), bank[(m + G_OUT[l]) % SLOTS][:, :]).then_inc(evac[(m + G_OUT[l]) % SLOTS], 1)
            items(dve, KD, SLOTS, body)

        def dve_post(dve, name, l, gain, before):
            c = NORMS.index(name)
            dve.wait_ge(rstd_ready, c + 1)
            for kt in range(KD + 1):
                if kt < KD:
                    if kt >= 3:
                        dve.wait_ge(x_ready, before * KD + kt - 2)
                    dve.scalar_tensor_tensor(nt[:, kt % 3, :], f[:, kt, :], col(gain, l * KD + kt), rstd, ALU.mult, ALU.mult
                                             ).then_inc(nt_ready, 1)
                if kt >= 1:
                    k = kt - 1
                    dve.wait_ge(nt_ready, N_BASE[c] + k + 1)
                    dve.tensor_tensor(x[:, k, :], x[:, k, :], nt[:, k % 3, :], ALU.add).then_inc(x_ready, 1)

        def tile_of(t_, n=T):
            return lambda kt: t_[:, kt, 0:n]

        def gains(name, l):
            return lambda kt: col(name, l * KD + kt)

        block = ctx.enter_context(nc.Block())
        r_mlstm = G_ABOUT[0] // SLOTS + 1

        @block.sync
        def _(sp):
            for dst, src in ((pc[:, :], pcol), (cm[:, :], cmat), (x[:, :, :], xT), (xc[:, :, :], cT),
                             (cond_sb[:, :], cond), (wg_raw, wgate), (lam_in, lam)):
                sp.dma_start(dst, src).then_inc(consts_in, 16)

            def load(r, s):
                sp.wait_ge(lo_ready, r * SLOTS + (s + 1 - SLOTS))
                sp.dma_start(w_raw[:, s, :], stream[r * SLOTS + s]).then_inc(raw_full[s], 16)

            for g in range(SLOTS):
                sp.dma_start(w_raw[:, g, :], stream[g]).then_inc(raw_full[g], 16)
            for k in range(ADA_FIRST):
                sp.dma_start(ada_place(k), ada[k]).then_inc(ada_first[k], 16)
            with sp.Fori(1, r_mlstm) as r:
                for s in range(SLOTS):
                    load(r, s)
            sp.wait_ge(gates_sum, 1)
            for s in range(SLOTS):
                sp.dma_start(spare[s], ada[ADA_FIRST + s]).then_inc(ada_in[s], 16)
            turns = (n_ada - ADA_FIRST) // SLOTS
            with sp.Fori(1, turns) as r:
                for s in range(SLOTS):
                    sp.wait_ge(ada_used, r * SLOTS + (ADA_FIRST + s - SLOTS + 1))
                    sp.dma_start(spare[s], ada[r * SLOTS + (ADA_FIRST + s)]).then_inc(ada_in[s], 16)
            for k in range(ADA_FIRST + turns * SLOTS, n_ada):
                s = (k - ADA_FIRST) % SLOTS
                sp.wait_ge(ada_used, k - SLOTS + 1)
                sp.dma_start(spare[s], ada[k]).then_inc(ada_in[s], 16)
            with sp.Fori(r_mlstm, G_ALL // SLOTS) as r:
                for s in range(SLOTS):
                    load(r, s)
            for g in range(G_ALL // SLOTS * SLOTS, G_ALL):
                sp.wait_ge(lo_ready, g - SLOTS + 1)
                sp.dma_start(w_raw[:, g % SLOTS, :], stream[g]).then_inc(raw_full[g % SLOTS], 16)
            for kt in range(KD):
                sp.wait_ge(x_ready, (2 * LAYERS - 1) * KD + kt + 1)
                sp.dma_start(out[:, kt, :], x[:, kt, :]).then_inc(stored, 16)
            sp.wait_ge(stored, 16 * KD)

        @block.gpsimd
        def _(pool):
            def lo_part(g, s):
                pool.wait_ge(hi_ready, g + 1)
                pool.tensor_tensor(w_lo[:, s, :], w_raw[:, s, :], w_hi[:, s, :].bitcast(F32), ALU.subtract
                                   ).then_inc(lo_ready, 1)

            with pool.Fori(0, r_mlstm) as r:
                for s in range(SLOTS):
                    lo_part(r * SLOTS + s, s)
            pool.wait_ge(padded, 1)
            pool.wait_ge(*ev(G_GLU[1] + 7))
            pool.wait_ge(gates_sum, 1)
            pool_conv(pool)
            with pool.Fori(r_mlstm, G_ALL // SLOTS) as r:
                for s in range(SLOTS):
                    lo_part(r * SLOTS + s, s)
            for g in range(G_ALL // SLOTS * SLOTS, G_ALL):
                lo_part(g, g % SLOTS)
        @block.tensor
        def _(pe):
            pe.sem_inc(chunk_done, SLOTS)
            pe.sem_inc(pt_ready, 2)
            pe.sem_inc(pv_ready, CR)
            pe.wait_ge(consts_in, 112)
            pe.wait_ge(silu_done, 1)

            pe_norm(pe, "mix_lat", T)
            for k in range(ADA_FIRST):
                pe_ada(pe, k)
                if k % 2 and k > 1:
                    pe_ada_turn(pe, k // 2 - 1)
            pe_ada_turn(pe, ADA_FIRST // 2 - 1)
            pe_first_chunks(pe, G_GLU[0], 2, normed("mix_lat"), H, T, T)
            pe_norm(pe, "mix_ctx", C)
            pe_glu(pe, 0, 2)
            pe.wait_ge(nlo_ready, norm_done("mix_ctx"))
            pe_glu(pe, 1)
            pe_qkvo(pe, 0)
            pe_qkvo(pe, 1)
            pe_mlstm(pe)
            pe_ln(pe, 0, "ln_lat")
            pe_ln(pe, 1, "ln_ctx")
            pe.wait_ge(hs_lo, 2 * HEADS_M)
            pe.wait_ge(mod_ready, 2)
            pe.wait_ge(nlo_ready, norm_done("ln_lat"))
            pe_out(pe, G_ABOUT[0], H, T, T)
            pe.wait_ge(nlo_ready, norm_done("ln_ctx"))
            pe_out(pe, G_ABOUT[1], B, C, C)
            pe_norm(pe, "ffn_lat", T)
            pe_ffn(pe, 0, "ffn_lat", T, T)
            pe_norm(pe, "ffn_ctx", C)
            pe_ffn(pe, 1, "ffn_ctx", C, C)
            pe_norm(pe, "mla_lat", T)
            pe_mla_in(pe)
            pe_norm(pe, "cq", T)
            pe_norm(pe, "ckv_ctx", C)
            pe_norm(pe, "ckv_lat", T)
            pe_mla_heads(pe)
            pe_out(pe, G_MLAOUT, B, T, T, ready=lambda kt: (o_lo, kt + 1))
            pe_norm(pe, "mla_ffn", T)
            pe_ffn(pe, 2, "mla_ffn", T, T)
            for l in range(LAYERS):
                pe_norm(pe, f"mixpre{l}", T)
                pe.wait_ge(nlo_ready, norm_done(f"mixpre{l}"))
                pe.wait_ge(rope_in, 32 + 48)
                pe_pairs(pe, l, 1, G_DIFF[l], a_diff(l), r_diff(l))
                pe_pairs(pe, l, 3, G_DIL[l], a_dil(l), r_dil(l))
                pe_merge(pe, l)
                pe_out(pe, G_OUT[l], H, T, T, ready=lambda kt: (m_lo, l * KD + kt + 1))
                pe_norm(pe, f"mixpost{l}", T)
                pe_norm(pe, f"ffnpre{l}", T)
                pe_ffn(pe, 3 + l, f"ffnpre{l}", T, T)
                pe_norm(pe, f"ffnpost{l}", T)

        @block.scalar
        def _(act):
            act.sem_inc(ptc_act, 1)
            act.sem_inc(e_ready, 2)
            act.wait_ge(consts_in, 112)
            act.activation(small[:, 484:500], cond_sb[:, :], ACT.Silu).then_inc(silu_done, 1)
            act.activation(wg_hi[:, :], wg_raw, ACT.Copy).then_inc(gate_w_hi, 1)
            act_hi_part(act, 0)
            act_hi_part(act, 1)
            xt, xct = tile_of(x), tile_of(xc, C)
            act_norm(act, "mix_lat", xt, T, T, None, lambda kt: modc(0, 0, kt, 0), (*H, 0))
            act_norm(act, "mix_ctx", xct, C, C, None, lambda kt: modc(0, 0, kt, 1), (*B, 0))
            act_glu(act, 0)
            act_glu(act, 1)
            act_qkvo(act, 0)
            act_qkvo(act, 1)
            act_mlstm(act)
            act_ln(act, 0, "ln_lat", H, T)
            act_ln(act, 1, "ln_ctx", B, C)
            act_out(act, G_ABOUT[0])
            act_out(act, G_ABOUT[1])
            act_norm(act, "ffn_lat", xt, T, T, ev(G_ABOUT[0] + KD - 1), lambda kt: modc(0, 3, kt, 0), (*H, 0),
                     done(G_ABOUT[0] + KD - 1))
            act.wait_ge(padded, 2)
            act.wait_ge(chunk_done, done(G_ABOUT[1] + KD - 1))
            act_ffn(act, 0, T, True)
            act_norm(act, "ffn_ctx", xct, C, C, ev(G_ABOUT[1] + KD - 1), lambda kt: modc(0, 3, kt, 1), (*H, 0),
                     done(g_ffn_end(0)))
            act.wait_ge(padded, 3)
            act_ffn(act, 1, C, True)
            act.dma_start(cosm, trope[0]).then_inc(rope_in, 16)
            act.dma_start(sinm, trope[1]).then_inc(rope_in, 16)
            act_norm(act, "mla_lat", xt, T, T, ev(g_ffn_end(0)), lambda kt: modc(1, 0, kt, 0), (*H, 0), done(g_ffn_end(1)))
            act_norm(act, "mla_ctx", xct, C, C, ev(g_ffn_end(1)), lambda kt: modc(1, 0, kt, 1), (*B, 0), done(g_ffn_end(1)))
            act_mla_in(act)
            act_norm(act, "cq", tile_of(cq), T, T, ev(G_MLA[1] + 2), None, (*B, KD * T // 2), done(G_MLA[1] + 2))
            act_norm(act, "ckv_ctx", tile_of(ckv, C), C, TC, None, None, (*H, 0))
            act_norm(act, "ckv_lat", lambda kt: ckv[:, kt, C:TC], T, TC, None, None, (*H, C))
            act_mla_heads(act)
            act.wait_ge(o_turned, KD)
            for dst, src in ((masks, bmask), (cos2, brope[0]), (sin2, brope[1])):
                act.dma_start(dst, src).then_inc(rope_in, 16)
            act_out(act, G_MLAOUT, SLOTS)
            act_norm(act, "mla_ffn", xt, T, T, ev(G_MLAOUT + KD - 1), lambda kt: modc(1, 3, kt, 0), (*H, 0),
                     done(G_MLAOUT + KD - 1))
            act.wait_ge(padded, 4)
            act_ffn(act, 2, T, True)
            act_permute(act)
            act.wait_ge(lam_sums, 2 * LAYERS)
            act.activation(lam_s, lam_s, ACT.Exp).then_inc(lam_exp, 1)
            act.wait_ge(perm_b, KD)
            ft = tile_of(f)
            for l in range(LAYERS):
                act_norm(act, f"mixpre{l}", xt, T, T, (x_ready, 2 * l * KD) if l else None, None, (*H, 0), done(G_DIFF[l] - 1))
                act_pairs(act, l, 1, G_DIFF[l], a_diff(l), r_diff(l))
                act_pairs(act, l, 3, G_DIL[l], a_dil(l), r_dil(l))
                act_merge(act, l)
                act_out(act, G_OUT[l])
                act_norm(act, f"mixpost{l}", ft, T, T, ev(G_OUT[l] + KD - 1))
                act_norm(act, f"ffnpre{l}", xt, T, T, (x_ready, (2 * l + 1) * KD), None, (*H, 0), done(G_OUT[l] + KD - 1))
                act_ffn(act, 3 + l, T, False)
                act_norm(act, f"ffnpost{l}", ft, T, T, ev(g_ffn_end(3 + l)))

        @block.vector
        def _(dve):
            for b in range(SLOTS):
                dve.sem_inc(evac[b], 1)
            dve.sem_inc(conv_ready, SLOTS)
            dve.sem_inc(act_lo, SLOTS)
            dve.sem_inc(merged, 1)
            dve.sem_inc(ptc_dve, 1)
            dve.sem_inc(o_ready, 2)
            dve.sem_inc(hq_ready, 1)
            dve.sem_inc(hq_step, 1)
            dve.sem_inc(rope_done, 2)
            link = link_on(dve_link)
            dve.wait_ge(consts_in, 112)
            dve.wait_ge(gate_w_hi, 1)
            dve.tensor_tensor(wg_lo[:, :], wg_raw, wg_hi[:, :].bitcast(F32), ALU.subtract).then_inc(gate_w_lo, 1)
            for l in range(LAYERS):
                for e in range(2):
                    o = l * 256 + e * 128
                    dve.tensor_tensor_reduce(lam_junk[:, :], lam_in[:, o:o + 64], lam_in[:, o + 64:o + 128], 1.0, 0.0, ALU.mult, ALU.add,
                                             lam_s[:, 2 * l + e:2 * l + e + 1]).then_inc(lam_sums, 1)
                    dve.wait_ge(lam_sums, 2 * l + e + 1)
            for g in range(ADA_FIRST // 2):
                dve_ada(dve, g)
            dve_mod(dve, link, 0, ADA_FIRST // 2, 1)
            for s in range(2):
                dve.memset(up[s][:, :, 0:PADW], 0.0)
                dve.memset(up[s][:, :, PADW + NTOK[s]:2 * PADW + NTOK[s]], 0.0)
            dve.memset(vm.rearrange("p a (h e) -> p (a h) e", e=V_M + 1)[:, :, V_M:V_M + 1], 1.0).then_inc(padded, 1)
            dve.wait_ge(padded, 1)
            xt, xct = tile_of(x), tile_of(xc, C)

            def mods(l, part, s):
                return lambda kt: modc(l, part, kt, s)

            def pad_gates(n, count):
                dve.memset(gpad[:, :, 0:1], 0.0)
                dve.memset(gpad[:, :, n + 1:n + 2], 0.0).then_inc(padded, 1)
                dve.wait_ge(padded, count)

            dve_norm(dve, "mix_lat", xt, T, T, mods(0, 1, 0), mods(0, 0, 0), (*H, 0))
            dve_norm(dve, "mix_ctx", xct, C, C, mods(0, 1, 1), mods(0, 0, 1), (*B, 0))
            dve_glu(dve, 0)
            dve_glu(dve, 1)
            dve.wait_ge(*ev(G_GLU[1] + 7))
            dve_conv(dve)
            dve_mlstm(dve, link)
            dve_mod(dve, link, ADA_FIRST // 2, n_ada // 2, 2)
            dve_ln(dve, 0, "ln_lat", H, T)
            dve_ln(dve, 1, "ln_ctx", B, C)
            dve_out_residual(dve, G_ABOUT[0], x, T, 0, 2, 0)
            dve_out_residual(dve, G_ABOUT[1], xc, C, 0, 2, 1)
            dve_norm(dve, "ffn_lat", xt, T, T, mods(0, 4, 0), mods(0, 3, 0), (*H, 0))
            pad_gates(T, 2)
            dve_ffn(dve, 0, T, True, 0, residual_body(dve, x, T, 0, 0))
            dve_norm(dve, "ffn_ctx", xct, C, C, mods(0, 4, 1), mods(0, 3, 1), (*H, 0))
            pad_gates(C, 3)
            dve_ffn(dve, 1, C, True, 0, residual_body(dve, xc, C, 0, 1))
            dve_norm(dve, "mla_lat", xt, T, T, mods(1, 1, 0), mods(1, 0, 0), (*H, 0))
            dve_norm(dve, "mla_ctx", xct, C, C, mods(1, 1, 1), mods(1, 0, 1), (*B, 0))
            dve_norm(dve, "cq", tile_of(cq), T, T, lambda kt: col("q_norm", kt), None, (*B, KD * T // 2))
            dve_norm(dve, "ckv_ctx", tile_of(ckv, C), C, TC, lambda kt: col("kv_norm", kt), None, (*H, 0))
            dve_norm(dve, "ckv_lat", lambda kt: ckv[:, kt, C:TC], T, TC, lambda kt: col("kv_norm", kt), None, (*H, C))
            dve.wait_ge(rope_in, 32)
            dve_mla_heads(dve)
            dve_out_residual(dve, G_MLAOUT, x, T, 1, 2, 0)
            dve_norm(dve, "mla_ffn", xt, T, T, mods(1, 4, 0), mods(1, 3, 0), (*H, 0))
            pad_gates(T, 4)
            dve_ffn(dve, 2, T, True, 1, residual_body(dve, x, T, 1, 0))
            dve_permute(dve)
            dve.wait_ge(lam_exp, 1)
            for l in range(LAYERS):
                nl = neg_lam[:, l:l + 1]
                link(dve, dve.tensor_tensor(nl, lam_s[:, 2 * l + 1:2 * l + 2], lam_s[:, 2 * l:2 * l + 1], ALU.subtract))
                link(dve, dve.tensor_scalar(nl, nl, lambda_init(l), None, ALU.subtract))
            dve.wait_ge(rope_in, 32 + 48)
            for l in range(LAYERS):
                dve_norm(dve, f"mixpre{l}", xt, T, T, gains("mix_pre", l), None, (*H, 0))
                dve_pairs(dve, l, 1, G_DIFF[l], a_diff(l), r_diff(l))
                dve_pairs(dve, l, 3, G_DIL[l], a_dil(l), r_dil(l))
                dve_merge(dve, l)
                dve_wout(dve, l)
                dve_post(dve, f"mixpost{l}", l, "mix_post", 2 * l)
                dve_norm(dve, f"ffnpre{l}", xt, T, T, gains("ffn_pre", l), None, (*H, 0))
                dve_ffn(dve, 3 + l, T, False, None, f_body(dve))
                dve_post(dve, f"ffnpost{l}", l, "ffn_post", 2 * l + 1)


def chunk(w, cols=P):
    k, n = w.shape
    c = np.zeros((P, KD, P), w.dtype)
    c[:, :k // P, :n] = w.reshape(k // P, P, n).transpose(1, 0, 2)
    return c.reshape(P, KD * P)


def columns(w):
    return [chunk(w[:, i:i + P]) for i in range(0, w.shape[1], P)]


def ffn_chunks(w_in, w_out):
    hidden = w_in.shape[1] // 2
    out = []
    for j0, nj in PIECES:
        for j in range(j0, j0 + nj):
            out.append(chunk(w_in[:, j * P:(j + 1) * P]))
            out.append(chunk(w_in[:, hidden + j * P:hidden + (j + 1) * P]))
        out += columns(w_out[j0 * P:(j0 + nj) * P])
    return out


PARTNER = np.arange(ROPE) ^ 1
WITH_PARTNERS = np.concatenate([np.arange(QK_A), NOPE + PARTNER])


def weight_stream(a):
    out = []
    w = a["ab_w_in"][0]
    glu = []
    for j in range(CT):
        glu += [chunk(w[:, 512 + j * P:512 + (j + 1) * P]), chunk(w[:, j * P:(j + 1) * P])]
    qkvo = columns(w[:, 1024:1024 + 12 * P])
    out += glu + glu + qkvo + qkvo
    out += columns(a["ab_w_out"][0]) * 2
    out += ffn_chunks(a["ffn_w_in"][0], a["ffn_w_out"][0]) * 2
    w = a["mla_w_in"][0]
    rope = np.zeros((D, P), w.dtype)
    rope[:, NOPE:QK_A] = w[:, 768:800]
    rope[:, QK_A:] = w[:, 768:800][:, PARTNER]
    out += columns(w[:, :512])
    kv = columns(w[:, 512:768]) + [chunk(rope)]
    out += kv + kv
    uq, ukv = a["mla_w_uq"][0], a["mla_w_ukv"][0]
    for h0 in range(0, HEADS_A, 4):
        for h in (h0, h0 + 2):
            pair = np.zeros((P, KD, P), uq.dtype)
            for e in range(2):
                pair[:, e * 4:e * 4 + 4] = uq[:, (h + e) * QK_A + WITH_PARTNERS].reshape(4, P, P).transpose(1, 0, 2)
            out.append(pair.reshape(P, KD * P))
        out.append(np.concatenate([ukv[:, h * P:(h + 1) * P].reshape(2, P, P).transpose(1, 0, 2) for h in range(h0, h0 + 4)], 1
                                  ).reshape(P, KD * P))
    out += columns(a["mla_w_out"][0])
    out += ffn_chunks(a["ffn_w_in"][1], a["ffn_w_out"][1])
    for l in range(LAYERS):
        w = a["w_in_2"][l]
        at = lambda part, j: chunk(w[:, part * 512 + j * P:part * 512 + (j + 1) * P])
        for j in range(HEADS_D):
            out += [at(0, j), at(1, j), at(2, j)]
        for j in range(4):
            out += [at(3 + 3 * gi + c, j) for gi in range(3) for c in range(2)] + [at(3 + 3 * gi + 2, j) for gi in range(3)]
        for m in range(KD):
            cs = slice(m * P, (m + 1) * P)
            gates = w[:, 12 * 512:]
            out += [chunk(gates[:, cs]), chunk(gates[:, D:][:, cs]), chunk(np.concatenate([a["w_a_2"][l][:, cs], a["w_b_2"][l][:, cs]], 0))]
        out += columns(a["w_out_2"][l])
        out += ffn_chunks(a["w_gate_up_2"][l], a["w_down_2"][l])
    assert len(out) == G_ALL
    return np.stack(out)


def feature_columns(a):
    p = np.zeros((P, N_PCOL), np.float32)

    def put(name, w):
        p[:, _cols[name]:_cols[name] + w.shape[1]] = w

    def cols_of(w):
        return w.reshape(-1, P).T

    put("ada_b", cols_of(a["ada_b"]))
    put("conv_w", a["ab_conv_w"][0].reshape(TAPS, CT, P).transpose(2, 1, 0).reshape(P, CT * TAPS))
    for n, k in (("conv_b", "ab_conv_b"), ("ln_g", "ab_ln_g"), ("ln_b", "ab_ln_b"), ("head_gain", "ab_head_gain"),
                 ("q_norm", "mla_q_norm"), ("kv_norm", "mla_kv_norm")):
        put(n, cols_of(a[k][0]))
    p[:, _cols["q_gain"]] = a["mla_q_gain"][0][WITH_PARTNERS]
    p[:, _cols["k_gain"]] = a["mla_k_gain"][0][WITH_PARTNERS]
    put("ffn_w", a["ffn_conv_w"].reshape(LAYERS * 3 * F_TILES, P).T)
    put("ffn_b", cols_of(a["ffn_conv_b"]))
    put("gate_bias", np.broadcast_to(a["ab_gate_bias"][0], (P, 16)))
    for n, k in (("mix_pre", "norm_mix_pre_2"), ("mix_post", "norm_mix_post_2"), ("ffn_pre", "norm_ffn_pre_2"), ("ffn_post", "norm_ffn_post_2"),
                 ("subln", "subln_g_2")):
        put(n, cols_of(a[k]))
    return p


def shape_constants():
    i = np.arange(P)
    cm = np.zeros((P, N_CM), np.float32)

    def put(name, m):
        cm[:m.shape[0], CM[name]:CM[name] + m.shape[1]] = m

    put("ident", np.eye(P))
    put("ones", np.ones((P, P)))
    put("upto", i[:, None] <= i[None, :])
    put("from", i[:, None] >= i[None, :])
    put("mask_f", np.where(i[None, :] <= i[:, None], 0.0, NEG))
    put("mask_b", np.where(i[None, :] >= i[:, None], 0.0, NEG))
    s = np.arange(T)
    inv = 10000.0 ** (-np.arange(0, 16, 2, dtype=np.float32) / 16)
    ang = np.concatenate([(s // 64)[:, None] * inv, (s % 64)[:, None] * inv], 1).astype(np.float32)
    trope = np.zeros((2, P, T), np.float32)
    trope[0, NOPE:QK_A] = np.repeat(np.cos(ang).T, 2, 0)
    trope[1, QK_A:] = np.repeat(np.sin(ang).T, 2, 0) * np.where(np.arange(ROPE) % 2 == 0, -1.0, 1.0)[:, None]
    tok = np.concatenate([np.arange(j, T, TB) for j in range(TB)])
    inv = 1.0 / (10000.0 ** (np.arange(0, 64, 2, dtype=np.float32) / 64))
    ang = (tok.astype(np.float32)[None, :] * inv[:, None]).astype(np.float32)
    sign = np.where(np.arange(P) % 64 < 32, 1.0, -1.0)[:, None]
    brope = np.stack([np.tile(np.cos(ang), (4, 1)), np.tile(np.sin(ang), (4, 1)) * sign]).astype(np.float32)
    mask = np.full((P, TB, KEYS_DIL), NEG, np.float32)
    for j in range(TB):
        q = tok[j * P:(j + 1) * P]
        for k0, keys_, dil in ((0, tok, 1), (T, q, 4), (T + P, q, 16)):
            near = ((q[:, None] - keys_[None, :]) % dil == 0) & (np.abs(q[:, None] - keys_[None, :]) <= SIDE * dil)
            mask[:, j, k0:k0 + len(keys_)] = np.where(near, 0.0, NEG)
    return cm, trope, brope, mask, tok


def kernel(**inputs):
    import concourse.bacc as bacc
    from concourse.bass_utils import run_bass_kernel_spmd

    a = {k: np.asarray(w) for k, w in inputs.items()}
    cm, trope, brope, mask, tok = shape_constants()
    tiles_of = lambda m: np.ascontiguousarray(m.T.reshape(-1, P, m.shape[0]).transpose(1, 0, 2))
    ada = a["ada_w"].reshape(LAYERS, 2, KD // 2, P, ADA_M // ADA_G, ADA_G * P).transpose(0, 4, 1, 3, 2, 5).reshape(-1, P, KD // 2 * ADA_G * P)
    arrays = {
        "stream": weight_stream(a),
        "ada": np.ascontiguousarray(ada),
        "xT": tiles_of(a["x"][0]),
        "cT": tiles_of(a["ctx"][0]),
        "cond": np.stack([a["c"][0].reshape(KD, P).T, a["c_ctx"].reshape(KD, P).T], 2).reshape(P, 2 * KD),
        "wgate": np.ascontiguousarray(a["ab_w_in"][0][:, 2560:2576].reshape(KD, P, 16).transpose(1, 0, 2).reshape(P, KD * 16)),
        "lam": np.ascontiguousarray(np.broadcast_to(a["lam_2"].reshape(1, -1), (P, LAYERS * 256))),
        "pcol": feature_columns(a),
        "cmat": cm, "trope": trope, "brope": brope, "bmask": mask,
    }
    nc = bacc.Bacc("TRN2", target_bir_lowering=False, num_devices=1)
    d = {k: nc.dram_tensor(k, w.shape, F32, kind="ExternalInput").ap() for k, w in arrays.items()}
    out = nc.dram_tensor("out", (P, KD, T), F32, kind="ExternalOutput").ap()
    program(nc, d["stream"], d["ada"], d["xT"], d["cT"], d["cond"], d["wgate"], d["lam"], d["pcol"], d["cmat"], d["trope"], d["brope"],
            d["bmask"], out)
    got = run_bass_kernel_spmd(nc, [arrays], core_ids=[0]).results[0]["out"]
    y = np.empty((T, D), got.dtype)
    y[tok] = got.transpose(2, 1, 0).reshape(T, D)
    return y[None]
```
